# Optimizing a Trainium2 kernel written in Bass

```python
import math
import jax, jax.numpy as jnp
from jax import lax
import numpy as np

D_MODEL = 1024
BATCH = 1
SEQ = 512
DEPTH = 1

EPS = 1e-6
CONV_WIDTH = 4
N_BRANCHES = 3
GMLP_WIDTH = D_MODEL
GMLP_GROUPS = 8
GMLP_GROUP_DIM = GMLP_WIDTH // GMLP_GROUPS
GMLP_CHUNK = 128
LRU_WIDTH = D_MODEL
LRU_HEADS = 8
LRU_HEAD_DIM = LRU_WIDTH // LRU_HEADS
LRU_C = 8.0
SSD_WIDTH = D_MODEL
SSD_HEAD_DIM = 64
SSD_HEADS = SSD_WIDTH // SSD_HEAD_DIM
SSD_GROUPS = 4
SSD_HEADS_PER_GROUP = SSD_HEADS // SSD_GROUPS
SSD_STATE = 128
SSD_CHUNK = 128
SSD_CONV_DIM = SSD_WIDTH + 2 * SSD_GROUPS * SSD_STATE
MLP_HIDDEN = 4 * D_MODEL
GMLP_IN = 2 * GMLP_WIDTH
LRU_IN = 2 * LRU_WIDTH
SSD_IN = SSD_WIDTH + SSD_CONV_DIM + SSD_HEADS
GATE_IN = N_BRANCHES * D_MODEL
D_IN = GMLP_IN + LRU_IN + SSD_IN + GATE_IN
SPLIT_POINTS = (GMLP_IN,
                GMLP_IN + LRU_IN,
                GMLP_IN + LRU_IN + SSD_WIDTH,
                GMLP_IN + LRU_IN + SSD_WIDTH + SSD_CONV_DIM,
                GMLP_IN + LRU_IN + SSD_IN)


def rms_norm(x, g):
    x32 = x.astype(jnp.float32)
    y = x32 * lax.rsqrt(jnp.mean(x32 * x32, axis=-1, keepdims=True) + EPS)
    return (y * g.astype(jnp.float32)).astype(x.dtype)

def layer_norm(x, g, b):
    x32 = x.astype(jnp.float32)
    mu = jnp.mean(x32, axis=-1, keepdims=True)
    xc = x32 - mu
    y = xc * lax.rsqrt(jnp.mean(xc * xc, axis=-1, keepdims=True) + EPS)
    return (y * g.astype(jnp.float32) + b.astype(jnp.float32)).astype(x.dtype)

def causal_dwconv(x, w, b):
    k, c = w.shape
    y = lax.conv_general_dilated(x, w[:, None, :], window_strides=(1,), padding=[(k - 1, 0)],
                                 dimension_numbers=('NWC', 'WIO', 'NWC'), feature_group_count=c)
    return y + b

def gmlp_mixer(za, ln_g, ln_b, w_s, b_s):
    bsz, seq, _ = za.shape
    u, v = jnp.split(jax.nn.gelu(za), 2, axis=-1)
    v = layer_norm(v, ln_g, ln_b)
    nc = seq // GMLP_CHUNK
    vc = v.reshape(bsz, nc, GMLP_CHUNK, GMLP_GROUPS, GMLP_GROUP_DIM)
    causal = jnp.tril(jnp.ones((GMLP_CHUNK, GMLP_CHUNK), dtype=bool))
    w = jnp.where(causal, w_s, 0)
    mixed = jnp.einsum('gts,bcsgd->bctgd', w, vc) + b_s.T[:, :, None]
    return u * mixed.reshape(bsz, seq, GMLP_WIDTH)

def rg_lru_mixer(zb, conv_w, conv_b, w_r, b_r, w_i, b_i, lam):
    bsz, seq, _ = zb.shape
    xb, gate = jnp.split(zb, 2, axis=-1)
    xb = causal_dwconv(xb, conv_w, conv_b)
    xh = xb.reshape(bsz, seq, LRU_HEADS, LRU_HEAD_DIM)
    r = jax.nn.sigmoid(jnp.einsum('bshi,hij->bshj', xh, w_r).reshape(bsz, seq, LRU_WIDTH) + b_r)
    i = jax.nn.sigmoid(jnp.einsum('bshi,hij->bshj', xh, w_i).reshape(bsz, seq, LRU_WIDTH) + b_i)
    log_a = -LRU_C * r.astype(jnp.float32) * jax.nn.softplus(-lam.astype(jnp.float32))
    a = jnp.exp(log_a)
    inp = jnp.sqrt(-jnp.expm1(2.0 * log_a)) * (i * xb).astype(jnp.float32)

    def combine(c1, c2):
        a1, b1 = c1
        a2, b2 = c2
        return a1 * a2, a2 * b1 + b2

    _, h = lax.associative_scan(combine, (a, inp), axis=1)
    return jax.nn.gelu(gate) * h.astype(gate.dtype)

def segsum(x):
    t = x.shape[-1]
    cs = jnp.cumsum(x, axis=-1)
    seg = cs[..., :, None] - cs[..., None, :]
    return jnp.where(jnp.tril(jnp.ones((t, t), dtype=bool)), seg, -jnp.inf)

def ssd_mixer(z, xbc, dt_raw, conv_w, conv_b, dt_bias, a_log, d_skip, norm_g):
    bsz, seq, _ = z.shape
    nc = seq // SSD_CHUNK
    g, r, q = SSD_GROUPS, SSD_HEADS_PER_GROUP, SSD_CHUNK
    xbc = jax.nn.silu(causal_dwconv(xbc, conv_w, conv_b))
    xs, bm, cm = jnp.split(xbc, [SSD_WIDTH, SSD_WIDTH + g * SSD_STATE], axis=-1)
    dt = jax.nn.softplus((dt_raw + dt_bias).astype(jnp.float32))
    a = -jnp.exp(a_log.astype(jnp.float32))
    x32 = xs.astype(jnp.float32).reshape(bsz, nc, q, g, r, SSD_HEAD_DIM)
    xdt = x32 * dt.reshape(bsz, nc, q, g, r)[..., None]
    bc = bm.astype(jnp.float32).reshape(bsz, nc, q, g, SSD_STATE)
    cc = cm.astype(jnp.float32).reshape(bsz, nc, q, g, SSD_STATE)
    adt = (dt * a).reshape(bsz, nc, q, g, r).transpose(0, 3, 4, 1, 2)
    a_cs = jnp.cumsum(adt, axis=-1)
    decay = jnp.exp(segsum(adt))
    cb = jnp.einsum('bclgn,bcsgn->bgcls', cc, bc)
    y_diag = jnp.einsum('bgcls,bgrcls,bcsgrp->bclgrp', cb, decay, xdt)
    decay_states = jnp.exp(a_cs[..., -1:] - a_cs)
    states = jnp.einsum('bcsgn,bgrcs,bcsgrp->cbgrpn', bc, decay_states, xdt)
    chunk_decay = jnp.exp(a_cs[..., -1]).transpose(3, 0, 1, 2)

    def step(h, inp):
        dec, st = inp
        return h * dec[..., None, None] + st, h

    _, prev = lax.scan(step, jnp.zeros_like(states[0]), (chunk_decay, states))
    y_off = jnp.einsum('bclgn,cbgrpn,bgrcl->bclgrp', cc, prev, jnp.exp(a_cs))
    y = y_diag + y_off + x32 * d_skip.astype(jnp.float32).reshape(g, r)[:, :, None]
    y = y.reshape(bsz, seq, SSD_WIDTH) * jax.nn.silu(z.astype(jnp.float32))
    yg = y.reshape(bsz, seq, g, SSD_WIDTH // g)
    yg = yg * lax.rsqrt(jnp.mean(yg * yg, axis=-1, keepdims=True) + EPS)
    y = yg.reshape(bsz, seq, SSD_WIDTH) * norm_g.astype(jnp.float32)
    return y.astype(z.dtype)

def _normal(k, shape, scale):
    return scale * jax.random.normal(k, shape, jnp.float32)

def first_inputs(seed: int = 0) -> dict:
    key = jax.random.key(seed)
    ks = jax.random.split(key, 32)
    L = DEPTH
    a0 = jax.random.uniform(ks[15], (L, LRU_WIDTH), jnp.float32, minval=0.9, maxval=0.999)
    dt0 = jnp.exp(jax.random.uniform(ks[18], (L, SSD_HEADS), jnp.float32,
                                     minval=math.log(1e-3), maxval=math.log(1e-1)))
    return {
        'x': _normal(ks[0], (BATCH, SEQ, D_MODEL), 1.0),
        'norm_mix_g': 1.0 + _normal(ks[1], (L, D_MODEL), 0.1),
        'w_in': _normal(ks[2], (L, D_MODEL, D_IN), D_MODEL ** -0.5),
        'b_gate': _normal(ks[3], (L, N_BRANCHES, D_MODEL), 0.1),
        'gmlp_ln_g': 1.0 + _normal(ks[4], (L, GMLP_WIDTH), 0.1),
        'gmlp_ln_b': _normal(ks[5], (L, GMLP_WIDTH), 0.1),
        'gmlp_w_s': _normal(ks[6], (L, GMLP_GROUPS, GMLP_CHUNK, GMLP_CHUNK), GMLP_CHUNK ** -0.5),
        'gmlp_b_s': 1.0 + _normal(ks[7], (L, GMLP_GROUPS, GMLP_CHUNK), 0.1),
        'lru_conv_w': _normal(ks[8], (L, CONV_WIDTH, LRU_WIDTH), CONV_WIDTH ** -0.5),
        'lru_conv_b': _normal(ks[9], (L, LRU_WIDTH), 0.1),
        'lru_w_r': _normal(ks[10], (L, LRU_HEADS, LRU_HEAD_DIM, LRU_HEAD_DIM), LRU_HEAD_DIM ** -0.5),
        'lru_b_r': _normal(ks[11], (L, LRU_WIDTH), 0.1),
        'lru_w_i': _normal(ks[12], (L, LRU_HEADS, LRU_HEAD_DIM, LRU_HEAD_DIM), LRU_HEAD_DIM ** -0.5),
        'lru_b_i': _normal(ks[13], (L, LRU_WIDTH), 0.1),
        'lru_lambda': jnp.log(a0) - jnp.log1p(-a0),
        'ssd_conv_w': _normal(ks[16], (L, CONV_WIDTH, SSD_CONV_DIM), CONV_WIDTH ** -0.5),
        'ssd_conv_b': _normal(ks[17], (L, SSD_CONV_DIM), 0.1),
        'ssd_dt_bias': dt0 + jnp.log(-jnp.expm1(-dt0)),
        'ssd_a_log': jnp.log(jax.random.uniform(ks[19], (L, SSD_HEADS), jnp.float32, minval=1.0, maxval=16.0)),
        'ssd_d': 1.0 + _normal(ks[20], (L, SSD_HEADS), 0.1),
        'ssd_norm_g': 1.0 + _normal(ks[21], (L, SSD_WIDTH), 0.1),
        'w_branch_a': _normal(ks[22], (L, GMLP_WIDTH, D_MODEL), GMLP_WIDTH ** -0.5),
        'w_branch_b': _normal(ks[23], (L, LRU_WIDTH, D_MODEL), LRU_WIDTH ** -0.5),
        'w_branch_c': _normal(ks[24], (L, SSD_WIDTH, D_MODEL), SSD_WIDTH ** -0.5),
        'w_out': _normal(ks[25], (L, D_MODEL, D_MODEL), D_MODEL ** -0.5),
        'norm_mlp_g': 1.0 + _normal(ks[26], (L, D_MODEL), 0.1),
        'w_mlp_up': _normal(ks[27], (L, D_MODEL, MLP_HIDDEN), D_MODEL ** -0.5),
        'w_mlp_down': _normal(ks[28], (L, MLP_HIDDEN, D_MODEL), MLP_HIDDEN ** -0.5),
        'final_norm_g': 1.0 + _normal(ks[29], (D_MODEL,), 0.1),
    }

def first_block(x, norm_mix_g, w_in, b_gate, gmlp_ln_g, gmlp_ln_b, gmlp_w_s, gmlp_b_s,
              lru_conv_w, lru_conv_b, lru_w_r, lru_b_r, lru_w_i, lru_b_i, lru_lambda,
              ssd_conv_w, ssd_conv_b, ssd_dt_bias, ssd_a_log, ssd_d, ssd_norm_g,
              w_branch_a, w_branch_b, w_branch_c, w_out, norm_mlp_g, w_mlp_up, w_mlp_down,
              final_norm_g):
    bsz, seq, _ = x.shape
    h = x
    for l in range(DEPTH):
        hn = rms_norm(h, norm_mix_g[l])
        proj = jnp.einsum('bsd,de->bse', hn, w_in[l])
        za, zb, zc, xbc, dt_raw, g_raw = jnp.split(proj, SPLIT_POINTS, axis=-1)
        ya = gmlp_mixer(za, gmlp_ln_g[l], gmlp_ln_b[l], gmlp_w_s[l], gmlp_b_s[l])
        yb = rg_lru_mixer(zb, lru_conv_w[l], lru_conv_b[l], lru_w_r[l], lru_b_r[l],
                          lru_w_i[l], lru_b_i[l], lru_lambda[l])
        yc = ssd_mixer(zc, xbc, dt_raw, ssd_conv_w[l], ssd_conv_b[l], ssd_dt_bias[l],
                       ssd_a_log[l], ssd_d[l], ssd_norm_g[l])
        gates = jax.nn.sigmoid(g_raw.reshape(bsz, seq, N_BRANCHES, D_MODEL) + b_gate[l])
        merged = (gates[:, :, 0] * jnp.einsum('bse,ed->bsd', ya, w_branch_a[l])
                  + gates[:, :, 1] * jnp.einsum('bse,ed->bsd', yb, w_branch_b[l])
                  + gates[:, :, 2] * jnp.einsum('bse,ed->bsd', yc, w_branch_c[l]))
        h = h + jnp.einsum('bsd,de->bse', merged, w_out[l])
        hn = rms_norm(h, norm_mlp_g[l])
        up = jax.nn.relu(jnp.einsum('bsd,df->bsf', hn, w_mlp_up[l]))
        h = h + jnp.einsum('bsf,fd->bsd', up * up, w_mlp_down[l])
    return rms_norm(h, final_norm_g)


DEPTH_2 = 2

MEM_LEN = 256
D_FF = 2816
CONV_CH = 256
CONV_W = 31
SC_CH = 256
SC_W = 3
N_HEADS = 8
HEAD_DIM = 64
ATT_W = N_HEADS * HEAD_DIM
IDX_HEADS = 4
IDX_DIM = 64
TOPK_MAX = 256
Q_BLOCK = 128
ROPE_THETA = 10000.0
XA_HEADS = 4
XA_DIM = D_MODEL // XA_HEADS
MIX_W = CONV_CH + SC_CH + ATT_W
SPLIT_SIZES = (CONV_CH, CONV_CH,
               SC_CH, SC_CH, SC_CH,
               ATT_W, ATT_W, ATT_W,
               IDX_HEADS * IDX_DIM, IDX_DIM, IDX_HEADS)
N_IN = sum(SPLIT_SIZES)
SPLIT_POINTS_2 = tuple(int(v) for v in np.cumsum(SPLIT_SIZES)[:-1])
IDX_SCALE = (IDX_HEADS ** -0.5) * (IDX_DIM ** -0.5)


def rms_norm_2(x, g, eps=1e-6):
    xf = x.astype(jnp.float32)
    y = xf * lax.rsqrt(jnp.mean(xf * xf, axis=-1, keepdims=True) + eps)
    return (y * g.astype(jnp.float32)).astype(x.dtype)

def layer_norm_2(x, g, b, eps=1e-5):
    xf = x.astype(jnp.float32)
    mu = jnp.mean(xf, axis=-1, keepdims=True)
    var = jnp.mean(jnp.square(xf - mu), axis=-1, keepdims=True)
    y = (xf - mu) * lax.rsqrt(var + eps)
    return (y * g.astype(jnp.float32) + b.astype(jnp.float32)).astype(x.dtype)

def swiglu(h, w_gate, w_up, w_down):
    return (jax.nn.silu(h @ w_gate) * (h @ w_up)) @ w_down

def causal_dwconv_2(x, w):
    width, ch = w.shape
    return lax.conv_general_dilated(
        x, w[:, None, :].astype(x.dtype), window_strides=(1,), padding=[(width - 1, 0)],
        dimension_numbers=('NWC', 'WIO', 'NWC'), feature_group_count=ch)

def rope_tables(positions, dim):
    inv_freq = ROPE_THETA ** (-jnp.arange(0, dim, 2, dtype=jnp.float32) / dim)
    ang = positions.astype(jnp.float32)[..., None] * inv_freq
    return jnp.cos(ang), jnp.sin(ang)

def apply_rope(t, cos, sin):
    tf = t.astype(jnp.float32)
    half = tf.shape[-1] // 2
    t1, t2 = tf[..., :half], tf[..., half:]
    c, s = cos[:, :, None, :], sin[:, :, None, :]
    return jnp.concatenate([t1 * c - t2 * s, t2 * c + t1 * s], axis=-1).astype(t.dtype)

def conformer_conv(a_val, a_gate, dw, dw_b, ln_g, ln_b):
    h = a_val * jax.nn.sigmoid(a_gate)
    h = causal_dwconv_2(h, dw) + dw_b
    return jax.nn.silu(layer_norm_2(h, ln_g, ln_b))

def short_gated_conv(b_gate, c_gate, h, w):
    return b_gate * causal_dwconv_2(c_gate * h, w)

def dsa_attention(q, k, v, q_idx, k_idx, w_idx):
    bsz, seq, nh, dh = q.shape
    topk = min(TOPK_MAX, seq // 4)
    nb = seq // Q_BLOCK
    key_pos = jnp.arange(seq)
    b_ar = jnp.arange(bsz)[:, None, None]

    def to_blocks(t):
        return jnp.moveaxis(t.reshape(bsz, nb, Q_BLOCK, *t.shape[2:]), 1, 0)

    q_pos = jnp.arange(seq).reshape(nb, Q_BLOCK)

    def one_block(args):
        qb, qib, wb, tb = args
        logits = jnp.einsum('bqhd,bsd->bqhs', qib, k_idx).astype(jnp.float32)
        score = jnp.einsum('bqh,bqhs->bqs', wb.astype(jnp.float32), jax.nn.relu(logits)) * IDX_SCALE
        causal = key_pos[None, :] <= tb[:, None]
        score = jnp.where(causal[None], score, -jnp.inf)
        top_val, top_idx = lax.top_k(score, topk)
        k_sel = k[b_ar, top_idx]
        v_sel = v[b_ar, top_idx]
        s = jnp.einsum('bqhd,bqkhd->bqhk', qb, k_sel).astype(jnp.float32) * (dh ** -0.5)
        s = jnp.where(jnp.isfinite(top_val)[:, :, None, :], s, -jnp.inf)
        p = jax.nn.softmax(s, axis=-1).astype(v.dtype)
        return jnp.einsum('bqhk,bqkhd->bqhd', p, v_sel)

    out = lax.map(one_block, (to_blocks(q), to_blocks(q_idx), to_blocks(w_idx), q_pos))
    return jnp.moveaxis(out, 0, 1).reshape(bsz, seq, nh * dh)

def memory_cross_attention(h, mem_n, wq, wkv, wo):
    bsz, seq, _ = h.shape
    m = mem_n.shape[1]
    q = (h @ wq).reshape(bsz, seq, XA_HEADS, XA_DIM)
    k, v = jnp.split(mem_n @ wkv, 2, axis=-1)
    k = k.reshape(bsz, m, XA_HEADS, XA_DIM)
    v = v.reshape(bsz, m, XA_HEADS, XA_DIM)
    s = jnp.einsum('bshd,bmhd->bhsm', q, k).astype(jnp.float32) * (XA_DIM ** -0.5)
    p = jax.nn.softmax(s, axis=-1).astype(v.dtype)
    o = jnp.einsum('bhsm,bmhd->bshd', p, v).reshape(bsz, seq, D_MODEL)
    return o @ wo

def second_inputs(seed: int = 0) -> dict:
    key = jax.random.key(seed)
    ks = iter(jax.random.split(key, 32))
    L, D, F = DEPTH_2, D_MODEL, D_FF

    def w(shape, fan_in):
        return jax.random.normal(next(ks), shape, jnp.float32) * (fan_in ** -0.5)

    def gain(shape):
        return 1.0 + 0.01 * jax.random.normal(next(ks), shape, jnp.float32)

    def bias(shape):
        return 0.01 * jax.random.normal(next(ks), shape, jnp.float32)

    x = jax.random.normal(next(ks), (BATCH, SEQ, D), jnp.float32)
    mem = jax.random.normal(next(ks), (BATCH, MEM_LEN, D), jnp.float32)
    start = jax.random.randint(next(ks), (BATCH, 1), 0, 1024, dtype=jnp.int32)
    positions = (start + jnp.arange(SEQ, dtype=jnp.int32)[None, :]).astype(jnp.int32)
    return {
        "x": x, "mem": mem, "positions": positions,
        "ffn1_norm": gain((L, D)), "ffn1_w_gate": w((L, D, F), D), "ffn1_w_up": w((L, D, F), D),
        "ffn1_w_down": w((L, F, D), F),
        "mix_norm": gain((L, D)), "w_in": w((L, D, N_IN), D),
        "conf_dw": w((L, CONV_W, CONV_CH), CONV_W), "conf_dw_b": bias((L, CONV_CH)),
        "conf_ln_g": gain((L, CONV_CH)), "conf_ln_b": bias((L, CONV_CH)),
        "sc_dw": w((L, SC_W, SC_CH), SC_W),
        "w_out": w((L, MIX_W, D), MIX_W),
        "xa_norm": gain((L, D)), "mem_norm": gain((L, D)),
        "xa_wq": w((L, D, D), D), "xa_wkv": w((L, D, 2 * D), D), "xa_wo": w((L, D, D), D),
        "ffn2_norm": gain((L, D)), "ffn2_w_gate": w((L, D, F), D), "ffn2_w_up": w((L, D, F), D),
        "ffn2_w_down": w((L, F, D), F),
        "final_norm": gain((D,)),
    }

def second_block(x, mem, positions, ffn1_norm, ffn1_w_gate, ffn1_w_up, ffn1_w_down, mix_norm, w_in,
              conf_dw, conf_dw_b, conf_ln_g, conf_ln_b, sc_dw, w_out, xa_norm, mem_norm,
              xa_wq, xa_wkv, xa_wo, ffn2_norm, ffn2_w_gate, ffn2_w_up, ffn2_w_down, final_norm):
    bsz, seq, _ = x.shape
    cos, sin = rope_tables(positions, HEAD_DIM)
    for l in range(DEPTH_2):
        x = x + 0.5 * swiglu(rms_norm_2(x, ffn1_norm[l]), ffn1_w_gate[l], ffn1_w_up[l], ffn1_w_down[l])
        h = rms_norm_2(x, mix_norm[l])
        (a_val, a_gate, b_gate, c_gate, b_h, q, k, v,
         q_idx, k_idx, w_idx) = jnp.split(h @ w_in[l], SPLIT_POINTS_2, axis=-1)
        y_a = conformer_conv(a_val, a_gate, conf_dw[l], conf_dw_b[l], conf_ln_g[l], conf_ln_b[l])
        y_b = short_gated_conv(b_gate, c_gate, b_h, sc_dw[l])
        q = apply_rope(q.reshape(bsz, seq, N_HEADS, HEAD_DIM), cos, sin)
        k = apply_rope(k.reshape(bsz, seq, N_HEADS, HEAD_DIM), cos, sin)
        v = v.reshape(bsz, seq, N_HEADS, HEAD_DIM)
        q_idx = apply_rope(q_idx.reshape(bsz, seq, IDX_HEADS, IDX_DIM), cos, sin)
        k_idx = apply_rope(k_idx[:, :, None, :], cos, sin)[:, :, 0, :]
        y_c = dsa_attention(q, k, v, q_idx, k_idx, w_idx)
        x = x + jnp.concatenate([y_a, y_b, y_c], axis=-1) @ w_out[l]
        x = x + memory_cross_attention(rms_norm_2(x, xa_norm[l]), rms_norm_2(mem, mem_norm[l]),
                                       xa_wq[l], xa_wkv[l], xa_wo[l])
        x = x + 0.5 * swiglu(rms_norm_2(x, ffn2_norm[l]), ffn2_w_gate[l], ffn2_w_up[l], ffn2_w_down[l])
    return rms_norm_2(x, final_norm)


def setup_inputs(seed=0):
    out = dict(first_inputs(seed))
    for name, value in second_inputs(seed + 1).items():
        if name != "x":
            out[name + "_2"] = value
    return out


def reference(
    x, norm_mix_g, w_in, b_gate, gmlp_ln_g, gmlp_ln_b, gmlp_w_s, gmlp_b_s, lru_conv_w,
    lru_conv_b, lru_w_r, lru_b_r, lru_w_i, lru_b_i, lru_lambda, ssd_conv_w, ssd_conv_b,
    ssd_dt_bias, ssd_a_log, ssd_d, ssd_norm_g, w_branch_a, w_branch_b, w_branch_c, w_out,
    norm_mlp_g, w_mlp_up, w_mlp_down, final_norm_g, mem_2, positions_2, ffn1_norm_2,
    ffn1_w_gate_2, ffn1_w_up_2, ffn1_w_down_2, mix_norm_2, w_in_2, conf_dw_2, conf_dw_b_2,
    conf_ln_g_2, conf_ln_b_2, sc_dw_2, w_out_2, xa_norm_2, mem_norm_2, xa_wq_2, xa_wkv_2,
    xa_wo_2, ffn2_norm_2, ffn2_w_gate_2, ffn2_w_up_2, ffn2_w_down_2, final_norm_2,
):
    x = first_block(
        x, norm_mix_g, w_in, b_gate, gmlp_ln_g, gmlp_ln_b, gmlp_w_s, gmlp_b_s, lru_conv_w,
        lru_conv_b, lru_w_r, lru_b_r, lru_w_i, lru_b_i, lru_lambda, ssd_conv_w, ssd_conv_b,
        ssd_dt_bias, ssd_a_log, ssd_d, ssd_norm_g, w_branch_a, w_branch_b, w_branch_c, w_out,
        norm_mlp_g, w_mlp_up, w_mlp_down, final_norm_g,
    )
    return second_block(
        x, mem_2, positions_2, ffn1_norm_2, ffn1_w_gate_2, ffn1_w_up_2, ffn1_w_down_2,
        mix_norm_2, w_in_2, conf_dw_2, conf_dw_b_2, conf_ln_g_2, conf_ln_b_2, sc_dw_2, w_out_2,
        xa_norm_2, mem_norm_2, xa_wq_2, xa_wkv_2, xa_wo_2, ffn2_norm_2, ffn2_w_gate_2,
        ffn2_w_up_2, ffn2_w_down_2, final_norm_2,
    )


_drawn_inputs = setup_inputs


def setup_inputs(seed=0):
    import zlib

    import numpy as np

    out = dict(_drawn_inputs(seed))
    spreads = {}
    factors = {'lru_b_r': 5.982,
     'lru_b_i': 3.912,
     'ffn1_norm_2': 5.429,
     'mix_norm_2': 3.491,
     'conf_dw_b_2': 6.214,
     'conf_ln_g_2': 36.245,
     'conf_ln_b_2': 36.623,
     'xa_norm_2': 8.0,
     'mem_norm_2': 8.0,
     'ffn2_norm_2': 8.0,
     'final_norm_2': 32.283}
    for name, (base, spread) in spreads.items():
        noise = np.random.default_rng([zlib.crc32(name.encode()), seed]).standard_normal(out[name].shape)
        drawn = base * np.exp(spread * noise) if base else spread * noise
        out[name] = __import__('jax').numpy.asarray(drawn.astype(out[name].dtype))
    for name, factor in factors.items():
        out[name] = (out[name] * factor).astype(out[name].dtype)
    return out
```

```python
from contextlib import ExitStack

import numpy as np

import concourse.bass as bass
from concourse import mybir

P = 128
S = 512
D = 1024
KT = D // P
NB = S // P
MEM = 256
EPS = 1e-6
LN_EPS_2 = 1e-5
F_GMLP_U, F_GMLP_V, F_LRU_X, F_LRU_G, F_Z, F_XBC, F_DT, F_GATE = 0, 1024, 2048, 3072, 4096, 5120, 7168, 7184
FFN_PARTS = (8, 8, 6)
DFF = 2816
HEADS2, IDXH = 8, 4
TOPK = 128
NEG = -1.0e30
TAKEN = -3.0e38
IDX_SCALE = 0.0625
CONV_TAPS = 31

F32 = mybir.dt.float32
F32R = mybir.dt.float32r
I32 = mybir.dt.int32
ACT = mybir.ActivationFunctionType
ALU = mybir.AluOpType
AX = mybir.AxisListType

BATCHES = [
    [("norm_mix_g", 8), ("b_gate", 24), ("lru_conv_b", 8), ("lru_b_r", 8), ("lru_b_i", 8),
     ("lru_lambda", 8), ("ssd_conv_b", 16), ("ssd_norm_g", 8), ("norm_mlp_g", 8), ("final_norm_g", 8),
     ("final_norm_2", 8)],
    [("lru_conv_w", 32), ("ssd_conv_w", 64), ("conf_dw_b_2", 4), ("conf_ln_g_2", 4), ("conf_ln_b_2", 4),
     ("sc_dw_2", 12)],
    [("ffn1_norm_2", 16), ("mix_norm_2", 16), ("xa_norm_2", 16), ("mem_norm_2", 16), ("ffn2_norm_2", 16)],
    [("conf_dw_2", 124)],
]
COL = {}
for _b, _items in enumerate(BATCHES):
    _r = 0
    for _n, _c in _items:
        COL[_n] = _b * P + _r
        _r += _c
    assert _r <= P
N_PARAM_DMAS = sum(len(b) for b in BATCHES)

PHASES = [("u", 4, 8), ("v", 4, 8), ("ga", 8, 8), ("lru", 8, 8), ("gb", 8, 8), ("xbc", 8, 8), ("dt", 1, 8),
          ("z", 4, 8), ("gc", 8, 8), ("wo", 4, 8)]
for _p in range(4):
    PHASES += [(f"up{_p}", 4, 8), (f"down{_p}", 4, 8)]
for _l in range(2):
    for _i, _n in enumerate(FFN_PARTS):
        PHASES += [(f"f1u{_l}{_i}", _n, 8), (f"f1d{_l}{_i}", 4, _n)]
    PHASES += [(f"conv{_l}", 5, 8), (f"kidx{_l}", 1, 8), (f"qidx{_l}", 1, 8), (f"q{_l}", 2, 8), (f"k{_l}", 2, 8),
               (f"vv{_l}", 2, 8),
               (f"mwo{_l}", 4, 8), (f"xk{_l}", 4, 8), (f"xv{_l}", 4, 8), (f"xq{_l}", 4, 8), (f"xo{_l}", 4, 8)]
    for _i, _n in enumerate(FFN_PARTS):
        PHASES += [(f"f2u{_l}{_i}", _n, 8), (f"f2d{_l}{_i}", 4, _n)]
P0, NPAIR, KTS = {}, {}, {}
_at = 0
for _name, _n, _k in PHASES:
    P0[_name], NPAIR[_name], KTS[_name] = _at, _n, _k
    _at += _n
TOTAL = _at
BANK = {}
ROUND = 12582912.0
PI = 3.1415925
TURN = (6.28125, 0.001934051513671875, 1.2556659146e-06)


def three_dmas(name):
    return name.startswith("kidx")


def kind(name):
    if name in ("ga", "gb", "gc"):
        return "gated"
    if name.startswith("up"):
        return "relu2"
    if name[:3] in ("f1u", "f2u"):
        return "swiglu"
    return ""


INCS = {"gated": (1, 0, 0), "relu2": (2, 2, 2), "swiglu": (1, 1, 1), "": (0, 0, 0)}
BASE = {}
_acc = [0, 0, 0]
for _name, _n, _k in PHASES:
    BASE[_name] = tuple(_acc)
    _acc = [a + _n * d for a, d in zip(_acc, INCS[kind(_name)])]
LANDED = []
_slot = [0, 0]
for _name, _n, _k in PHASES:
    for _i in range(_n):
        _s = len(LANDED) % 2
        _slot[_s] += 48 if three_dmas(_name) else 32
        LANDED.append(_slot[_s])
LANDED.append(0)


def loop_pairs(eng, name, body, unroll=False):
    count, p0 = NPAIR[name], P0[name]
    done = 0
    if count >= 4 and not unroll:
        done = count // 2 * 2
        with eng.Fori(0, count // 2) as it:
            for b in range(2):
                body(2 * it + b, 2 * it + (p0 + b), (p0 + b) % 2, it * 32 + LANDED[p0 + b + 1])
    for i in range(done, count):
        body(i, p0 + i, (p0 + i) % 2, LANDED[p0 + i + 1])


def _acc_at(name):
    return BASE[name][2] + INCS[kind(name)][2] * NPAIR[name]


class Signal:
    marks = {}

    def __init__(self, sem, name):
        self.sem, self.name, self.n = sem, name, 0

    def mark(self, *key):
        self.n += 1
        Signal.marks[self.name, key] = self.n
        return 1

    def total(self):
        return max([v for (n, k), v in Signal.marks.items() if n == self.name], default=0)

    def at(self, *key):
        return Signal.marks.get((self.name, key), 1)


def cut(t, i, n=S):
    if isinstance(i, int):
        return t[:, i * n:(i + 1) * n]
    return t[:, bass.ds(i * n, n)]


def build_program(nc, A, out, dbg=None, stop=None):
    names = [n for n, _, _ in PHASES]
    if stop:
        names = names[:names.index(stop) + 1]
    last_pair = P0[names[-1]] + NPAIR[names[-1]] - 1
    whole = not stop

    def on(name):
        return name in names

    with ExitStack() as ctx:
        def sb(name, shape, dt=F32):
            return ctx.enter_context(nc.sbuf_tensor(name, shape, dt))

        def sem(name):
            return ctx.enter_context(nc.semaphore(name))

        def signal(name):
            return Signal(sem(name), name)

        raw = sb("raw", [P, 2, KT, 256])
        w_hi = sb("w_hi", [P, 2, KT, P], F32R)
        w_lo = sb("w_lo", [P, 2, KT, P], F32R)
        xn_hi = sb("xn_hi", [P, KT * S], F32R)
        xn_lo = sb("xn_lo", [P, KT * S], F32R)
        y_hi = sb("y_hi", [P, KT * S], F32R)
        y_lo = sb("y_lo", [P, KT * S], F32R)
        h = sb("h", [P, KT * S])
        consts = sb("consts", [P, 5 * P + 1])
        ident, ones, causal, rot, qcausal = (consts[:, i * P:(i + 1) * P] for i in range(5))
        inv_freq = consts[:, 5 * P:5 * P + 1]
        par = sb("par", [P, 4 * P])
        temps = sb("temps", [P, 6 * S])
        stat = sb("stat", [P, S])
        rstd = sb("rstd", [P, S])
        small = sb("small", [P, 256])
        size = 37 * S
        arena = sb("arena", [P, size])

        def tmp(i, n=S):
            return temps[:, i * S:i * S + n]

        def at(off, *shape):
            n = int(np.prod(shape))
            assert off + n <= size, (off, shape, size)
            v = arena[:, off:off + n]
            if len(shape) == 1:
                return v
            dims = "abcd"[:len(shape)]
            return v.rearrange(f"p ({' '.join(dims)}) -> p {' '.join(dims)}", **dict(zip(dims[:-1], shape[:-1])))

        def col(name, i=0, rows=P):
            if isinstance(i, int):
                return par[0:rows, COL[name] + i:COL[name] + i + 1]
            return par[0:rows, bass.ds(i + COL[name], 1)]

        G = [ctx.enter_context(nc.psum_tensor(f"G{i}", [P, S], F32)) for i in range(4)]
        B = [ctx.enter_context(nc.psum_tensor(f"B{i}", [P, S], F32)) for i in range(4)]

        s_load = [sem("s_load0"), sem("s_load1")]
        s_whi, s_wlo = sem("s_weights_hi"), sem("s_weights_lo")
        s_mm, s_free = sem("s_panels_multiplied"), sem("s_pairs_evacuated")
        s_ao, s_yh, s_yl = sem("s_act_out"), sem("s_y_hi"), sem("s_y_lo")
        s_const, s_par, s_x, s_gw, s_gb, s_lw, s_sp, s_mem, s_pos, s_out = (sem("s_" + n) for n in (
            "const_in", "params_in", "x_in", "gmlp_w_in", "gmlp_rows_in", "lru_w_in", "ssd_params_in", "mem_in",
            "pos_in", "out"))
        full = signal("s_bank_full")
        norm_a, norm_v = signal("s_norm_act"), signal("s_norm_vector")
        turn_a, turn_v = signal("s_turned_out_act"), signal("s_turned_out_vector")
        gmlp_v, gmlp_a, gmlp_p = signal("s_gmlp_vector"), signal("s_gmlp_act"), signal("s_gmlp_pool")
        lru_v, lru_a = signal("s_lru_vector"), signal("s_lru_act")
        xbc_v, xbc_a = signal("s_xbc_vector"), signal("s_xbc_act")
        ssd_v, ssd_a = signal("s_ssd_vector"), signal("s_ssd_act")
        z_v, z_a = signal("s_z_vector"), signal("s_z_act")
        split_a, split_v = signal("s_split_hi"), signal("s_split_lo")
        trig_v, trig_a = signal("s_angles"), signal("s_sines")
        rope_v = signal("s_rope")
        conv_v, conv_a = signal("s_conv_vector"), signal("s_conv_act")
        dsa_v, dsa_a, dsa_p = signal("s_dsa_vector"), signal("s_dsa_act"), signal("s_dsa_masked")
        xa_v, xa_a = signal("s_cross_vector"), signal("s_cross_act")
        s_dve, s_act = sem("s_vector_chain"), sem("s_act_chain")
        loads_free = signal("s_loads_free")

        T = S
        MERGED = 0
        merged = arena[:, 0:8 * T]
        u = arena[:, 8 * T:16 * T]
        vt = arena[:, 16 * T:24 * T]
        v_tok = at(24 * T, NB, D)
        w_sp = at(32 * T, 8, P)
        w_spT = at(34 * T, 8, P)
        g_bc, b_bc, bs_bc = at(0, D), at(D, D), at(2 * D, D)
        x_in = at(8 * T, NB, D)
        prow = at(16 * T, 4, P)
        lru_w = at(8 * T, 2, 8, P)
        xpad = [at(12 * T + q * (S + 3), S + 3) for q in range(2)]
        lt = [at(12 * T + 2 * (S + 3) + i * T, T) for i in range(16)]
        xbc = arena[:, 8 * T:24 * T]
        sst = at(24 * T, NB, 96)
        chunk_decay = at(24 * T + 384, NB, 16)
        acs = at(25 * T, T)
        pre = [at((26 + i) * T, T) for i in range(11)]
        stk = pre[0]
        b_tok = at(26 * T, NB, P)
        xdt = at(27 * T, NB, 256)
        xdd = at(29 * T, NB, 256)
        cb = at(31 * T, NB, P)
        st = at(32 * T, 3, 256)
        cpad = [at(26 * T + i * (S + 3), S + 3) for i in range(4)]
        cacc = [at(31 * T + i * T, T) for i in range(2)]
        memn = arena[:, 0:8 * MEM]
        sincos = at(4 * T, 2, T)
        mem_in = at(6 * T, 2, D)
        mem_t = arena[:, 10 * T:14 * T]
        ang = [at((14 + i) * T, T) for i in range(5)]
        qkv = arena[:, 6 * T:14 * T]
        qi = arena[:, 14 * T:16 * T]
        ki = arena[:, 16 * T:17 * T]
        vt2 = arena[:, 17 * T:21 * T]
        wi = arena[:, 21 * T:22 * T]
        v_key = at(22 * T, NB, 512)
        w_tok = small[:, 128:144].rearrange("p (t h) -> p t h", h=4)
        av = [at(22 * T + k * (S + 30), S + 30) for k in range(2)]
        hc = [at(24 * T + 128 + k * (S + 2), S + 2) for k in range(2)]
        bg = [at((27 + k) * T, T) for k in range(2)]
        cv = [at((29 + k) * T, T) for k in range(2)]
        score, work = at(26 * T, T), at(27 * T, T)
        bias = at(28 * T, T)
        att = [at((29 + i) * T, T) for i in range(4)]
        o_t = arena[:, 33 * T:37 * T]
        xq = arena[:, 6 * T:14 * T]
        xk = arena[:, 14 * T:18 * T]
        xvt = arena[:, 18 * T:22 * T]
        xv = at(22 * T, 2, D)
        xp = [at(26 * T + i * MEM, MEM) for i in range(2)]
        xpt = [at((27 + 2 * i) * T, 2, S) for i in range(2)]

        def source(name, i):
            nk = KTS[name]
            l = int(name[-1]) if name[-1].isdigit() else 0

            def columns(W, c0, r0=0):
                v = W[r0:r0 + nk * P, bass.ds(c0, 256)].rearrange("(k p) n -> p k n", p=P)
                hk = nk // 2
                return [((slice(0, hk), slice(0, 256)), v[:, 0:hk, :]), ((slice(hk, nk), slice(0, 256)), v[:, hk:nk, :])]

            def two(W1, c1, W2, c2):
                return [((slice(0, 8), slice(0, P)), W1[:, bass.ds(c1, P)].rearrange("(k p) n -> p k n", p=P)),
                        ((slice(0, 8), slice(P, 256)), W2[:, bass.ds(c2, P)].rearrange("(k p) n -> p k n", p=P))]

            w_in = A["w_in"][0]
            if name in ("u", "v", "xbc", "z"):
                return columns(w_in, i * 256 + {"u": F_GMLP_U, "v": F_GMLP_V, "xbc": F_XBC, "z": F_Z}[name])
            if name in ("ga", "gb", "gc"):
                return two(w_in, i * P + (F_GATE + "abc".index(name[1]) * D), A["w_branch_" + name[1]][0], i * P)
            if name == "lru":
                return two(w_in, i * P + F_LRU_X, w_in, i * P + F_LRU_G)
            if name == "dt":
                v = w_in[:, F_DT:F_DT + 16].rearrange("(k p) n -> p k n", p=P)
                return [((slice(a, a + 4), slice(0, 16)), v[:, a:a + 4, :]) for a in (0, 4)]
            if name == "wo":
                return columns(A["w_out"][0], i * 256)
            if name.startswith("up"):
                return columns(A["w_mlp_up"][0], i * 256 + l * D)
            if name.startswith("down"):
                return columns(A["w_mlp_down"][0], i * 256, l * D)
            if name[0] == "f":
                layer, part = int(name[3]), int(name[4])
                k0 = sum(FFN_PARTS[:part]) * P
                f = "ffn" + name[1]
                if name[2] == "u":
                    return two(A[f + "_w_gate_2"][layer], i * P + k0, A[f + "_w_up_2"][layer], i * P + k0)
                return columns(A[f + "_w_down_2"][layer], i * 256, k0)
            w2, n = A["w_in_2"][l], name[:-1]
            if n == "kidx":
                v = w2[:, 3072:3136].rearrange("(k p) n -> p k n", p=P)
                w = w2[:, 3136:3140].rearrange("(k p) n -> p k n", p=P)
                return [((slice(0, 8), slice(0, 64)), v), ((slice(0, 8), slice(64, P)), v),
                        ((slice(0, 8), slice(P, P + 4)), w)]
            first = {"conv": 0, "q": 1280, "k": 1792, "vv": 2304, "qidx": 2816}
            if n in first:
                return columns(w2, i * 256 + first[n])
            W, c0 = {"mwo": ("w_out_2", 0), "xk": ("xa_wkv_2", 0), "xv": ("xa_wkv_2", D), "xq": ("xa_wq_2", 0),
                     "xo": ("xa_wo_2", 0)}[n]
            return columns(A[W][l], i * 256 + c0)

        def v_out(t):
            return arena[:, (2 * t) * T:(2 * t + 2) * T]

        block = ctx.enter_context(nc.Block())

        @block.sync
        def _(sp):
            for name in names:
                def load(i, n, q, landed):
                    if not isinstance(n, int) or n >= 2:
                        sp.wait_ge(s_wlo, 2 * n - 2)
                    for (ks, cs), src in source(name, i):
                        sp.dma_start(raw[:, q, ks, cs], src).then_inc(s_load[q], 16)
                loop_pairs(sp, name, load, unroll=P0[name] < 2)
            if whole:
                for t in range(NB):
                    sp.wait_ge(turn_v.sem, turn_v.at("out", t, 1))
                    sp.dma_start(out[0, t * P:(t + 1) * P, :], v_out(t)).then_inc(s_out, 16)
                sp.wait_ge(s_out, 16 * NB)
            else:
                sp.wait_ge(s_free, last_pair + 1)
                for s_, v_ in [(s_yl, _acc_at(names[-1]))] + [(x.sem, x.total()) for x in (split_v, lru_v, gmlp_v, norm_v, ssd_v, rope_v, dsa_v, xa_v, z_v, conv_v)]:
                    if v_:
                        sp.wait_ge(s_, v_)
                sp.dma_start(dbg["h"], h[:, :]).then_inc(s_out, 16)
                sp.dma_start(dbg["y"], y_hi[:, :].bitcast(F32)).then_inc(s_out, 16)
                sp.wait_ge(s_out, 32)

        def ssd_pe(pe, take, turn):
            pe.wait_ge(ssd_a.sem, ssd_a.at("stk"))
            turn(("sst",), [stk[:, c * P:(c + 1) * P] for c in range(NB)], (ssd_a, ("sst",)))
            pe.wait_ge(ssd_v.sem, ssd_v.at("ends"))
            bank = take(("ends",), (ssd_a, ("ends",)))
            pe.matmul(bank[:, 0:64], ones[0:16, :], small[0:16, 32:96], start=True, stop=True)\
              .then_inc(full.sem, full.mark("ends"))
            for g in range(4):
                bt, ct = cut(xbc, 8 + g), cut(xbc, 12 + g)
                if g == 0:
                    pe.wait_ge(xbc_a.sem, xbc_a.at("silu", 15))
                turn(("b_tok", g), [bt[:, c * P:(c + 1) * P] for c in range(NB)], (ssd_a, ("b_tok", g)))
                for k in range(2):
                    turn(("x_tok", g, k), [cut(xbc, 2 * g + k)[:, c * P:(c + 1) * P] for c in range(NB)],
                         (ssd_v, ("xdt", g, k)))
                bank = take(("cb", g), (ssd_v, ("cb", g)))
                for c in range(NB):
                    cs = slice(c * P, (c + 1) * P)
                    m = pe.matmul(bank[:, cs], bt[:, cs], ct[:, cs], start=True, stop=True)
                m.then_inc(full.sem, full.mark("cb", g))
                pe.wait_ge(ssd_a.sem, ssd_a.at("b_tok", g))
                pe.wait_ge(ssd_v.sem, ssd_v.at("xdd", g))
                for o in range(2):
                    bank = take(("st", g, o), (ssd_v, ("st", g, o)))
                    for c in range(2 * o, min(2 * o + 2, 3)):
                        m = pe.matmul(bank[:, (c % 2) * 256:(c % 2) * 256 + 256], b_tok[:, c, :], xdd[:, c, :],
                                      start=True, stop=True)
                    m.then_inc(full.sem, full.mark("st", g, o))

                def row(r):
                    hh = 4 * g + r
                    bank = take(("row", g, r), (ssd_v, ("seg", g, r)))
                    pe.matmul(bank[:, :], ident[0:16, hh:hh + 1].to_broadcast([16, P]), acs[0:16, :],
                              start=True, stop=True).then_inc(full.sem, full.mark("row", g, r))
                row(0)
                for r in range(4):
                    if r % 2 == 0:
                        bank = take(("y", g, r // 2), (ssd_v, ("y", g, r // 2)))
                    if r < 3:
                        row(r + 1)
                    pe.wait_ge(ssd_v.sem, ssd_v.at("m", g, r))
                    if r == 0:
                        pe.wait_ge(ssd_v.sem, ssd_v.at("st", g, 1))
                    o = bank[64 * (r % 2):64 * (r % 2) + 64, :]
                    for c in range(NB):
                        cs = slice(c * P, (c + 1) * P)
                        m = pe.matmul(o[:, cs], xdt[:, c, 64 * r:64 * r + 64], pre[10][:, cs], start=True, stop=c == 0)
                        if c:
                            m = pe.matmul(o[:, cs], st[:, c - 1, 64 * r:64 * r + 64], tmp(0)[:, cs],
                                          start=False, stop=True)
                    m.then_inc(full.sem, full.mark("y", g, r))

        def dsa_pe(pe, l, take, turn):
            tiles = [("q", t) for t in range(4)] + [("k", t) for t in range(4)] + [("qi", t) for t in range(2)] + [("ki", 0)]
            pe.wait_ge(s_free, P0[f"vv{l}"] + 2)
            turn(("w_tok", l), [wi[:, t * P:(t + 1) * P] for t in range(NB)], (rope_v, ("w_tok", l)))
            for key in tiles:
                bank = take(("rot", l) + key, (rope_v, ("rot", l) + key))
                pe.matmul(bank[:, :], rot, rope_tile(key), start=True, stop=True)\
                  .then_inc(full.sem, full.mark("rot", l, *key))
            for t in range(4):
                turn(("v_key", l, t), [cut(vt2, t)[:, b * P:(b + 1) * P] for b in range(NB)], (rope_v, ("v_key", l, t)))
            pe.wait_ge(rope_v.sem, rope_v.at("v_key", l, 3))

            def scores(b, hh):
                o, w = 64 * (hh % 2), (b + 1) * P
                bank = take(("s", l, b, hh), (dsa_v, ("s", l, b, hh)))
                pe.matmul(bank[:, 0:w], cut(qkv, hh // 2)[o:o + 64, b * P:(b + 1) * P],
                          cut(qkv, 4 + hh // 2)[o:o + 64, 0:w], start=True, stop=True)\
                  .then_inc(full.sem, full.mark("s", l, b, hh))

            for b in range(NB):
                w = (b + 1) * P
                if b:
                    for i in range(IDXH):
                        o = 64 * (i % 2)
                        bank = take(("idx", l, b, i), (dsa_a, ("idx", l, b, i)))
                        pe.matmul(bank[:, 0:w], cut(qi, i // 2)[o:o + 64, b * P:(b + 1) * P], ki[o:o + 64, 0:w],
                                  start=True, stop=True).then_inc(full.sem, full.mark("idx", l, b, i))
                scores(b, 0)
                for hh in range(HEADS2):
                    if hh + 1 < HEADS2:
                        scores(b, hh + 1)
                    pe.wait_ge(dsa_v.sem, dsa_v.at("p", l, b, hh))
                    turn(("p", l, b, hh), [att[2][:, t * P:(t + 1) * P] if hh % 2 else att[0][:, t * P:(t + 1) * P]
                                           for t in range(b + 1)], (dsa_a, ("pt", l, b, hh)))
                    if hh % 2 == 0:
                        obank = take(("o", l, b, hh // 2), (dsa_v, ("o", l, b, hh // 2)))
                    pe.wait_ge(dsa_a.sem, dsa_a.at("pt", l, b, hh))
                    o = 64 * (hh % 2)
                    for t in range(b + 1):
                        m = pe.matmul(obank[o:o + 64, 0:P], v_key[:, t, hh * 64:hh * 64 + 64],
                                      att[3 if hh % 2 else 1][:, t * P:(t + 1) * P], start=t == 0, stop=t == b)
                    m.then_inc(full.sem, full.mark("o", l, b, hh))

        def rope_tile(key):
            kind_, t = key
            return {"q": lambda: cut(qkv, t), "k": lambda: cut(qkv, 4 + t), "qi": lambda: cut(qi, t), "ki": lambda: ki}[kind_]()

        def cross_pe(pe, l, take, turn):
            pe.wait_ge(s_free, P0[f"xq{l}"] + 4)
            for j in range(0, KT, 2):
                turn(("xv", l, j), [xvt[:, (j + d) * MEM + t * P:(j + d) * MEM + (t + 1) * P] for d in range(2) for t in range(2)],
                     (xa_v, ("xv", l, j)))
            pe.wait_ge(xa_v.sem, xa_v.at("xv", l, 6))

            def scores(x, b):
                bank = take(("xs", l, x, b), (xa_a, ("p", l, x, b)))
                for d in range(2):
                    m = pe.matmul(bank[:, 0:MEM], cut(xq, 2 * x + d)[:, b * P:(b + 1) * P], cut(xk, 2 * x + d, MEM),
                                  start=d == 0, stop=d == 1)
                m.then_inc(full.sem, full.mark("xs", l, x, b))

            steps = [(x, b) for x in range(4) for b in range(NB)]
            scores(*steps[0])
            for n, (x, b) in enumerate(steps):
                if n + 1 < len(steps):
                    scores(*steps[n + 1])
                pe.wait_ge(xa_v.sem, xa_v.at("p", l, x, b))
                turn(("xp", l, x, b), [xp[b % 2][:, t * P:(t + 1) * P] for t in range(2)], (xa_a, ("pt", l, x, b)))
                if b == NB - 1:
                    pe.wait_ge(xa_a.sem, xa_a.at("pt", l, x, b))
                    for d in range(2):
                        bank = take(("xo", l, x, d), (xa_v, ("lo", l, 2 * x + d)))
                        for t in range(2):
                            m = pe.matmul(bank[:, :], xv[:, t, (2 * x + d) * P:(2 * x + d + 1) * P],
                                          xpt[x % 2][:, t, :], start=t == 0, stop=t == 1)
                        m.then_inc(full.sem, full.mark("xo", l, x, d))

        banks = {"next": 0, "until": [None] * 4}

        @block.tensor
        def _(pe):
            banks["next"], banks["until"] = 0, [None] * 4

            def take(key, until):
                b = banks["next"] % 4
                banks["next"] += 1
                if banks["until"][b] is not None:
                    s_, k_ = banks["until"][b]
                    pe.wait_ge(s_.sem, s_.at(*k_))
                banks["until"][b] = until
                BANK[key] = b
                return B[b]

            def turn(key, blocks, until, idn=None):
                bank, m = take(key, until), None
                for o, src in enumerate(blocks):
                    m = pe.transpose(bank[0:src.shape[1], o * P:o * P + src.shape[0]], src,
                                     ident[0:src.shape[0], 0:src.shape[0]])
                m.then_inc(full.sem, full.mark(*key))

            def panel(k, bank, hi, lo, nk, n):
                m = None
                for kt in range(nk):
                    for t, (a, b) in enumerate(((w_hi, hi), (w_hi, lo), (w_lo, hi))):
                        m = pe.matmul(bank[:, 0:n], a[:, k, kt, :], b[:, kt * S:kt * S + n],
                                      start=(kt == 0 and t == 0), stop=(kt == nk - 1 and t == 2))
                return m

            def pair(name, i, n, q, first, second, width):
                if not isinstance(n, int) or n >= 2:
                    pe.wait_ge(s_free, n - 1)
                for k, (hi, lo) in enumerate((first, second)):
                    pe.wait_ge(s_wlo, 2 * n + (k + 1))
                    panel(k, G[2 * q + k], hi, lo, KTS[name], width).then_inc(s_mm, 1)

            xn, y = (xn_hi, xn_lo), (y_hi, y_lo)

            def gemm(name, first, second=None, width=S, unroll=False):
                if on(name):
                    loop_pairs(pe, name, lambda i, n, q, landed: pair(name, i, n, q, first, second or first, width),
                               unroll=unroll or P0[name] < 2)

            def norm_pe(r, n=S):
                bank = take(("norm", r), (norm_v, ("var", r)))
                for j in range(KT):
                    pe.wait_ge(norm_a.sem, norm_a.at("square", r, j))
                    pe.matmul(bank[:, 0:n], ones, tmp(j % 2, n), start=j == 0, stop=j == KT - 1)\
                      .then_inc(full.sem, full.mark("norm", r, j))

            def normed(r):
                pe.wait_ge(norm_v.sem, norm_v.at("lo", r, KT - 1))

            pe.wait_ge(s_const, 16)
            pe.wait_ge(s_par, 16 * N_PARAM_DMAS)
            for b in range(4):
                n = sum(c for _, c in BATCHES[b])
                turn(("par", b), [prow[0:n, b, :]], (turn_v, ("par", b)))
            pe.wait_ge(s_x, 16)
            for j in range(KT):
                turn(("x", j), [x_in[:, t, j * P:(j + 1) * P] for t in range(NB)], (turn_v, ("x", j)))
            norm_pe(0)
            normed(0)
            gemm("u", xn, unroll=True)
            gemm("v", xn)
            if on("v"):
                pe.wait_ge(s_gw, 16)
                for g in range(0, 8, 4):
                    turn(("w_sp", g), [w_sp[:, g + i, :] for i in range(4)], (gmlp_v, ("w_sp", g)))
                pe.wait_ge(s_free, P0["v"] + 4)
                for j in range(KT):
                    turn(("v", j), [vt[:, j * S + t * P:j * S + (t + 1) * P] for t in range(NB)], (gmlp_a, ("v", j)))
                pe.wait_ge(gmlp_v.sem, gmlp_v.at("normed", NB - 1))
                for g in range(8):
                    bank = take(("mix", g), (gmlp_v, ("mixed", g)))
                    for c in range(NB):
                        m = pe.matmul(bank[:, c * P:(c + 1) * P], v_tok[:, c, g * P:(g + 1) * P], w_spT[:, g, :],
                                      start=True, stop=True)
                    m.then_inc(full.sem, full.mark("mix", g))
                pe.wait_ge(gmlp_v.sem, gmlp_v.at("lo", 7))
            gemm("ga", xn, y)
            if on("lru"):
                pe.wait_ge(s_lw, 32)
                for j in range(9):
                    if j < 8:
                        n = P0["lru"] + j
                        pair("lru", j, n, n % 2, xn, xn, S)
                    if j >= 1:
                        jj = j - 1
                        pe.wait_ge(lru_v.sem, lru_v.at("conv", jj))
                        for g in range(2):
                            bank = take(("ri", jj, g), (lru_a, ("ri", jj, g)))
                            pe.matmul(bank[:, :], lru_w[:, g, jj, :], lt[jj % 2], start=True, stop=True)\
                              .then_inc(full.sem, full.mark("ri", jj, g))
                pe.wait_ge(lru_v.sem, lru_v.at("lo", 7))
            gemm("gb", xn, y)
            gemm("xbc", xn, unroll=True)
            gemm("dt", xn)
            if on("dt"):
                ssd_pe(pe, take, turn)
            gemm("z", xn, unroll=True)
            if on("z"):
                for g in range(4):
                    bank = take(("zsum", g), (z_v, ("var", g)))
                    for k in range(2):
                        pe.wait_ge(z_a.sem, z_a.at("square", g, k))
                        m = pe.matmul(bank[:, :], ones, tmp(k), start=k == 0, stop=k == 1)
                    m.then_inc(full.sem, full.mark("zsum", g))
                pe.wait_ge(z_v.sem, z_v.at("lo", 7))
            gemm("gc", xn, y)
            if on("wo"):
                pe.wait_ge(split_v.sem, split_v.at("merged", 7))
            gemm("wo", y)
            if on("up0"):
                norm_pe(1)
                normed(1)
            for p in range(4):
                gemm(f"up{p}", xn)
                if on(f"down{p}"):
                    pe.wait_ge(s_yl, BASE[f"down{p}"][2])
                gemm(f"down{p}", y)
            if on("f1u00"):
                norm_pe(2)
                pe.wait_ge(s_mem, 16)
                for j in range(0, KT, 2):
                    turn(("mem", j), [mem_in[:, t, (j + d) * P:(j + d + 1) * P] for d in range(2) for t in range(2)],
                         (turn_v, ("mem", j)))
                norm_pe(3, MEM)
            for l in range(2):
                def ffn(f, r):
                    if not on(f"{f}u{l}0"):
                        return
                    norm_pe(r)
                    normed(r)
                    for part in range(3):
                        gemm(f"{f}u{l}{part}", xn)
                        if on(f"{f}d{l}{part}"):
                            pe.wait_ge(s_yl, BASE[f"{f}d{l}{part}"][2])
                        gemm(f"{f}d{l}{part}", y)
                r = 4 + 5 * l
                ffn("f1", r)
                if on(f"conv{l}"):
                    norm_pe(r + 1)
                    normed(r + 1)
                    for name in ("conv", "kidx", "qidx", "q", "k", "vv"):
                        gemm(f"{name}{l}", xn, unroll=name == "conv")
                if on(f"vv{l}"):
                    for step in range(2):
                        bank = take(("cln", l, step), (conv_v, ("stat", l, step)))
                        for k in range(2):
                            pe.wait_ge(conv_v.sem, conv_v.at("summand", l, step, k))
                            m = pe.matmul(bank[:, :], ones, cv[k] if step == 0 else tmp(k), start=k == 0, stop=k == 1)
                        m.then_inc(full.sem, full.mark("cln", l, step))
                    dsa_pe(pe, l, take, turn)
                    pe.wait_ge(split_v.sem, split_v.at("dsa", l, 3))
                gemm(f"mwo{l}", y)
                if on(f"xk{l}"):
                    pe.wait_ge(norm_v.sem, norm_v.at("mem_lo", l, KT - 1))
                    gemm(f"xk{l}", y, width=MEM)
                    gemm(f"xv{l}", y, width=MEM)
                    norm_pe(r + 2)
                    normed(r + 2)
                    gemm(f"xq{l}", xn)
                    if on(f"xq{l}"):
                        cross_pe(pe, l, take, turn)
                        pe.wait_ge(xa_v.sem, xa_v.at("lo", l, 7))
                    gemm(f"xo{l}", y)
                ffn("f2", r + 3)
            if whole:
                norm_pe(14)
                pe.wait_ge(norm_v.sem, norm_v.at("xn", 14, KT - 1))
                for t in range(NB):
                    for o in range(2):
                        turn(("out", t, o), [cut(h, 4 * o + j)[:, t * P:(t + 1) * P] for j in range(4)],
                             (turn_v, ("out", t, o)))


        def ssd_act(act, link):
            act.wait_ge(s_sp, 48)
            act.activation(small[0:16, 178:179], small[0:16, 177:178], ACT.Exp).then_inc(ssd_a.sem, ssd_a.mark("a"))
            act.wait_ge(ssd_v.sem, ssd_v.at("z"))
            link(act.activation(pre[2][0:16, :], pre[1][0:16, :], ACT.Abs))
            act.activation(pre[3][0:16, :], pre[2][0:16, :], ACT.Exp, scale=-1.0).then_inc(ssd_a.sem, ssd_a.mark("exp"))
            act.wait_ge(ssd_v.sem, ssd_v.at("to_end"))
            act.activation(stk[32:48, :], acs[0:16, :], ACT.Copy)
            act.activation(stk[64:80, :], pre[7][0:16, :], ACT.Exp).then_inc(ssd_a.sem, ssd_a.mark("stk"))
            act.wait_ge(full.sem, full.at("sst"))
            act.activation(sst[:, :, :], B[BANK.get(("sst",), 0)][:, :].rearrange("p (c n) -> p c n", c=NB)[:, :, 0:96], ACT.Copy)\
               .then_inc(ssd_a.sem, ssd_a.mark("sst"))
            act.wait_ge(full.sem, full.at("ends"))
            act.activation(chunk_decay[:, :, :].rearrange("p c h -> p (c h)"), B[BANK.get(("ends",), 0)][:, 0:64], ACT.Exp)\
               .then_inc(ssd_a.sem, ssd_a.mark("ends"))
            for g in range(4):
                act.wait_ge(full.sem, full.at("b_tok", g))
                if g:
                    act.wait_ge(full.sem, full.at("st", g - 1, 1))
                act.activation(b_tok[:, :, :].rearrange("p c n -> p (c n)"), B[BANK.get(("b_tok", g), 0)][:, :], ACT.Copy)\
                   .then_inc(ssd_a.sem, ssd_a.mark("b_tok", g))
                for r in range(4):
                    act.wait_ge(full.sem, full.at("row", g, r))
                    if (g, r) != (0, 0):
                        act.wait_ge(ssd_v.sem, ssd_v.at("ce", *((g, r - 1) if r else (g - 1, 3))))
                    act.activation(pre[8], B[BANK.get(("row", g, r), 0)][:, :], ACT.Exp).then_inc(ssd_a.sem, ssd_a.mark("row", g, r))
                    act.wait_ge(ssd_v.sem, ssd_v.at("min", g, r))
                    act.activation(pre[9], pre[9], ACT.Exp).then_inc(ssd_a.sem, ssd_a.mark("decay", g, r))

        def dsa_act(act, l):
            for b in range(NB):
                w = (b + 1) * P
                if b:
                    for i in range(IDXH):
                        act.wait_ge(full.sem, full.at("idx", l, b, i))
                        if i >= 2 or b >= 2:
                            act.wait_ge(dsa_v.sem, dsa_v.at("idx", l, *((b, i - 2) if i >= 2 else (b - 1, i + 2))))
                        act.activation(tmp(i % 2, w), B[BANK.get(("idx", l, b, i), 0)][:, 0:w], ACT.Relu, scale=IDX_SCALE)\
                           .then_inc(dsa_a.sem, dsa_a.mark("idx", l, b, i))
                for hh in range(HEADS2):
                    p, pt = (att[2], att[3]) if hh % 2 else (att[0], att[1])
                    act.wait_ge(dsa_v.sem, dsa_v.at("neg", l, b, hh))
                    act.activation(p[:, 0:w], p[:, 0:w], ACT.Exp, bias=small[:, 146 + hh % 2:147 + hh % 2],
                                   accum_out=small[:, 148 + hh % 2:149 + hh % 2]).then_inc(dsa_a.sem, dsa_a.mark("exp", l, b, hh))
                    act.wait_ge(full.sem, full.at("p", l, b, hh))
                    act.activation(pt[:, 0:w], B[BANK.get(("p", l, b, hh), 0)][:, 0:w], ACT.Copy)\
                       .then_inc(dsa_a.sem, dsa_a.mark("pt", l, b, hh))
            for t in range(4):
                act.wait_ge(dsa_v.sem, dsa_v.at("o", l, NB - 1, t))
                act.activation(cut(y_hi, 4 + t), cut(o_t, t), ACT.Copy).then_inc(split_a.sem, split_a.mark("dsa", l, t))

        def cross_act(act, l):
            for x in range(4):
                for b in range(NB):
                    act.wait_ge(xa_v.sem, xa_v.at("neg", l, x, b))
                    act.activation(xp[b % 2], B[BANK.get(("xs", l, x, b), 0)][:, 0:MEM], ACT.Exp, scale=1.0 / 16.0,
                                   bias=small[:, 152 + b % 2:153 + b % 2],
                                   accum_out=small[:, 154 + b % 2:155 + b % 2]).then_inc(xa_a.sem, xa_a.mark("p", l, x, b))
                    act.wait_ge(full.sem, full.at("xp", l, x, b))
                    act.activation(xpt[x % 2][:, :, b * P:(b + 1) * P],
                                   B[BANK.get(("xp", l, x, b), 0)][:, 0:MEM].rearrange("p (t q) -> p t q", t=2), ACT.Copy)\
                       .then_inc(xa_a.sem, xa_a.mark("pt", l, x, b))
                for d in range(2):
                    act.wait_ge(full.sem, full.at("xo", l, x, d))
                    act.activation(cut(y_hi, 2 * x + d), B[BANK.get(("xo", l, x, d), 0)][:, :], ACT.Copy)\
                       .then_inc(xa_a.sem, xa_a.mark("hi", l, 2 * x + d))

        @block.scalar
        def _(act):
            chain = [0]

            def link(ins):
                chain[0] += 1
                ins.then_inc(s_act, 1)
                act.wait_ge(s_act, chain[0])

            def prep(n, q, landed, k):
                if isinstance(n, int) and n + 1 > last_pair:
                    return
                act.wait_ge(s_load[1 - q], landed)
                act.wait_ge(s_mm, 2 * n + (k + 1))
                act.activation(w_hi[:, k], raw[:, 1 - q, :, k * P:(k + 1) * P], ACT.Copy).then_inc(s_whi, 1)

            def product(n, k):
                act.wait_ge(s_mm, 2 * n + (k + 1))

            def evacuate(name, store, unroll=False):
                def body(i, n, q, landed):
                    for k in range(2):
                        prep(n, q, landed, k)
                        if k == 0 and (not isinstance(n, int) or n >= 1):
                            act.wait_ge(s_free, n)
                        product(n, k)
                        ins = store(i, k, G[2 * q + k])
                        if k == 1:
                            ins.then_inc(s_free, 1)
                if on(name):
                    loop_pairs(act, name, body, unroll=unroll or name == names[-1])

            def gates(name, n_):
                def body(i, n, q, landed):
                    prep(n, q, landed, 0)
                    act.wait_ge(s_free, n - 1)
                    product(n, 0)
                    act.activation(tmp(q), G[2 * q][:, :], ACT.Sigmoid, bias=col("b_gate", i + 8 * n_))\
                       .then_inc(s_ao, 1)
                    prep(n, q, landed, 1)
                if on(name):
                    loop_pairs(act, name, body, unroll=name == names[-1])

            def squared_relu(name):
                def body(i, n, q, landed):
                    for k in range(2):
                        prep(n, q, landed, k)
                        if k == 0:
                            act.wait_ge(s_free, n - 1)
                        product(n, k)
                        act.activation(tmp(2 * q + k), G[2 * q + k][:, :], ACT.Relu).then_inc(s_ao, 1)
                    act.wait_ge(s_ao, 2 * i + (BASE[name][0] + 2))
                    for k in range(2):
                        act.activation(cut(y_hi, 2 * i + k), tmp(2 * q + k), ACT.Square).then_inc(s_yh, 1)
                if on(name):
                    loop_pairs(act, name, body, unroll=name == names[-1])

            def swiglu(name):
                def body(i, n, q, landed):
                    prep(n, q, landed, 0)
                    act.wait_ge(s_free, n - 1)
                    product(n, 0)
                    act.activation(tmp(q), G[2 * q][:, :], ACT.Silu).then_inc(s_ao, 1)
                    prep(n, q, landed, 1)
                    act.wait_ge(s_free, n + 1)
                    act.activation(cut(y_hi, i), tmp(2 + q), ACT.Copy).then_inc(s_yh, 1)
                if on(name):
                    loop_pairs(act, name, body, unroll=name == names[-1])

            def only_prep(name):
                def body(i, n, q, landed):
                    prep(n, q, landed, 0)
                    prep(n, q, landed, 1)
                if on(name):
                    loop_pairs(act, name, body, unroll=name == names[-1])

            def norm_act(r, src, n=S, hi=True, dst=None, lo_key="lo"):
                for j in range(KT):
                    if j >= 2:
                        act.wait_ge(full.sem, full.at("norm", r, j - 2))
                    act.activation(tmp(j % 2, n), src(j), ACT.Square).then_inc(norm_a.sem, norm_a.mark("square", r, j))
                act.wait_ge(norm_v.sem, norm_v.at("var", r))
                act.activation(stat[:, 0:n], stat[:, 0:n], ACT.Sqrt).then_inc(norm_a.sem, norm_a.mark("std", r))
                if hi:
                    for j in range(KT):
                        act.wait_ge(norm_v.sem, norm_v.at("xn", r, j))
                        act.activation(cut(xn_hi, j), tmp(2 + j % 2), ACT.Copy).then_inc(norm_a.sem, norm_a.mark("hi", r, j))

            def gelu(dst):
                return lambda i, k, bank: act.activation(cut(dst, 2 * i + k), bank[:, :], ACT.Gelu_apprx_tanh)

            def copy_to(dst, width=S):
                return lambda i, k, bank: act.activation(cut(dst, 2 * i + k, width), bank[:, 0:width], ACT.Copy)

            for k in range(2):
                act.wait_ge(s_load[0], LANDED[0])
                act.activation(w_hi[:, k], raw[:, 0, :, k * P:(k + 1) * P], ACT.Copy).then_inc(s_whi, 1)
            for j in range(KT):
                act.wait_ge(turn_v.sem, turn_v.at("x", j))
                if j >= 2:
                    act.wait_ge(full.sem, full.at("norm", 0, j - 2))
                act.activation(tmp(j % 2), cut(h, j), ACT.Square).then_inc(norm_a.sem, norm_a.mark("square", 0, j))
            act.wait_ge(norm_v.sem, norm_v.at("var", 0))
            act.activation(stat[:, :], stat[:, :], ACT.Sqrt).then_inc(norm_a.sem, norm_a.mark("std", 0))
            for j in range(KT):
                act.wait_ge(norm_v.sem, norm_v.at("xn", 0, j))
                act.activation(cut(xn_hi, j), tmp(2 + j % 2), ACT.Copy).then_inc(norm_a.sem, norm_a.mark("hi", 0, j))

            evacuate("u", gelu(u), unroll=True)
            evacuate("v", gelu(vt))
            if on("v"):
                for j in range(KT):
                    act.wait_ge(full.sem, full.at("v", j))
                    act.activation(v_tok[:, :, j * P:(j + 1) * P], B[BANK.get(("v", j), 0)][:, :].rearrange("p (t f) -> p t f", t=NB),
                                   ACT.Copy).then_inc(gmlp_a.sem, gmlp_a.mark("v", j))
                act.wait_ge(gmlp_v.sem, gmlp_v.at("var"))
                act.activation(small[:, 0:4], small[:, 0:4], ACT.Sqrt).then_inc(gmlp_a.sem, gmlp_a.mark("std"))
                for g in range(8):
                    act.wait_ge(gmlp_v.sem, gmlp_v.at("y", g))
                    act.activation(cut(y_hi, g), tmp(4 + g % 2), ACT.Copy).then_inc(gmlp_a.sem, gmlp_a.mark("hi", g))
            gates("ga", 0)

            if on("lru"):
                act.activation(small[:, 16:24], par[:, COL["lru_lambda"]:COL["lru_lambda"] + 8], ACT.Abs)\
                   .then_inc(lru_a.sem, lru_a.mark("abs"))
                act.wait_ge(lru_a.sem, lru_a.at("abs"))
                act.activation(small[:, 16:24], small[:, 16:24], ACT.Exp, scale=-1.0)\
                   .then_inc(lru_a.sem, lru_a.mark("exp"))
                for j in range(9):
                    if j < 8:
                        n = P0["lru"] + j
                        q = n % 2
                        prep(n, q, LANDED[n + 1], 0)
                        product(n, 0)
                        act.wait_ge(s_free, n)
                        if j >= 2:
                            act.wait_ge(lru_v.sem, lru_v.at("conv", j - 2))
                        else:
                            act.wait_ge(lru_v.sem, lru_v.at("pads"))
                        act.activation(xpad[q][:, 3:3 + S], G[2 * q][:, :], ACT.Copy).then_inc(lru_a.sem, lru_a.mark("x", j))
                        prep(n, q, LANDED[n + 1], 1)
                        product(n, 1)
                        if j >= 2:
                            act.wait_ge(lru_v.sem, lru_v.at("y", j - 2))
                        act.activation(lt[2 + j % 2], G[2 * q + 1][:, :], ACT.Gelu_apprx_tanh).then_inc(s_free, 1)
                    if j >= 1:
                        jj = j - 1
                        if jj >= 1:
                            act.wait_ge(lru_v.sem, lru_v.at("inp", jj - 1))
                        for g in range(2):
                            act.wait_ge(full.sem, full.at("ri", jj, g))
                            act.activation(lt[4 + g], B[BANK.get(("ri", jj, g), 0)][:, :], ACT.Sigmoid,
                                           bias=col(("lru_b_r", "lru_b_i")[g], jj)).then_inc(lru_a.sem, lru_a.mark("ri", jj, g))
                        act.wait_ge(lru_a.sem, lru_a.at("ri", jj, 0))
                        act.wait_ge(lru_v.sem, lru_v.at("rate"))
                        act.activation(lt[6], lt[4], ACT.Tanh, scale=small[:, 24 + jj:25 + jj])\
                           .then_inc(lru_a.sem, lru_a.mark("tanh", jj))
                        act.wait_ge(lru_a.sem, lru_a.at("tanh", jj))
                        act.activation(lt[7], lt[6], ACT.Sqrt).then_inc(lru_a.sem, lru_a.mark("sqrt", jj))
                        act.wait_ge(lru_v.sem, lru_v.at("y", jj))
                        act.activation(cut(y_hi, jj), lt[12], ACT.Copy).then_inc(lru_a.sem, lru_a.mark("hi", jj))
            gates("gb", 1)

            if on("xbc"):
                for i in range(NPAIR["xbc"]):
                    n = P0["xbc"] + i
                    q = n % 2
                    for k in range(2):
                        j = 2 * i + k
                        prep(n, q, LANDED[n + 1], k)
                        product(n, k)
                        if k == 0:
                            act.wait_ge(s_free, n)
                        act.wait_ge(xbc_v.sem, xbc_v.at("pads") if j < 4 else xbc_v.at("conv", j - 4))
                        ins = act.activation(cpad[j % 4][:, 3:3 + S], G[2 * q + k][:, :], ACT.Copy)
                        if k == 1:
                            ins.then_inc(s_free, 1)
                        else:
                            ins.then_inc(xbc_a.sem, xbc_a.mark("x", j))
                    for k in range(2):
                        j = 2 * i + k
                        act.wait_ge(xbc_v.sem, xbc_v.at("conv", j))
                        act.activation(cut(xbc, j), cacc[k], ACT.Silu).then_inc(xbc_a.sem, xbc_a.mark("silu", j))
            only_prep("dt")
            if on("dt"):
                ssd_act(act, link)
            if on("z"):
                for i in range(NPAIR["z"]):
                    n = P0["z"] + i
                    q = n % 2
                    for k in range(2):
                        prep(n, q, LANDED[n + 1], k)
                        product(n, k)
                        if k == 0:
                            act.wait_ge(s_free, n)
                        if i >= 1:
                            act.wait_ge(z_v.sem, z_v.at("gated", 2 * i - 2 + k))
                        elif k == 0:
                            act.wait_ge(ssd_v.sem, ssd_v.at("y", 3, 1))
                        ins = act.activation(tmp(2 + k), G[2 * q + k][:, :], ACT.Silu)
                        if k == 1:
                            ins.then_inc(s_free, 1)
                        else:
                            ins.then_inc(z_a.sem, z_a.mark("silu", 2 * i))
                for g in range(4):
                    for k in range(2):
                        act.wait_ge(z_v.sem, z_v.at("gated", 2 * g + k))
                        if g >= 1:
                            act.wait_ge(full.sem, full.at("zsum", g - 1))
                        act.activation(tmp(k), cut(xbc, 2 * g + k), ACT.Square).then_inc(z_a.sem, z_a.mark("square", g, k))
                    act.wait_ge(z_v.sem, z_v.at("var", g))
                    act.activation(stat[:, :], stat[:, :], ACT.Sqrt).then_inc(z_a.sem, z_a.mark("std", g))
                    for k in range(2):
                        act.wait_ge(z_v.sem, z_v.at("y", 2 * g + k))
                        act.activation(cut(y_hi, 2 * g + k), tmp(4 + k), ACT.Copy).then_inc(z_a.sem, z_a.mark("hi", 2 * g + k))
            gates("gc", 2)
            if on("wo"):
                act.wait_ge(s_free, P0["wo"])
                for j in range(KT):
                    act.activation(cut(y_hi, j), cut(merged, j), ACT.Copy).then_inc(split_a.sem, split_a.mark("merged", j))
            only_prep("wo")
            if on("up0"):
                act.wait_ge(s_free, P0["up0"])
                norm_act(1, lambda j: cut(h, j))
            for p in range(4):
                squared_relu(f"up{p}")
                only_prep(f"down{p}")
            if on("f1u00"):
                act.wait_ge(s_free, P0["f1u00"])
                norm_act(2, lambda j: cut(h, j), hi=False)
                for j in range(KT):
                    if j % 2 == 0:
                        act.wait_ge(turn_v.sem, turn_v.at("mem", j))
                    act.wait_ge(full.sem, full.at("norm", 3, j - 2) if j >= 2 else full.at("norm", 2, 6 + j))
                    act.activation(tmp(j % 2, MEM), cut(mem_t, j, MEM), ACT.Square)\
                       .then_inc(norm_a.sem, norm_a.mark("square", 3, j))
                act.wait_ge(norm_v.sem, norm_v.at("var", 3))
                act.activation(stat[:, 0:MEM], stat[:, 0:MEM], ACT.Sqrt).then_inc(norm_a.sem, norm_a.mark("std", 3))
                for c in range(2):
                    act.wait_ge(trig_v.sem, trig_v.at("angle", c))
                    act.activation(sincos[:, c, :], ang[2 + c], ACT.Sin).then_inc(trig_a.sem, trig_a.mark(c))
            for l in range(2):
                def ffn(f, r):
                    if not on(f"{f}u{l}0"):
                        return
                    act.wait_ge(s_free, P0[f"{f}u{l}0"])
                    if f == "f1" and l == 0:
                        act.wait_ge(norm_v.sem, norm_v.at("xn", 2, KT - 1))
                    norm_act(r, lambda j: cut(h, j))
                    for part in range(3):
                        swiglu(f"{f}u{l}{part}")
                        only_prep(f"{f}d{l}{part}")
                r = 4 + 5 * l
                ffn("f1", r)
                if on(f"conv{l}"):
                    act.wait_ge(s_free, P0[f"conv{l}"])
                    norm_act(r + 1, lambda j: cut(h, j))
                    for i in range(5):
                        n = P0[f"conv{l}"] + i
                        q = n % 2
                        for k in range(2):
                            prep(n, q, LANDED[n + 1], k)
                            if i == 4:
                                continue
                            product(n, k)
                            if k == 0:
                                act.wait_ge(s_free, n)
                            if i == 0 and k == 0:
                                act.wait_ge(conv_v.sem, conv_v.at("pads", l))
                            bank = G[2 * q + k][:, :]
                            ins = (act.activation(av[k][:, 30:30 + S], bank, ACT.Copy) if i == 0 else
                                   act.activation(tmp(4 + k), bank, ACT.Sigmoid) if i == 1 else
                                   act.activation(bg[k], bank, ACT.Copy) if i == 2 else
                                   act.activation(hc[k][:, 2:2 + S], bank, ACT.Copy))
                            if k == 1:
                                ins.then_inc(s_free, 1)
                            else:
                                ins.then_inc(conv_a.sem, conv_a.mark("in", l, i))
                    n = P0[f"kidx{l}"]
                    q = n % 2
                    prep(n, q, LANDED[n + 1], 0)
                    product(n, 0)
                    act.wait_ge(s_free, n)
                    act.activation(ki, G[2 * q][:, :], ACT.Copy)
                    prep(n, q, LANDED[n + 1], 1)
                    product(n, 1)
                    act.activation(wi, G[2 * q + 1][:, :], ACT.Copy).then_inc(s_free, 1)
                    evacuate(f"qidx{l}", copy_to(qi))
                    evacuate(f"q{l}", copy_to(qkv))
                    evacuate(f"k{l}", lambda i, k, bank: act.activation(cut(qkv, 4 + 2 * i + k), bank[:, :], ACT.Copy))
                    evacuate(f"vv{l}", copy_to(vt2))
                if on(f"vv{l}"):
                    for k in range(2):
                        act.wait_ge(conv_v.sem, conv_v.at("short", l, k))
                        act.activation(cut(y_hi, 2 + k), tmp(4 + k), ACT.Copy).then_inc(conv_a.sem, conv_a.mark("hi", l, 2 + k))
                    act.wait_ge(conv_v.sem, conv_v.at("stat", l, 1))
                    act.activation(stat[:, :], stat[:, :], ACT.Sqrt).then_inc(conv_a.sem, conv_a.mark("std", l))
                    for k in range(2):
                        act.wait_ge(conv_v.sem, conv_v.at("ln", l, k))
                        act.activation(cv[k], cv[k], ACT.Silu, scale=col("conf_ln_g_2", 2 * l + k),
                                       bias=col("conf_ln_b_2", 2 * l + k)).then_inc(conv_a.sem, conv_a.mark("y", l, k))
                    act.wait_ge(conv_a.sem, conv_a.at("y", l, 1))
                    for k in range(2):
                        act.activation(cut(y_hi, k), cv[k], ACT.Copy).then_inc(conv_a.sem, conv_a.mark("hi", l, k))
                    dsa_act(act, l)
                only_prep(f"mwo{l}")
                if on(f"xk{l}"):
                    act.wait_ge(s_free, P0[f"xk{l}"])
                    for j in range(KT):
                        act.wait_ge(norm_v.sem, norm_v.at("mem_xn", l, j))
                        act.activation(cut(y_hi, j)[:, 0:MEM], tmp(2 + j % 2, MEM), ACT.Copy)\
                           .then_inc(norm_a.sem, norm_a.mark("mem_hi", l, j))
                    evacuate(f"xk{l}", copy_to(xk, MEM))
                    evacuate(f"xv{l}", copy_to(xvt, MEM))
                    norm_act(r + 2, lambda j: cut(h, j))
                    evacuate(f"xq{l}", copy_to(xq))
                    if on(f"xq{l}"):
                        cross_act(act, l)
                only_prep(f"xo{l}")
                ffn("f2", r + 3)
            if whole:
                act.wait_ge(s_free, last_pair + 1)
                norm_act(14, lambda j: cut(h, j), hi=False)


        def ssd_dve(dve, link, log1p):
            n = P0["dt"]
            z, relu, e, acc, a, b = (pre[i][0:16, :] for i in (1, 4, 3, 5, 6, 7))
            link(dve.memset(stk, 0.0))
            dve.wait_ge(s_sp, 48)
            for r in range(2):
                link(dve.tensor_copy(small[64 * r:64 * r + 64, 184:192], small[64 * r:64 * r + 64, 200 + r:216:2]))
            dve.wait_ge(s_free, n)
            dve.wait_ge(s_mm, 2 * n + 2)
            dve.tensor_scalar(z, G[2 * (n % 2)][0:16, :], small[0:16, 176:177], None, ALU.add).then_inc(s_free, 1)
            dve.wait_ge(s_free, n + 1)
            dve.tensor_scalar(relu, z, 0.0, None, ALU.max).then_inc(ssd_v.sem, ssd_v.mark("z"))
            dve.wait_ge(ssd_a.sem, ssd_a.at("exp"))
            log1p(acc, e, a, b)
            link(dve.scalar_tensor_tensor(stk[0:16, :], acc, 2.0, relu, ALU.mult, ALU.add))
            link(dve.tensor_scalar(a, stk[0:16, :], small[0:16, 178:179], -1.0, ALU.mult, ALU.mult))
            for c in range(NB):
                cs = slice(c * P, (c + 1) * P)
                ins = dve.tensor_tensor_scan(acs[0:16, cs], ones[0:16, :], a[:, cs], 0.0, ALU.mult, ALU.add)
            link(ins)
            ends = acs[0:16, P - 1:S:P]
            dve.tensor_tensor(small[0:16, 32:96].rearrange("p (c h) -> p c h", c=NB),
                              ident[0:16, None, 0:16].to_broadcast([16, NB, 16]),
                              ends[:, :, None].to_broadcast([16, NB, 16]), ALU.mult).then_inc(ssd_v.sem, ssd_v.mark("ends"))
            for c in range(NB):
                ins = dve.tensor_scalar(b[:, c * P:(c + 1) * P], acs[0:16, c * P:(c + 1) * P],
                                        acs[0:16, (c + 1) * P - 1:(c + 1) * P], -1.0, ALU.subtract, ALU.mult)
            ins.then_inc(ssd_v.sem, ssd_v.mark("to_end"))
            dve.wait_ge(ssd_a.sem, ssd_a.at("sst"))

            def by_head(part, g, k):
                h0 = part + 4 * g + 2 * k
                return sst[:, :, h0:h0 + 2][:, :, :, None].to_broadcast([P, NB, 2, 64])

            for g in range(4):
                for k in range(2):
                    dve.wait_ge(full.sem, full.at("x_tok", g, k))
                    dve.tensor_tensor(xdt[:, :, k * P:(k + 1) * P].rearrange("p c (r d) -> p c r d", r=2),
                                      B[BANK.get(("x_tok", g, k), 0)][:, :].rearrange("p (c r d) -> p c r d", c=NB, r=2),
                                      by_head(0, g, k), ALU.mult).then_inc(ssd_v.sem, ssd_v.mark("xdt", g, k))
                dve.wait_ge(ssd_v.sem, ssd_v.at("xdt", g, 1))
                for k in range(2):
                    ins = dve.tensor_tensor(xdd[:, :, k * P:(k + 1) * P].rearrange("p c (r d) -> p c r d", r=2),
                                            xdt[:, :, k * P:(k + 1) * P].rearrange("p c (r d) -> p c r d", r=2),
                                            by_head(64, g, k), ALU.mult)
                ins.then_inc(ssd_v.sem, ssd_v.mark("xdd", g))
                dve.wait_ge(full.sem, full.at("cb", g))
                dve.tensor_tensor(cb[:, :, :], B[BANK.get(("cb", g), 0)][:, :].rearrange("p (c l) -> p c l", c=NB),
                                  causal[:, None, :].to_broadcast([P, NB, P]), ALU.mult)\
                   .then_inc(ssd_v.sem, ssd_v.mark("cb", g))
                dve.wait_ge(ssd_a.sem, ssd_a.at("ends"))
                dve.wait_ge(full.sem, full.at("st", g, 0))
                b0 = B[BANK.get(("st", g, 0), 0)]
                link(dve.tensor_copy(st[:, 0, :], b0[:, 0:256]))
                decay = lambda c: chunk_decay[:, c, 4 * g:4 * g + 4][:, :, None].to_broadcast([P, 4, 64])
                heads = lambda x: x.rearrange("p (r d) -> p r d", r=4)
                link(dve.tensor_tensor(heads(st[:, 1, :]), heads(st[:, 0, :]), decay(1), ALU.mult))
                dve.tensor_tensor(st[:, 1, :], st[:, 1, :], b0[:, 256:512], ALU.add).then_inc(ssd_v.sem, ssd_v.mark("st", g, 0))
                dve.wait_ge(ssd_v.sem, ssd_v.at("st", g, 0))
                link(dve.tensor_tensor(heads(st[:, 2, :]), heads(st[:, 1, :]), decay(2), ALU.mult))
                dve.wait_ge(full.sem, full.at("st", g, 1))
                dve.tensor_tensor(st[:, 2, :], st[:, 2, :], B[BANK.get(("st", g, 1), 0)][:, 0:256], ALU.add)\
                   .then_inc(ssd_v.sem, ssd_v.mark("st", g, 1))
                for r in range(4):
                    hh = 4 * g + r
                    dve.wait_ge(ssd_a.sem, ssd_a.at("row", g, r))
                    if (g, r) != (0, 0):
                        dve.wait_ge(ssd_v.sem, ssd_v.at("m", *((g, r - 1) if r else (g - 1, 3))))
                    dve.tensor_tensor(pre[9].rearrange("p (c l) -> p c l", c=NB),
                                      B[BANK.get(("row", g, r), 0)][:, :].rearrange("p (c l) -> p c l", c=NB),
                                      sst[:, :, 32 + hh:33 + hh].to_broadcast([P, NB, P]), ALU.subtract)\
                       .then_inc(ssd_v.sem, ssd_v.mark("seg", g, r))
                    dve.wait_ge(ssd_v.sem, ssd_v.at("seg", g, r))
                    dve.tensor_scalar(pre[9], pre[9], 0.0, None, ALU.min).then_inc(ssd_v.sem, ssd_v.mark("min", g, r))
                    if (g, r) != (0, 0):
                        dve.wait_ge(full.sem, full.at("y", *((g, r - 1) if r else (g - 1, 3))))
                    dve.tensor_tensor(tmp(0), cut(xbc, 12 + g), pre[8], ALU.mult).then_inc(ssd_v.sem, ssd_v.mark("ce", g, r))
                    if r == 2:
                        skip(dve, g, 0)
                    dve.wait_ge(ssd_a.sem, ssd_a.at("decay", g, r))
                    dve.tensor_tensor(pre[10], pre[9], cb[:, :, :].rearrange("p c l -> p (c l)"), ALU.mult)\
                       .then_inc(ssd_v.sem, ssd_v.mark("m", g, r))
                skip(dve, g, 1)

        def skip(dve, g, k):
            dve.wait_ge(full.sem, full.at("y", g, 2 * k + 1))
            x = cut(xbc, 2 * g + k)
            dve.scalar_tensor_tensor(x, x, small[:, 184 + 2 * g + k:185 + 2 * g + k], B[BANK.get(("y", g, k), 0)][:, :],
                                     ALU.mult, ALU.add).then_inc(ssd_v.sem, ssd_v.mark("y", g, k))

        def dsa_dve(dve, link, l, lo_of):
            dve.wait_ge(full.sem, full.at("w_tok", l))
            dve.tensor_copy(w_tok[:, :, :], B[BANK.get(("w_tok", l), 0)][:, :].rearrange("p (t h) -> p t h", t=NB)[:, :, 0:4])\
               .then_inc(rope_v.sem, rope_v.mark("w_tok", l))
            dve.wait_ge(trig_a.sem, trig_a.at(1))
            tiles = [("q", t) for t in range(4)] + [("k", t) for t in range(4)] + [("qi", t) for t in range(2)] + [("ki", 0)]
            for i, key in enumerate(tiles):
                x = rope_tile(key)
                dve.wait_ge(full.sem, full.at("rot", l, *key))
                dve.tensor_tensor(tmp(2 + i % 2), B[BANK.get(("rot", l) + key, 0)][:, :], sincos[:, 1, :], ALU.mult)\
                   .then_inc(rope_v.sem, rope_v.mark("rot", l, *key))
                link(dve.tensor_tensor(x, x, sincos[:, 0, :], ALU.mult))
                dve.tensor_tensor(x, x, tmp(2 + i % 2), ALU.add)
            for t in range(4):
                dve.wait_ge(full.sem, full.at("v_key", l, t))
                dve.tensor_copy(v_key[:, :, t * P:(t + 1) * P], B[BANK.get(("v_key", l, t), 0)][:, :].rearrange("p (b f) -> p b f", b=NB))\
                   .then_inc(rope_v.sem, rope_v.mark("v_key", l, t))
            for b in range(NB):
                w = (b + 1) * P
                if b:
                    for i in range(IDXH):
                        dve.wait_ge(dsa_a.sem, dsa_a.at("idx", l, b, i))
                        if i == 0:
                            ins = dve.tensor_scalar(score[:, 0:w], tmp(0, w), w_tok[:, b, 0:1], None, ALU.mult)
                        else:
                            ins = dve.scalar_tensor_tensor(score[:, 0:w], tmp(i % 2, w), w_tok[:, b, i:i + 1], score[:, 0:w],
                                                           ALU.mult, ALU.add)
                        ins.then_inc(dsa_v.sem, dsa_v.mark("idx", l, b, i))
                        dve.wait_ge(dsa_v.sem, dsa_v.at("idx", l, b, i))
                    dve.wait_ge(dsa_p.sem, dsa_p.at(l, b))
                    for n in range(TOPK // 8):
                        src = work if n else score
                        link(dve.max(small[:, 160:168], src[:, 0:w]))
                        link(dve.match_replace(work[:, 0:w], small[:, 160:168], src[:, 0:w], TAKEN))
                    link(dve.tensor_scalar(bias[:, 0:w], work[:, 0:w], TAKEN, NEG, ALU.is_gt, ALU.mult))

                def maximum(hh):
                    p = att[2] if hh % 2 else att[0]
                    m = small[:, 144 + hh % 2:145 + hh % 2]
                    dve.wait_ge(full.sem, full.at("s", l, b, hh))
                    if hh >= 2:
                        dve.wait_ge(full.sem, full.at("p", l, b, hh - 2))
                    elif b:
                        dve.wait_ge(full.sem, full.at("p", l, b - 1, 6 + hh))
                    dve.tensor_tensor_reduce(p[:, 0:w], B[BANK.get(("s", l, b, hh), 0)][:, 0:w], (bias if b else qcausal)[:, 0:w],
                                             0.125, -3.0e38, ALU.add, ALU.max, m).then_inc(dsa_v.sem, dsa_v.mark("s", l, b, hh))
                    dve.wait_ge(dsa_v.sem, dsa_v.at("s", l, b, hh))
                    dve.tensor_scalar(small[:, 146 + hh % 2:147 + hh % 2], m, -1.0, None, ALU.mult)\
                       .then_inc(dsa_v.sem, dsa_v.mark("neg", l, b, hh))

                def gather(t):
                    dve.wait_ge(full.sem, full.at("o", l, b, 2 * t + 1))
                    dve.tensor_copy(cut(o_t, t)[:, b * P:(b + 1) * P], B[BANK.get(("o", l, b, t), 0)][:, 0:P])\
                       .then_inc(dsa_v.sem, dsa_v.mark("o", l, b, t))

                maximum(0)
                for hh in range(HEADS2):
                    if hh + 1 < HEADS2:
                        maximum(hh + 1)
                    p = att[2] if hh % 2 else att[0]
                    dve.wait_ge(dsa_a.sem, dsa_a.at("exp", l, b, hh))
                    link(dve.reciprocal(small[:, 150 + hh % 2:151 + hh % 2], small[:, 148 + hh % 2:149 + hh % 2]))
                    dve.tensor_scalar(p[:, 0:w], p[:, 0:w], small[:, 150 + hh % 2:151 + hh % 2], None, ALU.mult)\
                       .then_inc(dsa_v.sem, dsa_v.mark("p", l, b, hh))
                    if hh % 2 == 0 and hh >= 2:
                        gather(hh // 2 - 1)
                gather(3)
            for t in range(4):
                dve.wait_ge(split_a.sem, split_a.at("dsa", l, t))
                lo_of(cut(y_lo, 4 + t), cut(o_t, t), cut(y_hi, 4 + t)).then_inc(split_v.sem, split_v.mark("dsa", l, t))

        def cross_dve(dve, link, l, lo_of):
            for j in range(0, KT, 2):
                dve.wait_ge(full.sem, full.at("xv", l, j))
                dve.tensor_copy(xv[:, :, j * P:(j + 2) * P].rearrange("p t (d f) -> p d t f", d=2),
                                B[BANK.get(("xv", l, j), 0)][:, :].rearrange("p (d t f) -> p d t f", d=2, t=2))\
                   .then_inc(xa_v.sem, xa_v.mark("xv", l, j))

            def maximum(x, b):
                m = small[:, 168 + b % 2:169 + b % 2]
                dve.wait_ge(full.sem, full.at("xs", l, x, b))
                link(dve.tensor_reduce(m, B[BANK.get(("xs", l, x, b), 0)][:, 0:MEM], AX.X, ALU.max))
                dve.tensor_scalar(small[:, 152 + b % 2:153 + b % 2], m, -1.0 / 16.0, None, ALU.mult)\
                   .then_inc(xa_v.sem, xa_v.mark("neg", l, x, b))

            steps = [(x, b) for x in range(4) for b in range(NB)]
            maximum(*steps[0])
            for n, (x, b) in enumerate(steps):
                if n + 1 < len(steps):
                    maximum(*steps[n + 1])
                dve.wait_ge(xa_a.sem, xa_a.at("p", l, x, b))
                link(dve.reciprocal(small[:, 156 + b % 2:157 + b % 2], small[:, 154 + b % 2:155 + b % 2]))
                dve.tensor_scalar(xp[b % 2], xp[b % 2], small[:, 156 + b % 2:157 + b % 2], None, ALU.mult)\
                   .then_inc(xa_v.sem, xa_v.mark("p", l, x, b))
                if b == NB - 1:
                    for d in range(2):
                        dve.wait_ge(xa_a.sem, xa_a.at("hi", l, 2 * x + d))
                        lo_of(cut(y_lo, 2 * x + d), B[BANK.get(("xo", l, x, d), 0)][:, :], cut(y_hi, 2 * x + d))\
                            .then_inc(xa_v.sem, xa_v.mark("lo", l, 2 * x + d))

        @block.vector
        def _(dve):
            count = {"n": 0, "more": 0}

            def link(ins):
                count["n"] += 1
                ins.then_inc(s_dve, 1)
                dve.wait_ge(s_dve, count["more"] + count["n"])

            def chained(name, body, per_pair, unroll):
                base = count["n"]

                def wrapped(i, n, q, landed):
                    count["n"] = 0
                    count["more"] = i * per_pair + base
                    body(i, n, q, landed)
                    assert count["n"] == per_pair
                if on(name):
                    loop_pairs(dve, name, wrapped, unroll=unroll or name == names[-1])
                    count["n"], count["more"] = base + per_pair * NPAIR[name], 0

            def prep_lo(n, q, k):
                if isinstance(n, int) and n + 1 > last_pair:
                    return
                dve.wait_ge(s_whi, 2 * n + (k + 3))
                dve.tensor_tensor(w_lo[:, k], raw[:, 1 - q, :, k * P:(k + 1) * P], w_hi[:, k].bitcast(F32), ALU.subtract)\
                   .then_inc(s_wlo, 1)

            def only_prep(name, extra=None):
                def body(i, n, q, landed):
                    for k in range(2):
                        prep_lo(n, q, k)
                        if extra:
                            extra(2 * i + k)
                if on(name):
                    loop_pairs(dve, name, body, unroll=name == names[-1] or P0[name] < 2)

            def product(n, k):
                dve.wait_ge(s_mm, 2 * n + (k + 1))

            def lo_of(dst, value, hi):
                return dve.tensor_tensor(dst, value, hi.bitcast(F32), ALU.subtract)

            def residual(name, scale=1.0):
                def body(i, n, q, landed):
                    for k in range(2):
                        prep_lo(n, q, k)
                        if k == 0:
                            dve.wait_ge(s_free, n)
                        product(n, k)
                        ins = dve.scalar_tensor_tensor(cut(h, 2 * i + k), G[2 * q + k][:, :], scale, cut(h, 2 * i + k),
                                                       ALU.mult, ALU.add)
                        if k == 1:
                            ins.then_inc(s_free, 1)
                if on(name):
                    loop_pairs(dve, name, body, unroll=name == names[-1])

            def gates(name, n_):
                def body(i, n, q, landed):
                    prep_lo(n, q, 0)
                    prep_lo(n, q, 1)
                    dve.wait_ge(s_free, n)
                    product(n, 1)
                    dve.wait_ge(s_ao, i + (BASE[name][0] + 1))
                    if n_ == 0:
                        dve.tensor_tensor(cut(merged, i), G[2 * q + 1][:, :], tmp(q), ALU.mult).then_inc(s_free, 1)
                    else:
                        link(dve.tensor_tensor(tmp(4 + q), G[2 * q + 1][:, :], tmp(q), ALU.mult))
                        dve.tensor_tensor(cut(merged, i), cut(merged, i), tmp(4 + q), ALU.add).then_inc(s_free, 1)
                chained(name, body, 0 if n_ == 0 else 1, False)

            def squared_relu(name):
                def body(i, n, q, landed):
                    prep_lo(n, q, 0)
                    prep_lo(n, q, 1)
                    dve.wait_ge(s_free, n)
                    dve.wait_ge(s_wlo, 2 * n + 3)
                    for k in range(2):
                        dve.wait_ge(s_ao, 2 * i + (BASE[name][0] + k + 1))
                        ins = dve.tensor_tensor(tmp(4 + k), tmp(2 * q + k), tmp(2 * q + k), ALU.mult)
                        if k == 1:
                            ins.then_inc(s_free, 1)
                    dve.wait_ge(s_free, n + 1)
                    for k in range(2):
                        dve.wait_ge(s_yh, 2 * i + (BASE[name][1] + k + 1))
                        lo_of(cut(y_lo, 2 * i + k), tmp(4 + k), cut(y_hi, 2 * i + k)).then_inc(s_yl, 1)
                if on(name):
                    loop_pairs(dve, name, body, unroll=name == names[-1])

            def swiglu(name):
                def body(i, n, q, landed):
                    prep_lo(n, q, 0)
                    prep_lo(n, q, 1)
                    dve.wait_ge(s_free, n)
                    product(n, 1)
                    dve.wait_ge(s_ao, i + (BASE[name][0] + 1))
                    dve.wait_ge(s_yl, i + (BASE[name][2] - 1))
                    dve.tensor_tensor(tmp(2 + q), G[2 * q + 1][:, :], tmp(q), ALU.mult).then_inc(s_free, 1)
                    dve.wait_ge(s_yh, i + (BASE[name][1] + 1))
                    lo_of(cut(y_lo, i), tmp(2 + q), cut(y_hi, i)).then_inc(s_yl, 1)
                if on(name):
                    loop_pairs(dve, name, body, unroll=name == names[-1])

            def scale_by(r, scale, src_bank, eps, sig, var_key, std_sig, std_key, n=S):
                dve.tensor_scalar(stat[:, 0:n], src_bank[:, 0:n], scale, eps, ALU.mult, ALU.add)\
                   .then_inc(sig.sem, sig.mark(*var_key))
                dve.wait_ge(std_sig.sem, std_sig.at(*std_key))
                link(dve.reciprocal(rstd[:, 0:n], stat[:, 0:n]))

            def norm_stats(r, n=S):
                dve.wait_ge(full.sem, full.at("norm", r, KT - 1))
                scale_by(r, 1.0 / D, B[BANK.get(("norm", r), 0)], EPS, norm_v, ("var", r), norm_a, ("std", r), n)

            def norm_dve(r, gain, g0=0):
                norm_stats(r)
                for j in range(KT + 1):
                    if 2 <= j < KT:
                        dve.wait_ge(norm_v.sem, norm_v.at("lo", r, j - 2))
                    if j < KT:
                        dve.scalar_tensor_tensor(tmp(2 + j % 2), cut(h, j), col(gain, g0 + j), rstd[:, :], ALU.mult, ALU.mult)\
                           .then_inc(norm_v.sem, norm_v.mark("xn", r, j))
                    if j >= 1:
                        dve.wait_ge(norm_a.sem, norm_a.at("hi", r, j - 1))
                        lo_of(cut(xn_lo, j - 1), tmp(2 + (j - 1) % 2), cut(xn_hi, j - 1))\
                            .then_inc(norm_v.sem, norm_v.mark("lo", r, j - 1))

            def norm_in_place(r, gain):
                norm_stats(r)
                for j in range(KT):
                    dve.scalar_tensor_tensor(cut(h, j), cut(h, j), col(gain, j), rstd[:, :], ALU.mult, ALU.mult)\
                       .then_inc(norm_v.sem, norm_v.mark("xn", r, j))

            def log1p(dst, e, a, b):
                link(dve.tensor_scalar(a, e, 2.0, None, ALU.add))
                link(dve.reciprocal(b, a))
                link(dve.tensor_tensor(a, e, b, ALU.mult))
                link(dve.tensor_tensor(b, a, a, ALU.mult))
                link(dve.tensor_scalar(dst, b, 1.0 / 17, None, ALU.mult))
                for d in range(15, 1, -2):
                    link(dve.scalar_tensor_tensor(dst, dst, 1.0 / d, b, ALU.add, ALU.mult))
                link(dve.scalar_tensor_tensor(dst, dst, 1.0, a, ALU.add, ALU.mult))

            for k in range(2):
                dve.wait_ge(s_whi, k + 1)
                dve.tensor_tensor(w_lo[:, k], raw[:, 0, :, k * P:(k + 1) * P], w_hi[:, k].bitcast(F32), ALU.subtract)\
                   .then_inc(s_wlo, 1)
            for b in range(4):
                n = sum(c for _, c in BATCHES[b])
                dve.wait_ge(full.sem, full.at("par", b))
                dve.tensor_copy(par[:, b * P:b * P + n], B[BANK.get(("par", b), 0)][:, 0:n])\
                   .then_inc(turn_v.sem, turn_v.mark("par", b))
            for j in range(KT):
                dve.wait_ge(full.sem, full.at("x", j))
                dve.tensor_copy(cut(h, j), B[BANK.get(("x", j), 0)][:, :]).then_inc(turn_v.sem, turn_v.mark("x", j))
            dve.wait_ge(turn_v.sem, turn_v.at("x", KT - 1))
            norm_dve(0, "norm_mix_g")

            only_prep("u")
            only_prep("v")
            if on("v"):
                for g in range(0, 8, 4):
                    dve.wait_ge(full.sem, full.at("w_sp", g))
                    dve.tensor_tensor(w_spT[:, g:g + 4, :], B[BANK.get(("w_sp", g), 0)][:, :].rearrange("p (g t) -> p g t", g=4),
                                      causal[:, None, :].to_broadcast([P, 4, P]), ALU.mult)\
                       .then_inc(gmlp_v.sem, gmlp_v.mark("w_sp", g))
                dve.wait_ge(gmlp_a.sem, gmlp_a.at("v", 7))
                dve.wait_ge(s_gb, 48)
                for t in range(NB):
                    s0 = 32 + 16 * t
                    for o in range(2):
                        ins = dve.bn_stats(small[:, s0 + 6 * o:s0 + 6 * o + 6], v_tok[:, t, o * S:(o + 1) * S])
                    link(ins)
                    link(dve.bn_aggr(small[:, s0 + 12:s0 + 14], small[:, s0:s0 + 12]))
                    link(dve.tensor_scalar(small[:, t:t + 1], small[:, s0 + 13:s0 + 14], EPS, None, ALU.add))
                link_mark = dve.tensor_scalar(small[:, 4:5], small[:, 0:1], 0.0, None, ALU.add)
                link_mark.then_inc(gmlp_v.sem, gmlp_v.mark("var"))
                dve.wait_ge(gmlp_a.sem, gmlp_a.at("std"))
                link(dve.reciprocal(small[:, 4:8], small[:, 0:4]))
                for t in range(NB):
                    link(dve.scalar_tensor_tensor(v_tok[:, t, :], v_tok[:, t, :], small[:, 44 + 16 * t:45 + 16 * t], g_bc,
                                                  ALU.subtract, ALU.mult))
                    dve.scalar_tensor_tensor(v_tok[:, t, :], v_tok[:, t, :], small[:, 4 + t:5 + t], b_bc, ALU.mult, ALU.add)\
                       .then_inc(gmlp_v.sem, gmlp_v.mark("normed", t))
                for g in range(9):
                    if 2 <= g < 8:
                        dve.wait_ge(gmlp_v.sem, gmlp_v.at("lo", g - 2))
                    if g < 8:
                        dve.wait_ge(full.sem, full.at("mix", g))
                        dve.tensor_tensor(tmp(g % 2).rearrange("p (c t) -> p c t", c=NB),
                                          B[BANK.get(("mix", g), 0)][:, :].rearrange("p (c t) -> p c t", c=NB),
                                          bs_bc[:, None, g * P:(g + 1) * P].to_broadcast([P, NB, P]), ALU.add)\
                           .then_inc(gmlp_v.sem, gmlp_v.mark("mixed", g))
                        dve.wait_ge(gmlp_v.sem, gmlp_v.at("mixed", g))
                        dve.tensor_tensor(tmp(4 + g % 2), tmp(g % 2), cut(u, g), ALU.mult)\
                           .then_inc(gmlp_v.sem, gmlp_v.mark("y", g))
                    if g >= 1:
                        dve.wait_ge(gmlp_a.sem, gmlp_a.at("hi", g - 1))
                        lo_of(cut(y_lo, g - 1), tmp(4 + (g - 1) % 2), cut(y_hi, g - 1))\
                            .then_inc(gmlp_v.sem, gmlp_v.mark("lo", g - 1))
            gates("ga", 0)

            if on("lru"):
                dve.wait_ge(lru_a.sem, lru_a.at("exp"))
                lam = par[:, COL["lru_lambda"]:COL["lru_lambda"] + 8]
                log1p(small[:, 40:48], small[:, 16:24], small[:, 48:56], small[:, 56:64])
                link(dve.tensor_scalar(small[:, 32:40], lam, -1.0, 0.0, ALU.mult, ALU.max))
                link(dve.scalar_tensor_tensor(small[:, 24:32], small[:, 40:48], 2.0, small[:, 32:40], ALU.mult, ALU.add))
                dve.tensor_scalar(small[:, 24:32], small[:, 24:32], 4.0, None, ALU.mult).then_inc(lru_v.sem, lru_v.mark("rate"))
                for q in range(2):
                    ins = dve.memset(xpad[q][:, 0:3], 0.0)
                ins.then_inc(lru_v.sem, lru_v.mark("pads"))
                for j in range(9):
                    if j < 8:
                        n = P0["lru"] + j
                        q = n % 2
                        prep_lo(n, q, 0)
                        prep_lo(n, q, 1)
                        dve.wait_ge(lru_a.sem, lru_a.at("x", j))
                        x = xpad[q]
                        if j >= 2:
                            dve.wait_ge(full.sem, full.at("ri", j - 2, 1))
                        link(dve.tensor_scalar(lt[j % 2], x[:, 0:S], col("lru_conv_w", j), col("lru_conv_b", j),
                                               ALU.mult, ALU.add))
                        for k in range(1, 4):
                            ins = dve.scalar_tensor_tensor(lt[j % 2], x[:, k:k + S], col("lru_conv_w", 8 * k + j), lt[j % 2],
                                                           ALU.mult, ALU.add)
                            if k < 3:
                                link(ins)
                        ins.then_inc(lru_v.sem, lru_v.mark("conv", j))
                    if j >= 1:
                        jj = j - 1
                        dve.wait_ge(lru_a.sem, lru_a.at("tanh", jj))
                        link(dve.tensor_scalar(lt[8], lt[6], 1.0, None, ALU.add))
                        dve.reciprocal(lt[9], lt[8])
                        link(dve.tensor_scalar(lt[10], lt[6], -1.0, 1.0, ALU.mult, ALU.add))
                        dve.tensor_tensor(lt[10], lt[10], lt[9], ALU.mult)
                        link(dve.tensor_tensor(lt[8], lt[5], lt[jj % 2], ALU.mult))
                        link(dve.scalar_tensor_tensor(lt[8], lt[8], 2.0, lt[9], ALU.mult, ALU.mult))
                        dve.wait_ge(lru_a.sem, lru_a.at("sqrt", jj))
                        dve.tensor_tensor(lt[11], lt[8], lt[7], ALU.mult).then_inc(lru_v.sem, lru_v.mark("inp", jj))
                        dve.wait_ge(lru_v.sem, lru_v.at("inp", jj))
                        link(dve.tensor_tensor_scan(lt[13], lt[10], lt[11], 0.0, ALU.mult, ALU.add))
                        dve.wait_ge(s_free, P0["lru"] + jj + 1)
                        dve.tensor_tensor(lt[12], lt[13], lt[2 + jj % 2], ALU.mult).then_inc(lru_v.sem, lru_v.mark("y", jj))
                        dve.wait_ge(lru_a.sem, lru_a.at("hi", jj))
                        lo_of(cut(y_lo, jj), lt[12], cut(y_hi, jj)).then_inc(lru_v.sem, lru_v.mark("lo", jj))
            gates("gb", 1)

            if on("xbc"):
                for i in range(4):
                    ins = dve.memset(cpad[i][:, 0:3], 0.0)
                ins.then_inc(xbc_v.sem, xbc_v.mark("pads"))
                for i in range(NPAIR["xbc"]):
                    n = P0["xbc"] + i
                    q = n % 2
                    prep_lo(n, q, 0)
                    prep_lo(n, q, 1)
                    for k in range(2):
                        j = 2 * i + k
                        if k == 0:
                            dve.wait_ge(xbc_a.sem, xbc_a.at("x", j))
                        else:
                            dve.wait_ge(s_free, n + 1)
                        if i >= 1:
                            dve.wait_ge(xbc_a.sem, xbc_a.at("silu", j - 2))
                        link(dve.tensor_scalar(cacc[k], cpad[j % 4][:, 0:S], col("ssd_conv_w", j), col("ssd_conv_b", j),
                                               ALU.mult, ALU.add))
                        for w in range(1, 4):
                            ins = dve.scalar_tensor_tensor(cacc[k], cpad[j % 4][:, w:w + S], col("ssd_conv_w", 16 * w + j),
                                                           cacc[k], ALU.mult, ALU.add)
                            if w < 3:
                                link(ins)
                        ins.then_inc(xbc_v.sem, xbc_v.mark("conv", j))
            only_prep("dt")
            if on("dt"):
                ssd_dve(dve, link, log1p)
            if on("z"):
                for i in range(NPAIR["z"]):
                    n = P0["z"] + i
                    q = n % 2
                    for k in range(2):
                        prep_lo(n, q, k)
                    for k in range(2):
                        if k == 0:
                            dve.wait_ge(z_a.sem, z_a.at("silu", 2 * i))
                        else:
                            dve.wait_ge(s_free, n + 1)
                        dve.tensor_tensor(cut(xbc, 2 * i + k), cut(xbc, 2 * i + k), tmp(2 + k), ALU.mult)\
                           .then_inc(z_v.sem, z_v.mark("gated", 2 * i + k))
                for g in range(4):
                    dve.wait_ge(full.sem, full.at("zsum", g))
                    scale_by(0, 1.0 / 256, B[BANK.get(("zsum", g), 0)], EPS, z_v, ("var", g), z_a, ("std", g))
                    for k in range(2):
                        j = 2 * g + k
                        dve.scalar_tensor_tensor(tmp(4 + k), cut(xbc, j), col("ssd_norm_g", j), rstd[:, :], ALU.mult, ALU.mult)\
                           .then_inc(z_v.sem, z_v.mark("y", j))
                    for k in range(2):
                        j = 2 * g + k
                        dve.wait_ge(z_a.sem, z_a.at("hi", j))
                        lo_of(cut(y_lo, j), tmp(4 + k), cut(y_hi, j)).then_inc(z_v.sem, z_v.mark("lo", j))
            gates("gc", 2)
            if on("wo"):
                for j in range(KT):
                    dve.wait_ge(split_a.sem, split_a.at("merged", j))
                    lo_of(cut(y_lo, j), cut(merged, j), cut(y_hi, j)).then_inc(split_v.sem, split_v.mark("merged", j))
            residual("wo")
            if on("up0"):
                norm_dve(1, "norm_mlp_g")
            for p in range(4):
                squared_relu(f"up{p}")
                residual(f"down{p}")

            if on("f1u00"):
                norm_in_place(2, "final_norm_g")
                for j in range(0, KT, 2):
                    dve.wait_ge(full.sem, full.at("mem", j))
                    dve.tensor_copy(mem_t[:, j * MEM:(j + 2) * MEM], B[BANK.get(("mem", j), 0)][:, :])\
                       .then_inc(turn_v.sem, turn_v.mark("mem", j))
                dve.wait_ge(turn_v.sem, turn_v.at("mem", 6))
                norm_stats(3, MEM)
                link(dve.tensor_tensor(memn.rearrange("p (j m) -> p j m", j=KT), mem_t.rearrange("p (j m) -> p j m", j=KT),
                                       rstd[:, None, 0:MEM].to_broadcast([P, KT, MEM]), ALU.mult))
                dve.wait_ge(s_pos, 16)
                link(dve.tensor_copy(ang[0], ang[4].bitcast(I32)))
                link(dve.tensor_scalar(ang[1], ang[0], inv_freq, None, ALU.mult))
                for c in range(2):
                    link(dve.tensor_scalar(ang[0], ang[1], 1.0 / (2 * np.pi), 0.25 * (1 - c), ALU.mult, ALU.add))
                    link(dve.tensor_scalar(ang[0], ang[0], ROUND, ROUND, ALU.add, ALU.subtract))
                    link(dve.scalar_tensor_tensor(ang[2 + c], ang[0], -TURN[0], ang[1], ALU.mult, ALU.add))
                    for part in TURN[1:]:
                        link(dve.scalar_tensor_tensor(ang[2 + c], ang[0], -part, ang[2 + c], ALU.mult, ALU.add))
                    link(dve.tensor_scalar(ang[2 + c], ang[2 + c], (1 - c) * np.pi / 2, PI, ALU.add, ALU.min))
                    dve.tensor_scalar(ang[2 + c], ang[2 + c], -PI, None, ALU.max).then_inc(trig_v.sem, trig_v.mark("angle", c))
            for l in range(2):
                def ffn(f, r):
                    if not on(f"{f}u{l}0"):
                        return
                    norm_dve(r, "ffn1_norm_2" if f == "f1" else "ffn2_norm_2", 8 * l)
                    for part in range(3):
                        swiglu(f"{f}u{l}{part}")
                        residual(f"{f}d{l}{part}", 0.5)
                r = 4 + 5 * l
                ffn("f1", r)
                if on(f"conv{l}"):
                    norm_dve(r + 1, "mix_norm_2", 8 * l)
                    for k in range(2):
                        dve.memset(av[k][:, 0:30], 0.0)
                        ins = dve.memset(hc[k][:, 0:2], 0.0)
                    ins.then_inc(conv_v.sem, conv_v.mark("pads", l))
                    for i in range(5):
                        n = P0[f"conv{l}"] + i
                        q = n % 2
                        for k in range(2):
                            prep_lo(n, q, k)
                        if i == 1:
                            dve.wait_ge(conv_a.sem, conv_a.at("in", l, 1))
                            dve.tensor_tensor(av[0][:, 30:30 + S], av[0][:, 30:30 + S], tmp(4), ALU.mult)
                            dve.wait_ge(s_free, n + 1)
                            link(dve.tensor_tensor(av[1][:, 30:30 + S], av[1][:, 30:30 + S], tmp(5), ALU.mult))
                        if i == 4:
                            dve.wait_ge(s_free, n)
                            for k in range(2):
                                product(n, k)
                                ins = dve.tensor_tensor(hc[k][:, 2:2 + S], hc[k][:, 2:2 + S], G[2 * q + k][:, :], ALU.mult)
                            ins.then_inc(s_free, 1)
                            dve.wait_ge(s_free, n + 1)
                    total = sum(NPAIR[f"{x}{l}"] for x in ("kidx", "qidx", "q", "k", "vv")) * 2
                    step = {"at": 0}

                    def taps(_):
                        a = step["at"] * 4
                        step["at"] += 1
                        conv_taps(l, a, a + 4 if step["at"] < total else 2 * CONV_TAPS + 8)

                    def conv_taps(l, a, b):
                        for t in range(a, min(b, 2 * CONV_TAPS + 8)):
                            if t < 2 * CONV_TAPS:
                                k, t = t % 2, t // 2
                                w = col("conf_dw_2", (l * CONV_TAPS + t) * 2 + k)
                                x = av[k][:, t:t + S]
                                if t == 0:
                                    ins = dve.tensor_scalar(cv[k], x, w, col("conf_dw_b_2", 2 * l + k), ALU.mult, ALU.add)
                                else:
                                    ins = dve.scalar_tensor_tensor(cv[k], x, w, cv[k], ALU.mult, ALU.add)
                                if t == CONV_TAPS - 1:
                                    ins.then_inc(conv_v.sem, conv_v.mark("summand", l, 0, k))
                                    continue
                            else:
                                t -= 2 * CONV_TAPS
                                k, t = t % 2, t // 2
                                if t < 3:
                                    w = col("sc_dw_2", (l * 3 + t) * 2 + k)
                                    x = hc[k][:, t:t + S]
                                    if t == 0:
                                        ins = dve.tensor_scalar(tmp(2 + k), x, w, None, ALU.mult)
                                    else:
                                        ins = dve.scalar_tensor_tensor(tmp(2 + k), x, w, tmp(2 + k), ALU.mult, ALU.add)
                                else:
                                    dve.tensor_tensor(tmp(4 + k), tmp(2 + k), bg[k], ALU.mult)\
                                       .then_inc(conv_v.sem, conv_v.mark("short", l, k))
                                    continue
                            link(ins)

                    for x in ("kidx", "qidx", "q", "k", "vv"):
                        only_prep(f"{x}{l}", taps)
                if on(f"vv{l}"):
                    dve.wait_ge(full.sem, full.at("cln", l, 0))
                    dve.tensor_scalar(stat[:, :], B[BANK.get(("cln", l, 0), 0)][:, :], 1.0 / 256, None, ALU.mult)\
                       .then_inc(conv_v.sem, conv_v.mark("stat", l, 0))
                    dve.wait_ge(conv_v.sem, conv_v.at("stat", l, 0))
                    for k in range(2):
                        link(dve.tensor_tensor(cv[k], cv[k], stat[:, :], ALU.subtract))
                        dve.tensor_tensor(tmp(k), cv[k], cv[k], ALU.mult).then_inc(conv_v.sem, conv_v.mark("summand", l, 1, k))
                    for k in range(2):
                        dve.wait_ge(conv_a.sem, conv_a.at("hi", l, 2 + k))
                        lo_of(cut(y_lo, 2 + k), tmp(4 + k), cut(y_hi, 2 + k)).then_inc(conv_v.sem, conv_v.mark("short_lo", l, k))
                    dve.wait_ge(full.sem, full.at("cln", l, 1))
                    scale_by(0, 1.0 / 256, B[BANK.get(("cln", l, 1), 0)], LN_EPS_2, conv_v, ("stat", l, 1), conv_a, ("std", l))
                    for k in range(2):
                        dve.tensor_tensor(cv[k], cv[k], rstd[:, :], ALU.mult).then_inc(conv_v.sem, conv_v.mark("ln", l, k))
                    for k in range(2):
                        dve.wait_ge(conv_a.sem, conv_a.at("hi", l, k))
                        lo_of(cut(y_lo, k), cv[k], cut(y_hi, k)).then_inc(conv_v.sem, conv_v.mark("lo", l, k))
                    dsa_dve(dve, link, l, lo_of)
                residual(f"mwo{l}")
                if on(f"xk{l}"):
                    for j in range(KT + 1):
                        if 2 <= j < KT:
                            dve.wait_ge(norm_v.sem, norm_v.at("mem_lo", l, j - 2))
                        if j < KT:
                            dve.tensor_scalar(tmp(2 + j % 2, MEM), cut(memn, j, MEM), col("mem_norm_2", 8 * l + j), None, ALU.mult)\
                               .then_inc(norm_v.sem, norm_v.mark("mem_xn", l, j))
                        if j >= 1:
                            dve.wait_ge(norm_a.sem, norm_a.at("mem_hi", l, j - 1))
                            lo_of(cut(y_lo, j - 1)[:, 0:MEM], tmp(2 + (j - 1) % 2, MEM), cut(y_hi, j - 1)[:, 0:MEM])\
                                .then_inc(norm_v.sem, norm_v.mark("mem_lo", l, j - 1))
                    only_prep(f"xk{l}")
                    only_prep(f"xv{l}")
                    norm_dve(r + 2, "xa_norm_2", 8 * l)
                    only_prep(f"xq{l}")
                    if on(f"xq{l}"):
                        cross_dve(dve, link, l, lo_of)
                residual(f"xo{l}")
                ffn("f2", r + 3)
            if whole:
                norm_in_place(14, "final_norm_2")
                for t in range(NB):
                    for o in range(2):
                        dve.wait_ge(full.sem, full.at("out", t, o))
                        dve.tensor_copy(v_out(t)[:, o * S:(o + 1) * S], B[BANK.get(("out", t, o), 0)][:, :])\
                           .then_inc(turn_v.sem, turn_v.mark("out", t, o))

        @block.gpsimd
        def _(pool):
            pool.dma_start(x_in[:, :, :], A["x"][0].rearrange("(t p) d -> p t d", p=P)).then_inc(s_x, 16)
            pool.dma_start(consts[:, :], A["consts"]).then_inc(s_const, 16)
            for b, items in enumerate(BATCHES):
                r = 0
                for n, c in items:
                    v = A[n]
                    if len(v.shape) > 1:
                        v = v.rearrange({2: "a b -> (a b)", 3: "a b c -> (a b c)"}[len(v.shape)])
                    pool.dma_start(prow[r:r + c, b, :], v.rearrange("(r p) -> r p", p=P)).then_inc(s_par, 16)
                    r += c
            pool.dma_start(small[0:16, 176:177], A["ssd_dt_bias"].rearrange("o h -> h o")).then_inc(s_sp, 16)
            pool.dma_start(small[0:16, 177:178], A["ssd_a_log"].rearrange("o h -> h o")).then_inc(s_sp, 16)
            pool.dma_start(w_sp[:, :, :], A["gmlp_w_s"][0].rearrange("g t s -> t g s")).then_inc(s_gw, 16)
            for dst, src in ((g_bc, A["gmlp_ln_g"]), (b_bc, A["gmlp_ln_b"]),
                             (bs_bc, A["gmlp_b_s"].rearrange("o g t -> o (g t)"))):
                pool.dma_start(dst, src.to_broadcast([P, D])).then_inc(s_gb, 16)
            if on("lru"):
                pool.wait_ge(gmlp_v.sem, gmlp_v.at("lo", 7))
                for g, w in enumerate(("lru_w_r", "lru_w_i")):
                    pool.dma_start(lru_w[:, g, :, :], A[w][0].rearrange("h i j -> i h j")).then_inc(s_lw, 16)
            if on("dt"):
                pool.dma_start(small[:, 200:216], A["ssd_d"].to_broadcast([P, 16])).then_inc(s_sp, 16)
            if on("f1u00"):
                pool.wait_ge(s_mm, 2 * P0["up0"] + 2)
                pool.dma_start(mem_in[:, :, :], A["mem_2"][0].rearrange("(t p) d -> p t d", p=P)).then_inc(s_mem, 16)
                pool.dma_start(ang[4].bitcast(I32), A["positions_2"].to_broadcast([P, S])).then_inc(s_pos, 16)
            for l in range(2):
                if on(f"vv{l}"):
                    for b in range(1, NB):
                        pool.wait_ge(dsa_v.sem, dsa_v.at("idx", l, b, IDXH - 1))
                        pool.affine_select(out=score[:, b * P:(b + 1) * P], in_=score[:, b * P:(b + 1) * P],
                                           compare_op=ALU.is_ge, fill=NEG, base=0, pattern=[[-1, P]],
                                           channel_multiplier=1).then_inc(dsa_p.sem, dsa_p.mark(l, b))


def constants():
    i = np.arange(P)
    ident = np.eye(P, dtype=np.float32)
    ones = np.ones((P, P), np.float32)
    causal = (i[None, :] >= i[:, None]).astype(np.float32)
    rot = np.zeros((P, P), np.float32)
    for m in range(P):
        if m % 64 < 32:
            rot[m + 32, m] = -1.0
        else:
            rot[m - 32, m] = 1.0
    qcausal = np.where(i[None, :] <= i[:, None], 0.0, NEG).astype(np.float32)
    freq = np.float32(10000.0) ** (-np.arange(0, 64, 2, dtype=np.float32) / np.float32(64))
    return np.concatenate([ident, ones, causal, rot, qcausal, np.tile(freq, 4)[:, None].astype(np.float32)], axis=1)


NAMES = ["x", "norm_mix_g", "w_in", "b_gate", "gmlp_ln_g", "gmlp_ln_b", "gmlp_w_s", "gmlp_b_s", "lru_conv_w", "lru_conv_b",
         "lru_w_r", "lru_b_r", "lru_w_i", "lru_b_i", "lru_lambda", "ssd_conv_w", "ssd_conv_b", "ssd_dt_bias",
         "ssd_a_log", "ssd_d", "ssd_norm_g", "w_branch_a", "w_branch_b", "w_branch_c", "w_out", "norm_mlp_g",
         "w_mlp_up", "w_mlp_down", "final_norm_g", "mem_2", "positions_2", "ffn1_norm_2", "ffn1_w_gate_2",
         "ffn1_w_up_2", "ffn1_w_down_2", "mix_norm_2", "w_in_2", "conf_dw_2", "conf_dw_b_2", "conf_ln_g_2",
         "conf_ln_b_2", "sc_dw_2", "w_out_2", "xa_norm_2", "mem_norm_2", "xa_wq_2", "xa_wkv_2", "xa_wo_2",
         "ffn2_norm_2", "ffn2_w_gate_2", "ffn2_w_up_2", "ffn2_w_down_2", "final_norm_2"]


def kernel(**inputs):
    import concourse.bacc as bacc
    import concourse.bass_utils as bass_utils

    arrays = {f"in_{n}": np.ascontiguousarray(inputs[n]) for n in NAMES}
    arrays["in_consts"] = constants()

    def build():
        nc = bacc.Bacc("TRN2", target_bir_lowering=False, num_devices=1)
        A = {n[3:]: nc.dram_tensor(n, a.shape, mybir.dt.from_np(a.dtype), kind="ExternalInput").ap()
             for n, a in arrays.items()}
        out = nc.dram_tensor("out_0", (1, S, D), F32, kind="ExternalOutput").ap()
        build_program(nc, A, out)
        return nc

    build()
    nc = build()
    r = bass_utils.run_bass_kernel_spmd(nc, [arrays], core_ids=[0])
    return r.results[0]["out_0"]
```

```python
from contextlib import ExitStack

import numpy as np

import concourse.bass as bass
from concourse import mybir

P = 128
S = 512
D = 1024
KT = D // P
NB = S // P
MEM = 256
EPS = 1e-6
LN_EPS_2 = 1e-5
F_GMLP_U, F_GMLP_V, F_LRU_X, F_LRU_G, F_Z, F_XBC, F_DT, F_GATE = 0, 1024, 2048, 3072, 4096, 5120, 7168, 7184
FFN_PARTS = (8, 8, 6)
DFF = 2816
HEADS2, IDXH = 8, 4
TOPK = 128
NEG = -1.0e30
TAKEN = -3.0e38
IDX_SCALE = 0.0625
CONV_TAPS = 31

F32 = mybir.dt.float32
F32R = mybir.dt.float32r
I32 = mybir.dt.int32
ACT = mybir.ActivationFunctionType
ALU = mybir.AluOpType
AX = mybir.AxisListType

BATCHES = [
    [("norm_mix_g", 8), ("b_gate", 24), ("lru_conv_b", 8), ("lru_b_r", 8), ("lru_b_i", 8),
     ("lru_lambda", 8), ("ssd_conv_b", 16), ("ssd_norm_g", 8), ("norm_mlp_g", 8), ("final_norm_g", 8),
     ("final_norm_2", 8)],
    [("lru_conv_w", 32), ("ssd_conv_w", 64), ("conf_dw_b_2", 4), ("conf_ln_g_2", 4), ("conf_ln_b_2", 4),
     ("sc_dw_2", 12)],
    [("ffn1_norm_2", 16), ("mix_norm_2", 16), ("xa_norm_2", 16), ("mem_norm_2", 16), ("ffn2_norm_2", 16)],
    [("conf_dw_2", 124)],
]
COL = {}
for _b, _items in enumerate(BATCHES):
    _r = 0
    for _n, _c in _items:
        COL[_n] = _b * P + _r
        _r += _c
    assert _r <= P
N_PARAM_DMAS = sum(len(b) for b in BATCHES)

PHASES = [("u", 4, 8), ("v", 4, 8), ("ga", 8, 8), ("lru", 8, 8), ("gb", 8, 8), ("xbc", 8, 8), ("dt", 1, 8),
          ("z", 4, 8), ("gc", 8, 8), ("wo", 4, 8)]
for _p in range(4):
    PHASES += [(f"up{_p}", 4, 8), (f"down{_p}", 4, 8)]
for _l in range(2):
    for _i, _n in enumerate(FFN_PARTS):
        PHASES += [(f"f1u{_l}{_i}", _n, 8), (f"f1d{_l}{_i}", 4, _n)]
    PHASES += [(f"conv{_l}", 5, 8), (f"kidx{_l}", 1, 8), (f"qidx{_l}", 1, 8), (f"q{_l}", 2, 8), (f"k{_l}", 2, 8),
               (f"vv{_l}", 2, 8),
               (f"mwo{_l}", 4, 8), (f"xq{_l}", 4, 8), (f"xk{_l}", 4, 8), (f"xv{_l}", 4, 8), (f"xo{_l}", 4, 8)]
    for _i, _n in enumerate(FFN_PARTS):
        PHASES += [(f"f2u{_l}{_i}", _n, 8), (f"f2d{_l}{_i}", 4, _n)]
P0, NPAIR, KTS = {}, {}, {}
_at = 0
for _name, _n, _k in PHASES:
    P0[_name], NPAIR[_name], KTS[_name] = _at, _n, _k
    _at += _n
TOTAL = _at
BANK = {}
ROUND = 12582912.0
PI = 3.1415925
TURN = (6.28125, 0.001934051513671875, 1.2556659146e-06)


def three_dmas(name):
    return name.startswith("kidx")


def kind(name):
    if name in ("ga", "gb", "gc"):
        return "gated"
    if name.startswith("up"):
        return "relu2"
    if name[:3] in ("f1u", "f2u"):
        return "swiglu"
    return ""


INCS = {"gated": (1, 0, 0), "relu2": (1, 2, 2), "swiglu": (2, 2, 1), "": (0, 0, 0)}
BASE = {}
_acc = [0, 0, 0]
for _name, _n, _k in PHASES:
    BASE[_name] = tuple(_acc)
    _acc = [a + _n * d for a, d in zip(_acc, INCS[kind(_name)])]
LANDED = []
_slot = [0, 0]
for _name, _n, _k in PHASES:
    for _i in range(_n):
        _s = len(LANDED) % 2
        _slot[_s] += 48 if three_dmas(_name) else 32
        LANDED.append(_slot[_s])
LANDED.append(0)


def loop_pairs(eng, name, body, unroll=False, peel=0):
    count, p0 = NPAIR[name], P0[name]
    if unroll or count - peel < 4:
        peel = count
    for i in range(peel):
        body(i, p0 + i, (p0 + i) % 2, LANDED[p0 + i + 1])
    times = (count - peel) // 2
    if times:
        p1 = p0 + peel
        with eng.Fori(0, times) as it:
            for b in range(2):
                body(2 * it + (peel + b), 2 * it + (p1 + b), (p1 + b) % 2, it * 32 + LANDED[p1 + b + 1])
    for i in range(peel + 2 * times, count):
        body(i, p0 + i, (p0 + i) % 2, LANDED[p0 + i + 1])


def _acc_at(name):
    return BASE[name][2] + INCS[kind(name)][2] * NPAIR[name]


class Signal:
    marks = {}

    def __init__(self, sem, name):
        self.sem, self.name, self.n = sem, name, 0

    def mark(self, *key):
        self.n += 1
        Signal.marks[self.name, key] = self.n
        return 1

    def total(self):
        return max([v for (n, k), v in Signal.marks.items() if n == self.name], default=0)

    def at(self, *key):
        return Signal.marks.get((self.name, key), 1)


def cut(t, i, n=S):
    if isinstance(i, int):
        return t[:, i * n:(i + 1) * n]
    return t[:, bass.ds(i * n, n)]


def build_program(nc, A, out, dbg=None, stop=None):
    names = [n for n, _, _ in PHASES]
    if stop:
        names = names[:names.index(stop) + 1]
    last_pair = P0[names[-1]] + NPAIR[names[-1]] - 1
    whole = not stop

    def on(name):
        return name in names

    with ExitStack() as ctx:
        def sb(name, shape, dt=F32):
            return ctx.enter_context(nc.sbuf_tensor(name, shape, dt))

        def sem(name):
            return ctx.enter_context(nc.semaphore(name))

        def signal(name):
            return Signal(sem(name), name)

        raw = sb("raw", [P, 2, KT, 256])
        w_hi = sb("w_hi", [P, 2, KT, P], F32R)
        w_lo = sb("w_lo", [P, 2, KT, P], F32R)
        xn_hi = sb("xn_hi", [P, KT * S], F32R)
        xn_lo = sb("xn_lo", [P, KT * S], F32R)
        y_hi = sb("y_hi", [P, KT * S], F32R)
        y_lo = sb("y_lo", [P, KT * S], F32R)
        h = sb("h", [P, KT * S])
        consts = sb("consts", [P, 5 * P + 1])
        ident, ones, causal, rot, qcausal = (consts[:, i * P:(i + 1) * P] for i in range(5))
        inv_freq = consts[:, 5 * P:5 * P + 1]
        par = sb("par", [P, 4 * P])
        temps = sb("temps", [P, 6 * S])
        stat = sb("stat", [P, S])
        rstd = sb("rstd", [P, S])
        small = sb("small", [P, 256])
        size = 37 * S
        arena = sb("arena", [P, size])

        def tmp(i, n=S):
            return temps[:, i * S:i * S + n]

        def at(off, *shape):
            n = int(np.prod(shape))
            assert off + n <= size, (off, shape, size)
            v = arena[:, off:off + n]
            if len(shape) == 1:
                return v
            dims = "abcd"[:len(shape)]
            return v.rearrange(f"p ({' '.join(dims)}) -> p {' '.join(dims)}", **dict(zip(dims[:-1], shape[:-1])))

        def col(name, i=0, rows=P):
            if isinstance(i, int):
                return par[0:rows, COL[name] + i:COL[name] + i + 1]
            return par[0:rows, bass.ds(i + COL[name], 1)]

        G = [ctx.enter_context(nc.psum_tensor(f"G{i}", [P, S], F32)) for i in range(4)]
        B = [ctx.enter_context(nc.psum_tensor(f"B{i}", [P, S], F32)) for i in range(4)] + G

        s_load = [sem("s_load0"), sem("s_load1")]
        s_whi, s_wlo = sem("s_weights_hi"), sem("s_weights_lo")
        s_mm, s_free = sem("s_panels_multiplied"), sem("s_pairs_evacuated")
        s_ao, s_yh, s_yl = sem("s_evacuated_part"), sem("s_y_hi"), sem("s_y_lo")
        s_const, s_par, s_x, s_gw, s_gb, s_lw, s_sp, s_mem, s_pos, s_out = (sem("s_" + n) for n in (
            "const_in", "params_in", "x_in", "gmlp_w_in", "gmlp_rows_in", "lru_w_in", "ssd_params_in", "mem_in",
            "pos_in", "out"))
        full = signal("s_bank_full")
        norm_a, norm_v = signal("s_norm_act"), signal("s_norm_vector")
        turn_a, turn_v = signal("s_turned_out_act"), signal("s_turned_out_vector")
        gmlp_v, gmlp_a, gmlp_p = signal("s_gmlp_vector"), signal("s_gmlp_act"), signal("s_gmlp_pool")
        lru_v, lru_a = signal("s_lru_vector"), signal("s_lru_act")
        xbc_v, xbc_a = signal("s_xbc_vector"), signal("s_xbc_act")
        ssd_v, ssd_a = signal("s_ssd_vector"), signal("s_ssd_act")
        z_v, z_a = signal("s_z_vector"), signal("s_z_act")
        split_a, split_v = signal("s_split_hi"), signal("s_split_lo")
        trig_v, trig_a = signal("s_angles"), signal("s_sines")
        rope_v = signal("s_rope")
        conv_v, conv_a = signal("s_conv_vector"), signal("s_conv_act")
        dsa_v, dsa_a, dsa_p = signal("s_dsa_vector"), signal("s_dsa_act"), signal("s_dsa_masked")
        xa_v, xa_a = signal("s_cross_vector"), signal("s_cross_act")
        s_dve, s_act = sem("s_vector_chain"), sem("s_act_chain")
        loads_free = signal("s_loads_free")

        T = S
        MERGED = 0
        merged = arena[:, 0:8 * T]
        u = arena[:, 8 * T:16 * T]
        vt = arena[:, 16 * T:24 * T]
        v_tok = at(24 * T, NB, D)
        w_sp = at(32 * T, 8, P)
        w_spT = at(34 * T, 8, P)
        g_bc, b_bc, bs_bc = at(0, D), at(D, D), at(2 * D, D)
        x_in = at(8 * T, NB, D)
        prow = at(16 * T, 4, P)
        lru_w = at(8 * T, 2, 8, P)
        xpad = [at(12 * T + q * (S + 3), S + 3) for q in range(2)]
        lt = [at(12 * T + 2 * (S + 3) + i * T, T) for i in range(16)]
        xbc = arena[:, 8 * T:24 * T]
        sst = at(24 * T, NB, 96)
        chunk_decay = at(24 * T + 384, NB, 16)
        acs = at(25 * T, T)
        pre = [at((26 + i) * T, T) for i in range(11)]
        stk = pre[0]
        b_tok = at(26 * T, NB, P)
        xdt = at(27 * T, NB, 256)
        xdd = at(29 * T, NB, 256)
        cb = at(31 * T, NB, P)
        st = at(32 * T, 3, 256)
        cpad = [at(26 * T + i * (S + 3), S + 3) for i in range(4)]
        cacc = [at(31 * T + i * T, T) for i in range(2)]
        memn = arena[:, 0:8 * MEM]
        sincos = at(4 * T, 2, T)
        mem_in = at(6 * T, 2, D)
        mem_t = arena[:, 10 * T:14 * T]
        ang = [at((14 + i) * T, T) for i in range(5)]
        qkv = arena[:, 6 * T:14 * T]
        qi = arena[:, 14 * T:16 * T]
        ki = arena[:, 16 * T:17 * T]
        vt2 = arena[:, 17 * T:21 * T]
        wi = arena[:, 21 * T:22 * T]
        v_key = at(22 * T, NB, 512)
        w_tok = small[:, 128:144].rearrange("p (t h) -> p t h", h=4)
        av = [at(22 * T + k * (S + 30), S + 30) for k in range(2)]
        hc = [at(24 * T + 128 + k * (S + 2), S + 2) for k in range(2)]
        bg = [at((27 + k) * T, T) for k in range(2)]
        cv = [at((35 + k) * T, T) for k in range(2)]
        score, work = at(26 * T, T), at(27 * T, T)
        bias = [at(28 * T, T), at(21 * T, T)]
        att = [at((29 + i) * T, T) for i in range(4)]
        o_t = arena[:, 33 * T:37 * T]
        sincos_r = at(33 * T, 2, T)
        mem_rstd = at(20 * T, MEM)
        xq = arena[:, 6 * T:14 * T]
        xk = arena[:, 14 * T:18 * T]
        xvt = arena[:, 18 * T:22 * T]
        xv = at(22 * T, 2, D)
        xp = [at(26 * T + i * MEM, MEM) for i in range(2)]
        xpt = [at((27 + 2 * i) * T, 2, S) for i in range(2)]

        def source(name, i):
            nk = KTS[name]
            l = int(name[-1]) if name[-1].isdigit() else 0

            def columns(W, c0, r0=0):
                v = W[r0:r0 + nk * P, bass.ds(c0, 256)].rearrange("(k p) n -> p k n", p=P)
                hk = nk // 2
                return [((slice(0, hk), slice(0, 256)), v[:, 0:hk, :]), ((slice(hk, nk), slice(0, 256)), v[:, hk:nk, :])]

            def two(W1, c1, W2, c2):
                return [((slice(0, 8), slice(0, P)), W1[:, bass.ds(c1, P)].rearrange("(k p) n -> p k n", p=P)),
                        ((slice(0, 8), slice(P, 256)), W2[:, bass.ds(c2, P)].rearrange("(k p) n -> p k n", p=P))]

            w_in = A["w_in"][0]
            if name in ("u", "v", "xbc", "z"):
                return columns(w_in, i * 256 + {"u": F_GMLP_U, "v": F_GMLP_V, "xbc": F_XBC, "z": F_Z}[name])
            if name in ("ga", "gb", "gc"):
                return two(w_in, i * P + (F_GATE + "abc".index(name[1]) * D), A["w_branch_" + name[1]][0], i * P)
            if name == "lru":
                return two(w_in, i * P + F_LRU_X, w_in, i * P + F_LRU_G)
            if name == "dt":
                v = w_in[:, F_DT:F_DT + 16].rearrange("(k p) n -> p k n", p=P)
                return [((slice(a, a + 4), slice(0, 16)), v[:, a:a + 4, :]) for a in (0, 4)]
            if name == "wo":
                return columns(A["w_out"][0], i * 256)
            if name.startswith("up"):
                return columns(A["w_mlp_up"][0], i * 256 + l * D)
            if name.startswith("down"):
                return columns(A["w_mlp_down"][0], i * 256, l * D)
            if name[0] == "f":
                layer, part = int(name[3]), int(name[4])
                k0 = sum(FFN_PARTS[:part]) * P
                f = "ffn" + name[1]
                if name[2] == "u":
                    return two(A[f + "_w_gate_2"][layer], i * P + k0, A[f + "_w_up_2"][layer], i * P + k0)
                return columns(A[f + "_w_down_2"][layer], i * 256, k0)
            w2, n = A["w_in_2"][l], name[:-1]
            if n == "kidx":
                v = w2[:, 3072:3136].rearrange("(k p) n -> p k n", p=P)
                w = w2[:, 3136:3140].rearrange("(k p) n -> p k n", p=P)
                return [((slice(0, 8), slice(0, 64)), v), ((slice(0, 8), slice(64, P)), v),
                        ((slice(0, 8), slice(P, P + 4)), w)]
            first = {"conv": 0, "q": 1280, "k": 1792, "vv": 2304, "qidx": 2816}
            if n in first:
                return columns(w2, i * 256 + first[n])
            W, c0 = {"mwo": ("w_out_2", 0), "xk": ("xa_wkv_2", 0), "xv": ("xa_wkv_2", D), "xq": ("xa_wq_2", 0),
                     "xo": ("xa_wo_2", 0)}[n]
            return columns(A[W][l], i * 256 + c0)

        def v_out(t):
            return arena[:, (2 * t) * T:(2 * t + 2) * T]

        steps = [(b, hh) for b in range(NB) for hh in range(HEADS2)]
        rotations = {"q": [("qi", 0), ("qi", 1), ("ki", 0)], "k": [("q", t) for t in range(4)],
                     "vv": [("k", t) for t in range(4)]}
        mean_step, square_step, root_step = -2, 0, 2

        def topk_rounds(hh):
            return {1: range(0, 4), 2: range(4, 7), 3: range(7, 10), 4: range(10, 13), 5: range(13, 16)}.get(hh, ())

        def rope_tile(key):
            kind_, t = key
            return {"q": lambda: cut(qkv, t), "k": lambda: cut(qkv, 4 + t), "qi": lambda: cut(qi, t), "ki": lambda: ki}[kind_]()

        def att_p(s):
            return att[2 * (s % 2)]

        def att_pt(s):
            return att[2 * (s % 2) + 1]

        block = ctx.enter_context(nc.Block())

        @block.sync
        def _(sp):
            for name in names:
                def load(i, n, q, landed):
                    if not isinstance(n, int) or n >= 2:
                        sp.wait_ge(s_wlo, 2 * n - 2)
                    for (ks, cs), src in source(name, i):
                        sp.dma_start(raw[:, q, ks, cs], src).then_inc(s_load[q], 16)
                loop_pairs(sp, name, load, unroll=P0[name] < 2)
            if whole:
                for t in range(NB):
                    sp.wait_ge(turn_v.sem, turn_v.at("out", t, 1))
                    sp.dma_start(out[0, t * P:(t + 1) * P, :], v_out(t)).then_inc(s_out, 16)
                sp.wait_ge(s_out, 16 * NB)
            else:
                sp.wait_ge(s_free, last_pair + 1)
                for s_, v_ in [(s_yl, _acc_at(names[-1]))] + [(x.sem, x.total()) for x in (split_v, lru_v, gmlp_v, norm_v, ssd_v, rope_v, dsa_v, xa_v, z_v, conv_v)]:
                    if v_:
                        sp.wait_ge(s_, v_)
                sp.dma_start(dbg["h"], h[:, :]).then_inc(s_out, 16)
                sp.dma_start(dbg["y"], y_hi[:, :].bitcast(F32)).then_inc(s_out, 16)
                sp.wait_ge(s_out, 32)

        def ssd_pe(pe, take, turn):
            pe.wait_ge(ssd_a.sem, ssd_a.at("stk"))
            turn(("sst",), [stk[:, c * P:(c + 1) * P] for c in range(NB)], (ssd_a, ("sst",)))
            pe.wait_ge(ssd_v.sem, ssd_v.at("ends"))
            bank = take(("ends",), (ssd_a, ("ends",)))
            pe.matmul(bank[:, 0:64], ones[0:16, :], small[0:16, 32:96], start=True, stop=True)\
              .then_inc(full.sem, full.mark("ends"))
            for g in range(4):
                bt, ct = cut(xbc, 8 + g), cut(xbc, 12 + g)
                if g == 0:
                    pe.wait_ge(xbc_a.sem, xbc_a.at("silu", 15))
                turn(("b_tok", g), [bt[:, c * P:(c + 1) * P] for c in range(NB)], (ssd_a, ("b_tok", g)))
                for k in range(2):
                    turn(("x_tok", g, k), [cut(xbc, 2 * g + k)[:, c * P:(c + 1) * P] for c in range(NB)],
                         (ssd_v, ("xdt", g, k)))
                bank = take(("cb", g), (ssd_v, ("cb", g)))
                for c in range(NB):
                    cs = slice(c * P, (c + 1) * P)
                    m = pe.matmul(bank[:, cs], bt[:, cs], ct[:, cs], start=True, stop=True)
                m.then_inc(full.sem, full.mark("cb", g))
                pe.wait_ge(ssd_a.sem, ssd_a.at("b_tok", g))
                pe.wait_ge(ssd_v.sem, ssd_v.at("xdd", g))
                for o in range(2):
                    bank = take(("st", g, o), (ssd_v, ("st", g, o)))
                    for c in range(2 * o, min(2 * o + 2, 3)):
                        m = pe.matmul(bank[:, (c % 2) * 256:(c % 2) * 256 + 256], b_tok[:, c, :], xdd[:, c, :],
                                      start=True, stop=True)
                    m.then_inc(full.sem, full.mark("st", g, o))

                def row(r):
                    hh = 4 * g + r
                    bank = take(("row", g, r), (ssd_v, ("seg", g, r)))
                    pe.matmul(bank[:, :], ident[0:16, hh:hh + 1].to_broadcast([16, P]), acs[0:16, :],
                              start=True, stop=True).then_inc(full.sem, full.mark("row", g, r))
                row(0)
                for r in range(4):
                    if r % 2 == 0:
                        bank = take(("y", g, r // 2), (ssd_v, ("y", g, r // 2)))
                    if r < 3:
                        row(r + 1)
                    pe.wait_ge(ssd_v.sem, ssd_v.at("m", g, r))
                    if r == 0:
                        pe.wait_ge(ssd_v.sem, ssd_v.at("st", g, 1))
                    o = bank[64 * (r % 2):64 * (r % 2) + 64, :]
                    for c in range(NB):
                        cs = slice(c * P, (c + 1) * P)
                        m = pe.matmul(o[:, cs], xdt[:, c, 64 * r:64 * r + 64], pre[10][:, cs], start=True, stop=c == 0)
                        if c:
                            m = pe.matmul(o[:, cs], st[:, c - 1, 64 * r:64 * r + 64], tmp(0)[:, cs],
                                          start=False, stop=True)
                    m.then_inc(full.sem, full.mark("y", g, r))

        def dsa_pe(pe, l, take, turn):
            turn(("w_tok", l), [wi[:, t * P:(t + 1) * P] for t in range(NB)], (rope_v, ("w_tok", l)))
            for t in range(4):
                turn(("v_key", l, t), [cut(vt2, t)[:, b * P:(b + 1) * P] for b in range(NB)], (rope_v, ("v_key", l, t)))
            pe.wait_ge(rope_v.sem, rope_v.at("tile", l, "k", 3))

            def scores(s):
                b, hh = steps[s]
                o, w = 64 * (hh % 2), (b + 1) * P
                bank = take(("s", l, s), (dsa_v, ("s", l, s)))
                pe.matmul(bank[:, 0:w], cut(qkv, hh // 2)[o:o + 64, b * P:(b + 1) * P],
                          cut(qkv, 4 + hh // 2)[o:o + 64, 0:w], start=True, stop=True)\
                  .then_inc(full.sem, full.mark("s", l, s))

            def index_scores(b):
                w = (b + 1) * P
                for i in range(IDXH):
                    o = 64 * (i % 2)
                    bank = take(("idx", l, b, i), (dsa_a, ("idx", l, b, i)))
                    pe.matmul(bank[:, 0:w], cut(qi, i // 2)[o:o + 64, b * P:(b + 1) * P], ki[o:o + 64, 0:w],
                              start=True, stop=True).then_inc(full.sem, full.mark("idx", l, b, i))

            def sums(step):
                bank = take(("cln", l, step), (conv_v, ("stat", l, step)))
                for k in range(2):
                    pe.wait_ge(conv_v.sem, conv_v.at("summand", l, step, k))
                    m = pe.matmul(bank[:, :], ones, cv[k] if step == 0 else tmp(2 + k), start=k == 0, stop=k == 1)
                m.then_inc(full.sem, full.mark("cln", l, step))

            obank = None
            for i in range(-3, len(steps)):
                if i + 3 < len(steps):
                    scores(i + 3)
                if i >= 0 and steps[i][1] == 0 and steps[i][0] + 1 < NB:
                    index_scores(steps[i][0] + 1)
                if i == mean_step:
                    sums(0)
                if i == square_step:
                    sums(1)
                if i >= 0:
                    b, hh = steps[i]
                    if i == 0:
                        pe.wait_ge(rope_v.sem, rope_v.at("v_key", l, 3))
                    if hh % 2 == 0:
                        obank = take(("o", l, b, hh // 2), (dsa_v, ("o", l, b, hh // 2)))
                    pe.wait_ge(dsa_a.sem, dsa_a.at("pt", l, i))
                    o = 64 * (hh % 2)
                    for t in range(b + 1):
                        m = pe.matmul(obank[o:o + 64, 0:P], v_key[:, t, hh * 64:hh * 64 + 64],
                                      att_pt(i)[:, t * P:(t + 1) * P], start=t == 0, stop=t == b)
                    m.then_inc(full.sem, full.mark("o", l, b, hh))
                if 0 <= i + 1 < len(steps):
                    pe.wait_ge(dsa_a.sem, dsa_a.at("p", l, i + 1))
                    turn(("p", l, i + 1), [att_p(i + 1)[:, t * P:(t + 1) * P] for t in range(steps[i + 1][0] + 1)],
                         (dsa_a, ("pt", l, i + 1)))

        def cross_pe(pe, l, take, turn):
            pe.wait_ge(s_free, P0[f"xv{l}"] + 4)
            for j in range(0, KT, 2):
                turn(("xv", l, j), [xvt[:, (j + d) * MEM + t * P:(j + d) * MEM + (t + 1) * P] for d in range(2) for t in range(2)],
                     (xa_v, ("xv", l, j)))
            pe.wait_ge(xa_v.sem, xa_v.at("xv", l, 6))

            def scores(x, b):
                bank = take(("xs", l, x, b), (xa_a, ("p", l, x, b)))
                for d in range(2):
                    m = pe.matmul(bank[:, 0:MEM], cut(xq, 2 * x + d)[:, b * P:(b + 1) * P], cut(xk, 2 * x + d, MEM),
                                  start=d == 0, stop=d == 1)
                m.then_inc(full.sem, full.mark("xs", l, x, b))

            steps = [(x, b) for x in range(4) for b in range(NB)]
            scores(*steps[0])
            for n, (x, b) in enumerate(steps):
                if n + 1 < len(steps):
                    scores(*steps[n + 1])
                pe.wait_ge(xa_v.sem, xa_v.at("p", l, x, b))
                turn(("xp", l, x, b), [xp[b % 2][:, t * P:(t + 1) * P] for t in range(2)], (xa_a, ("pt", l, x, b)))
                if b == NB - 1:
                    pe.wait_ge(xa_a.sem, xa_a.at("pt", l, x, b))
                    for d in range(2):
                        bank = take(("xo", l, x, d), (xa_v, ("lo", l, 2 * x + d)))
                        for t in range(2):
                            m = pe.matmul(bank[:, :], xv[:, t, (2 * x + d) * P:(2 * x + d + 1) * P],
                                          xpt[x % 2][:, t, :], start=t == 0, stop=t == 1)
                        m.then_inc(full.sem, full.mark("xo", l, x, d))

        banks = {}

        @block.tensor
        def _(pe):
            banks.update(next=0, count=4, until=[None] * 8)

            def wide(on_):
                banks["count"] = 8 if on_ else 4
                if not on_:
                    for b in range(4, 8):
                        if banks["until"][b] is not None:
                            s_, k_ = banks["until"][b]
                            pe.wait_ge(s_.sem, s_.at(*k_))
                        banks["until"][b] = None

            def take(key, until):
                b = banks["next"] % banks["count"]
                banks["next"] += 1
                if banks["until"][b] is not None:
                    s_, k_ = banks["until"][b]
                    pe.wait_ge(s_.sem, s_.at(*k_))
                banks["until"][b] = until
                BANK[key] = b
                return B[b]

            def turn(key, blocks, until, idn=None):
                bank, m = take(key, until), None
                for o, src in enumerate(blocks):
                    m = pe.transpose(bank[0:src.shape[1], o * P:o * P + src.shape[0]], src,
                                     ident[0:src.shape[0], 0:src.shape[0]])
                m.then_inc(full.sem, full.mark(*key))

            def panel(k, bank, hi, lo, nk, n, ready=None):
                m = None
                for kt in range(nk):
                    if ready:
                        ready(k, kt)
                    for t, (a, b) in enumerate(((w_hi, hi), (w_hi, lo), (w_lo, hi))):
                        m = pe.matmul(bank[:, 0:n], a[:, k, kt, :], b[:, kt * S:kt * S + n],
                                      start=(kt == 0 and t == 0), stop=(kt == nk - 1 and t == 2))
                return m

            def pair(name, i, n, q, first, second, width, ready=None, after=None):
                if not isinstance(n, int) or n >= 2:
                    pe.wait_ge(s_free, n - 1)
                for k, (hi, lo) in enumerate((first, second)):
                    pe.wait_ge(s_wlo, 2 * n + (k + 1))
                    panel(k, G[2 * q + k], hi, lo, KTS[name], width, ready if isinstance(i, int) and i == 0 else None)\
                        .then_inc(s_mm, 1)
                    if after and isinstance(i, int):
                        after(i, k)

            xn, y = (xn_hi, xn_lo), (y_hi, y_lo)

            def gemm(name, first, second=None, width=S, unroll=False, ready=None, after=None):
                if on(name):
                    loop_pairs(pe, name,
                               lambda i, n, q, landed: pair(name, i, n, q, first, second or first, width, ready, after),
                               unroll=unroll or P0[name] < 2, peel=2 if ready else 0)

            def norm_pe(r, n=S):
                bank = take(("norm", r), (norm_v, ("var", r)))
                pe.wait_ge(norm_v.sem, norm_v.at("summed", r, KT - 1))
                pe.matmul(bank[:, 0:n], ones, stat[:, 0:n], start=True, stop=True)\
                  .then_inc(full.sem, full.mark("norm", r))

            def by_tile(sig, key, panel_=0):
                def ready(k, kt):
                    if k == panel_:
                        pe.wait_ge(sig.sem, sig.at(*key, kt))
                return ready

            def sums_after_first(r):
                return lambda i, k: norm_pe(r) if (i, k) == (0, 0) else None

            def y_ready(base, nk):
                def ready(k, kt):
                    if k == 0:
                        pe.wait_ge(s_yl, base - (nk - 1 - kt))
                return ready

            pe.wait_ge(s_const, 16)
            pe.wait_ge(s_par, 16 * N_PARAM_DMAS)
            for b in range(4):
                n = sum(c for _, c in BATCHES[b])
                turn(("par", b), [prow[0:n, b, :]], (turn_v, ("par", b)))
            pe.wait_ge(s_x, 16)
            for j in range(KT):
                turn(("x", j), [x_in[:, t, j * P:(j + 1) * P] for t in range(NB)], (turn_v, ("x", j)))
            norm_pe(0)
            gemm("u", xn, unroll=True, ready=by_tile(norm_v, ("lo", 0)))
            gemm("v", xn)
            if on("v"):
                pe.wait_ge(s_gw, 16)
                for g in range(0, 8, 4):
                    turn(("w_sp", g), [w_sp[:, g + i, :] for i in range(4)], (gmlp_v, ("w_sp", g)))
                pe.wait_ge(s_free, P0["v"] + 4)
                for j in range(KT):
                    turn(("v", j), [vt[:, j * S + t * P:j * S + (t + 1) * P] for t in range(NB)], (gmlp_a, ("v", j)))
                pe.wait_ge(gmlp_v.sem, gmlp_v.at("normed", NB - 1))
                for g in range(8):
                    bank = take(("mix", g), (gmlp_v, ("mixed", g)))
                    for c in range(NB):
                        m = pe.matmul(bank[:, c * P:(c + 1) * P], v_tok[:, c, g * P:(g + 1) * P], w_spT[:, g, :],
                                      start=True, stop=True)
                    m.then_inc(full.sem, full.mark("mix", g))
            gemm("ga", xn, y, ready=by_tile(gmlp_v, ("lo",), 1))
            if on("lru"):
                pe.wait_ge(s_lw, 32)
                for j in range(9):
                    if j < 8:
                        n = P0["lru"] + j
                        pair("lru", j, n, n % 2, xn, xn, S)
                    if j >= 1:
                        jj = j - 1
                        pe.wait_ge(lru_v.sem, lru_v.at("conv", jj))
                        for g in range(2):
                            bank = take(("ri", jj, g), (lru_a, ("ri", jj, g)))
                            pe.matmul(bank[:, :], lru_w[:, g, jj, :], lt[jj % 2], start=True, stop=True)\
                              .then_inc(full.sem, full.mark("ri", jj, g))
            gemm("gb", xn, y, ready=by_tile(lru_v, ("lo",), 1))
            gemm("xbc", xn, unroll=True)
            gemm("dt", xn)
            if on("dt"):
                ssd_pe(pe, take, turn)
            gemm("z", xn, unroll=True)
            if on("z"):
                for g in range(4):
                    bank = take(("zsum", g), (z_v, ("var", g)))
                    for k in range(2):
                        pe.wait_ge(z_a.sem, z_a.at("square", g, k))
                        m = pe.matmul(bank[:, :], ones, tmp(k), start=k == 0, stop=k == 1)
                    m.then_inc(full.sem, full.mark("zsum", g))
            gemm("gc", xn, y, ready=by_tile(z_v, ("lo",), 1))
            gemm("wo", y, ready=by_tile(split_v, ("merged",)))
            for p in range(4):
                gemm(f"up{p}", xn, ready=None if p else by_tile(norm_v, ("lo", 1)), after=None if p else sums_after_first(1))
                gemm(f"down{p}", y, ready=y_ready(BASE[f"down{p}"][2], 8))
            if on("f1u00"):
                norm_pe(2)

            def memory(i, k):
                if (i, k) == (0, 0):
                    pe.wait_ge(s_mem, 16)
                    for j in range(0, KT, 2):
                        turn(("mem", j), [mem_in[:, t, (j + d) * P:(j + d + 1) * P] for d in range(2) for t in range(2)],
                             (turn_v, ("mem", j)))
                if (i, k) == (2, 0):
                    norm_pe(3, MEM)
            for l in range(2):
                def ffn(f, r):
                    if not on(f"{f}u{l}0"):
                        return
                    for part in range(3):
                        gemm(f"{f}u{l}{part}", xn, ready=None if part else by_tile(norm_v, ("lo", r)),
                             after=None if part else sums_after_first(r))
                        first = (f, l, part) == ("f1", 0, 0)
                        gemm(f"{f}d{l}{part}", y, ready=y_ready(BASE[f"{f}d{l}{part}"][2], FFN_PARTS[part]),
                             after=memory if first else None, unroll=first)
                r = 4 + 5 * l
                ffn("f1", r)
                gemm(f"conv{l}", xn, unroll=True, ready=by_tile(norm_v, ("lo", r + 1)), after=sums_after_first(r + 1))
                def rotate(name):
                    def after(i, k):
                        if 2 * i + k < len(rotations[name]):
                            kind_, t = key = rotations[name][2 * i + k]
                            pe.wait_ge(s_free, P0[{"qi": "qidx", "ki": "kidx"}.get(kind_, kind_) + str(l)] + t // 2 + 1)
                            bank = take(("rot", l) + key, (rope_v, ("rot", l) + key))
                            pe.matmul(bank[:, :], rot, rope_tile(key), start=True, stop=True)\
                              .then_inc(full.sem, full.mark("rot", l, *key))
                    return after

                for name in ("kidx", "qidx", "q", "k", "vv"):
                    gemm(f"{name}{l}", xn, after=rotate(name) if name in rotations else None)
                if on(f"vv{l}"):
                    pe.wait_ge(s_free, P0[f"vv{l}"] + 2)
                    wide(True)
                    dsa_pe(pe, l, take, turn)
                    wide(False)
                if on(f"mwo{l}"):
                    pe.wait_ge(conv_v.sem, conv_v.at("lo", l, 1))
                    pe.wait_ge(split_v.sem, split_v.at("dsa", l, 3))
                gemm(f"mwo{l}", y)
                gemm(f"xq{l}", xn, ready=by_tile(norm_v, ("lo", r + 2)), after=sums_after_first(r + 2))
                gemm(f"xk{l}", y, width=MEM, ready=by_tile(norm_v, ("mem_lo", l)))
                gemm(f"xv{l}", y, width=MEM)
                if on(f"xv{l}"):
                    cross_pe(pe, l, take, turn)
                gemm(f"xo{l}", y, ready=by_tile(xa_v, ("lo", l)))
                ffn("f2", r + 3)
            if whole:
                norm_pe(14)
                pe.wait_ge(norm_v.sem, norm_v.at("xn", 14, KT - 1))
                for t in range(NB):
                    for o in range(2):
                        turn(("out", t, o), [cut(h, 4 * o + j)[:, t * P:(t + 1) * P] for j in range(4)],
                             (turn_v, ("out", t, o)))


        def ssd_act(act, link):
            act.wait_ge(s_sp, 48)
            act.activation(small[0:16, 178:179], small[0:16, 177:178], ACT.Exp).then_inc(ssd_a.sem, ssd_a.mark("a"))
            act.wait_ge(ssd_v.sem, ssd_v.at("z"))
            link(act.activation(pre[2][0:16, :], pre[1][0:16, :], ACT.Abs))
            act.activation(pre[3][0:16, :], pre[2][0:16, :], ACT.Exp, scale=-1.0).then_inc(ssd_a.sem, ssd_a.mark("exp"))
            act.wait_ge(ssd_v.sem, ssd_v.at("to_end"))
            act.activation(stk[32:48, :], acs[0:16, :], ACT.Copy)
            act.activation(stk[64:80, :], pre[7][0:16, :], ACT.Exp).then_inc(ssd_a.sem, ssd_a.mark("stk"))
            act.wait_ge(full.sem, full.at("sst"))
            act.activation(sst[:, :, :], B[BANK.get(("sst",), 0)][:, :].rearrange("p (c n) -> p c n", c=NB)[:, :, 0:96], ACT.Copy)\
               .then_inc(ssd_a.sem, ssd_a.mark("sst"))
            act.wait_ge(full.sem, full.at("ends"))
            act.activation(chunk_decay[:, :, :].rearrange("p c h -> p (c h)"), B[BANK.get(("ends",), 0)][:, 0:64], ACT.Exp)\
               .then_inc(ssd_a.sem, ssd_a.mark("ends"))
            for g in range(4):
                act.wait_ge(full.sem, full.at("b_tok", g))
                if g:
                    act.wait_ge(full.sem, full.at("st", g - 1, 1))
                act.activation(b_tok[:, :, :].rearrange("p c n -> p (c n)"), B[BANK.get(("b_tok", g), 0)][:, :], ACT.Copy)\
                   .then_inc(ssd_a.sem, ssd_a.mark("b_tok", g))
                for r in range(4):
                    act.wait_ge(full.sem, full.at("row", g, r))
                    if (g, r) != (0, 0):
                        act.wait_ge(ssd_v.sem, ssd_v.at("ce", *((g, r - 1) if r else (g - 1, 3))))
                    act.activation(pre[8], B[BANK.get(("row", g, r), 0)][:, :], ACT.Exp).then_inc(ssd_a.sem, ssd_a.mark("row", g, r))
                    act.wait_ge(ssd_v.sem, ssd_v.at("min", g, r))
                    act.activation(pre[9], pre[9], ACT.Exp).then_inc(ssd_a.sem, ssd_a.mark("decay", g, r))

        def dsa_act(act, l):
            for k in range(2):
                act.wait_ge(conv_v.sem, conv_v.at("short", l, k))
                act.activation(cut(y_hi, 2 + k), tmp(4 + k), ACT.Copy).then_inc(conv_a.sem, conv_a.mark("hi", l, 2 + k))
            for i in range(-2, len(steps)):
                if i >= 0 and steps[i][1] == 0 and steps[i][0] + 1 < NB:
                    b = steps[i][0] + 1
                    w = (b + 1) * P
                    for n in range(IDXH):
                        act.wait_ge(full.sem, full.at("idx", l, b, n))
                        if n >= 2 or b >= 2:
                            act.wait_ge(dsa_v.sem, dsa_v.at("idx", l, *((b, n - 2) if n >= 2 else (b - 1, n + 2))))
                        act.activation(tmp(n % 2, w), B[BANK.get(("idx", l, b, n), 0)][:, 0:w], ACT.Relu, scale=IDX_SCALE)\
                           .then_inc(dsa_a.sem, dsa_a.mark("idx", l, b, n))
                s = i + 1
                if 0 <= s < len(steps):
                    w = (steps[s][0] + 1) * P
                    act.wait_ge(dsa_v.sem, dsa_v.at("inverse", l, s))
                    act.activation(att_p(s)[:, 0:w], att_p(s)[:, 0:w], ACT.Copy, scale=small[:, 150 + s % 2:151 + s % 2])\
                       .then_inc(dsa_a.sem, dsa_a.mark("p", l, s))
                s = i + 2
                if s < len(steps):
                    w = (steps[s][0] + 1) * P
                    act.wait_ge(dsa_v.sem, dsa_v.at("neg", l, s))
                    act.activation(att_p(s)[:, 0:w], att_p(s)[:, 0:w], ACT.Exp, bias=small[:, 146 + s % 2:147 + s % 2],
                                   accum_out=small[:, 148 + s % 2:149 + s % 2]).then_inc(dsa_a.sem, dsa_a.mark("exp", l, s))
                s = i + 1
                if 0 <= s < len(steps):
                    w = (steps[s][0] + 1) * P
                    act.wait_ge(full.sem, full.at("p", l, s))
                    act.activation(att_pt(s)[:, 0:w], B[BANK.get(("p", l, s), 0)][:, 0:w], ACT.Copy)\
                       .then_inc(dsa_a.sem, dsa_a.mark("pt", l, s))
                if i == root_step:
                    act.wait_ge(conv_v.sem, conv_v.at("stat", l, 1))
                    act.activation(stat[:, :], stat[:, :], ACT.Sqrt).then_inc(conv_a.sem, conv_a.mark("std", l))
                if i == root_step + 1:
                    for k in range(2):
                        act.wait_ge(conv_v.sem, conv_v.at("ln", l, k))
                        act.activation(cv[k], cv[k], ACT.Silu, scale=col("conf_ln_g_2", 2 * l + k),
                                       bias=col("conf_ln_b_2", 2 * l + k)).then_inc(conv_a.sem, conv_a.mark("y", l, k))
                    act.wait_ge(conv_a.sem, conv_a.at("y", l, 1))
                    for k in range(2):
                        act.activation(cut(y_hi, k), cv[k], ACT.Copy).then_inc(conv_a.sem, conv_a.mark("hi", l, k))
            for t in range(4):
                act.wait_ge(dsa_v.sem, dsa_v.at("o", l, NB - 1, t))
                act.activation(cut(y_hi, 4 + t), cut(o_t, t), ACT.Copy).then_inc(split_a.sem, split_a.mark("dsa", l, t))

        def cross_act(act, l):
            for x in range(4):
                for b in range(NB):
                    act.wait_ge(xa_v.sem, xa_v.at("neg", l, x, b))
                    act.activation(xp[b % 2], B[BANK.get(("xs", l, x, b), 0)][:, 0:MEM], ACT.Exp, scale=1.0 / 16.0,
                                   bias=small[:, 152 + b % 2:153 + b % 2],
                                   accum_out=small[:, 154 + b % 2:155 + b % 2]).then_inc(xa_a.sem, xa_a.mark("p", l, x, b))
                    act.wait_ge(full.sem, full.at("xp", l, x, b))
                    act.activation(xpt[x % 2][:, :, b * P:(b + 1) * P],
                                   B[BANK.get(("xp", l, x, b), 0)][:, 0:MEM].rearrange("p (t q) -> p t q", t=2), ACT.Copy)\
                       .then_inc(xa_a.sem, xa_a.mark("pt", l, x, b))
                for d in range(2):
                    act.wait_ge(full.sem, full.at("xo", l, x, d))
                    act.activation(cut(y_hi, 2 * x + d), B[BANK.get(("xo", l, x, d), 0)][:, :], ACT.Copy)\
                       .then_inc(xa_a.sem, xa_a.mark("hi", l, 2 * x + d))

        @block.scalar
        def _(act):
            chain = [0]

            def link(ins):
                chain[0] += 1
                ins.then_inc(s_act, 1)
                act.wait_ge(s_act, chain[0])

            def prep(n, q, landed, k):
                if isinstance(n, int) and n + 1 > last_pair:
                    return
                act.wait_ge(s_load[1 - q], landed)
                act.wait_ge(s_mm, 2 * n + (k + 1))
                act.activation(w_hi[:, k], raw[:, 1 - q, :, k * P:(k + 1) * P], ACT.Copy).then_inc(s_whi, 1)

            def product(n, k):
                act.wait_ge(s_mm, 2 * n + (k + 1))

            def evacuate(name, store, unroll=False):
                def body(i, n, q, landed):
                    for k in range(2):
                        prep(n, q, landed, k)
                        if k == 0 and (not isinstance(n, int) or n >= 1):
                            act.wait_ge(s_free, n)
                        product(n, k)
                        ins = store(i, k, G[2 * q + k])
                        if k == 1:
                            ins.then_inc(s_free, 1)
                if on(name):
                    loop_pairs(act, name, body, unroll=unroll or name == names[-1])

            def gates(name, n_):
                def body(i, n, q, landed):
                    prep(n, q, landed, 0)
                    act.wait_ge(s_free, n - 1)
                    product(n, 0)
                    act.activation(tmp(q), G[2 * q][:, :], ACT.Sigmoid, bias=col("b_gate", i + 8 * n_))\
                       .then_inc(s_ao, 1)
                    prep(n, q, landed, 1)
                if on(name):
                    loop_pairs(act, name, body, unroll=name == names[-1])

            def squared_relu(name, r=None):
                def body(i, n, q, landed):
                    prep(n, q, landed, 0)
                    if r is not None and isinstance(i, int) and i == 0:
                        root(r)
                    prep(n, q, landed, 1)
                    for k in range(2):
                        if k == 0:
                            act.wait_ge(s_ao, i + (BASE[name][0] + 1))
                        else:
                            act.wait_ge(s_free, n + 1)
                        act.activation(cut(y_hi, 2 * i + k), tmp(2 * q + k), ACT.Square).then_inc(s_yh, 1)
                if on(name):
                    loop_pairs(act, name, body, unroll=name == names[-1], peel=0 if r is None else 2)

            def swiglu(name, r=None):
                def body(i, n, q, landed):
                    prep(n, q, landed, 0)
                    if r is not None and isinstance(i, int) and i == 0:
                        root(r)
                    act.wait_ge(s_ao, 2 * i + (BASE[name][0] + 1))
                    act.activation(tmp(q), tmp(q), ACT.Silu).then_inc(s_yh, 1)
                    prep(n, q, landed, 1)
                    act.wait_ge(s_ao, 2 * i + (BASE[name][0] + 2))
                    act.activation(cut(y_hi, i), tmp(2 + q), ACT.Copy).then_inc(s_yh, 1)
                if on(name):
                    loop_pairs(act, name, body, unroll=name == names[-1], peel=0 if r is None else 2)

            def only_prep(name, more=None):
                def body(i, n, q, landed):
                    for k in range(2):
                        prep(n, q, landed, k)
                        if more:
                            more(i, k, n)
                if on(name):
                    loop_pairs(act, name, body, unroll=bool(more) or name == names[-1])

            def root(r, n=S):
                act.wait_ge(norm_v.sem, norm_v.at("var", r))
                act.activation(stat[:, 0:n], stat[:, 0:n], ACT.Sqrt).then_inc(norm_a.sem, norm_a.mark("std", r))

            def norm_tile(r, j, gain=None, g0=0):
                if gain:
                    act.activation(cut(xn_hi, j), cut(h, j), ACT.Copy, scale=col(gain, g0 + j))\
                       .then_inc(norm_a.sem, norm_a.mark("hi", r, j))
                if j >= 3:
                    act.wait_ge(norm_v.sem, norm_v.at("summed", r, j - 2))
                act.activation(tmp(j % 2) if j else stat[:, :], cut(h, j), ACT.Square)\
                   .then_inc(norm_a.sem, norm_a.mark("square", r, j))

            def follow(name, r, gain=None, g0=0):
                def more(i, k, n):
                    if k == 0:
                        act.wait_ge(norm_v.sem, norm_v.at("h", r, 2 * i))
                    else:
                        act.wait_ge(s_free, n + 1)
                    norm_tile(r, 2 * i + k, gain, g0)
                only_prep(name, more)

            def gelu(dst):
                return lambda i, k, bank: act.activation(cut(dst, 2 * i + k), bank[:, :], ACT.Gelu_apprx_tanh)

            def copy_to(dst, width=S):
                return lambda i, k, bank: act.activation(cut(dst, 2 * i + k, width), bank[:, 0:width], ACT.Copy)

            for k in range(2):
                act.wait_ge(s_load[0], LANDED[0])
                act.activation(w_hi[:, k], raw[:, 0, :, k * P:(k + 1) * P], ACT.Copy).then_inc(s_whi, 1)
            for j in range(KT):
                act.wait_ge(turn_v.sem, turn_v.at("x", j))
                norm_tile(0, j)
            root(0)
            for j in range(KT):
                act.wait_ge(norm_v.sem, norm_v.at("xn", 0, j))
                act.activation(cut(xn_hi, j), tmp(2 + j % 2), ACT.Copy).then_inc(norm_a.sem, norm_a.mark("hi", 0, j))

            evacuate("u", gelu(u), unroll=True)
            evacuate("v", gelu(vt))
            if on("v"):
                for j in range(KT):
                    act.wait_ge(full.sem, full.at("v", j))
                    act.activation(v_tok[:, :, j * P:(j + 1) * P], B[BANK.get(("v", j), 0)][:, :].rearrange("p (t f) -> p t f", t=NB),
                                   ACT.Copy).then_inc(gmlp_a.sem, gmlp_a.mark("v", j))
                act.wait_ge(gmlp_v.sem, gmlp_v.at("var"))
                act.activation(small[:, 0:4], small[:, 0:4], ACT.Sqrt).then_inc(gmlp_a.sem, gmlp_a.mark("std"))
                for g in range(8):
                    act.wait_ge(gmlp_v.sem, gmlp_v.at("y", g))
                    act.activation(cut(y_hi, g), tmp(4 + g % 2), ACT.Copy).then_inc(gmlp_a.sem, gmlp_a.mark("hi", g))
            gates("ga", 0)

            if on("lru"):
                act.activation(small[:, 16:24], par[:, COL["lru_lambda"]:COL["lru_lambda"] + 8], ACT.Abs)\
                   .then_inc(lru_a.sem, lru_a.mark("abs"))
                act.wait_ge(lru_a.sem, lru_a.at("abs"))
                act.activation(small[:, 16:24], small[:, 16:24], ACT.Exp, scale=-1.0)\
                   .then_inc(lru_a.sem, lru_a.mark("exp"))
                for j in range(9):
                    if j < 8:
                        n = P0["lru"] + j
                        q = n % 2
                        prep(n, q, LANDED[n + 1], 0)
                        product(n, 0)
                        act.wait_ge(s_free, n)
                        if j >= 2:
                            act.wait_ge(lru_v.sem, lru_v.at("conv", j - 2))
                        else:
                            act.wait_ge(lru_v.sem, lru_v.at("pads"))
                        act.activation(xpad[q][:, 3:3 + S], G[2 * q][:, :], ACT.Copy).then_inc(lru_a.sem, lru_a.mark("x", j))
                        prep(n, q, LANDED[n + 1], 1)
                        product(n, 1)
                        if j >= 2:
                            act.wait_ge(lru_v.sem, lru_v.at("y", j - 2))
                        act.activation(lt[2 + j % 2], G[2 * q + 1][:, :], ACT.Gelu_apprx_tanh).then_inc(s_free, 1)
                    if j >= 1:
                        jj = j - 1
                        if jj >= 1:
                            act.wait_ge(lru_v.sem, lru_v.at("inp", jj - 1))
                        for g in range(2):
                            act.wait_ge(full.sem, full.at("ri", jj, g))
                            act.activation(lt[4 + g], B[BANK.get(("ri", jj, g), 0)][:, :], ACT.Sigmoid,
                                           bias=col(("lru_b_r", "lru_b_i")[g], jj)).then_inc(lru_a.sem, lru_a.mark("ri", jj, g))
                        act.wait_ge(lru_a.sem, lru_a.at("ri", jj, 0))
                        act.wait_ge(lru_v.sem, lru_v.at("rate"))
                        act.activation(lt[6], lt[4], ACT.Tanh, scale=small[:, 24 + jj:25 + jj])\
                           .then_inc(lru_a.sem, lru_a.mark("tanh", jj))
                        act.wait_ge(lru_a.sem, lru_a.at("tanh", jj))
                        act.activation(lt[7], lt[6], ACT.Sqrt).then_inc(lru_a.sem, lru_a.mark("sqrt", jj))
                        act.wait_ge(lru_v.sem, lru_v.at("y", jj))
                        act.activation(cut(y_hi, jj), lt[12], ACT.Copy).then_inc(lru_a.sem, lru_a.mark("hi", jj))
            gates("gb", 1)

            if on("xbc"):
                for i in range(NPAIR["xbc"]):
                    n = P0["xbc"] + i
                    q = n % 2
                    for k in range(2):
                        j = 2 * i + k
                        prep(n, q, LANDED[n + 1], k)
                        product(n, k)
                        if k == 0:
                            act.wait_ge(s_free, n)
                        act.wait_ge(xbc_v.sem, xbc_v.at("pads") if j < 4 else xbc_v.at("conv", j - 4))
                        ins = act.activation(cpad[j % 4][:, 3:3 + S], G[2 * q + k][:, :], ACT.Copy)
                        if k == 1:
                            ins.then_inc(s_free, 1)
                        else:
                            ins.then_inc(xbc_a.sem, xbc_a.mark("x", j))
                    for k in range(2):
                        j = 2 * i + k
                        act.wait_ge(xbc_v.sem, xbc_v.at("conv", j))
                        act.activation(cut(xbc, j), cacc[k], ACT.Silu).then_inc(xbc_a.sem, xbc_a.mark("silu", j))
            only_prep("dt")
            if on("dt"):
                ssd_act(act, link)
            if on("z"):
                for i in range(NPAIR["z"]):
                    n = P0["z"] + i
                    q = n % 2
                    for k in range(2):
                        prep(n, q, LANDED[n + 1], k)
                        product(n, k)
                        if k == 0:
                            act.wait_ge(s_free, n)
                        if i >= 1:
                            act.wait_ge(z_v.sem, z_v.at("gated", 2 * i - 2 + k))
                        elif k == 0:
                            act.wait_ge(ssd_v.sem, ssd_v.at("y", 3, 1))
                        ins = act.activation(tmp(2 + k), G[2 * q + k][:, :], ACT.Silu)
                        if k == 1:
                            ins.then_inc(s_free, 1)
                        else:
                            ins.then_inc(z_a.sem, z_a.mark("silu", 2 * i))
                for g in range(4):
                    for k in range(2):
                        act.wait_ge(z_v.sem, z_v.at("gated", 2 * g + k))
                        if g >= 1:
                            act.wait_ge(full.sem, full.at("zsum", g - 1))
                        act.activation(tmp(k), cut(xbc, 2 * g + k), ACT.Square).then_inc(z_a.sem, z_a.mark("square", g, k))
                    act.wait_ge(z_v.sem, z_v.at("var", g))
                    act.activation(stat[:, :], stat[:, :], ACT.Sqrt).then_inc(z_a.sem, z_a.mark("std", g))
                    for k in range(2):
                        act.wait_ge(z_v.sem, z_v.at("y", 2 * g + k))
                        act.activation(cut(y_hi, 2 * g + k), tmp(4 + k), ACT.Copy).then_inc(z_a.sem, z_a.mark("hi", 2 * g + k))
            gates("gc", 2)
            if on("wo"):
                act.wait_ge(s_free, P0["wo"])
                for j in range(KT):
                    act.activation(cut(y_hi, j), cut(merged, j), ACT.Copy).then_inc(split_a.sem, split_a.mark("merged", j))
            follow("wo", 1, "norm_mlp_g")
            for p in range(4):
                squared_relu(f"up{p}", None if p else 1)
                if p < 3:
                    only_prep(f"down{p}")
            follow("down3", 2)
            if on("f1u00"):
                root(2)

            def memory(i, k, n):
                if (i, k) == (1, 0):
                    act.wait_ge(turn_v.sem, turn_v.at("mem", 6))
                    act.activation(temps[:, 0:KT * MEM], mem_t, ACT.Square).then_inc(norm_a.sem, norm_a.mark("square", 3))
                if (i, k) == (2, 0):
                    root(3, MEM)

            def sines(i, k, n):
                if k == 1 and i < 2:
                    act.wait_ge(trig_v.sem, trig_v.at("angle", i))
                    act.activation(sincos[:, i, :], ang[2 + i], ACT.Sin).then_inc(trig_a.sem, trig_a.mark(i))
            for l in range(2):
                def ffn(f, r):
                    if not on(f"{f}u{l}0"):
                        return
                    if (f, l) == ("f1", 0):
                        for j in range(KT):
                            act.wait_ge(norm_v.sem, norm_v.at("xn", 2, j))
                            norm_tile(r, j, "ffn1_norm_2")
                    for part in range(3):
                        swiglu(f"{f}u{l}{part}", None if part else r)
                        if part < 2:
                            only_prep(f"{f}d{l}{part}", (memory, sines)[part] if (f, l) == ("f1", 0) else None)
                        elif (f, l) == ("f1", 0) or f == "f1":
                            follow(f"{f}d{l}{part}", r + 1, "mix_norm_2", 8 * l)
                        elif l == 0:
                            follow(f"{f}d{l}{part}", 9, "ffn1_norm_2", 8)
                        else:
                            follow(f"{f}d{l}{part}", 14)
                r = 4 + 5 * l
                ffn("f1", r)
                if on(f"conv{l}"):
                    for i in range(5):
                        n = P0[f"conv{l}"] + i
                        for k in range(2):
                            prep(n, n % 2, LANDED[n + 1], k)
                            if (i, k) == (0, 0):
                                root(r + 1)
                            if i == 1:
                                act.wait_ge(conv_v.sem, conv_v.at("gate", l, k))
                                act.activation(tmp(4 + k), tmp(4 + k), ACT.Sigmoid)\
                                   .then_inc(conv_a.sem, conv_a.mark("gate", l, k))
                    only_prep(f"kidx{l}")
                    evacuate(f"qidx{l}", copy_to(qi))
                    evacuate(f"q{l}", copy_to(qkv))
                    evacuate(f"k{l}", lambda i, k, bank: act.activation(cut(qkv, 4 + 2 * i + k), bank[:, :], ACT.Copy))
                    only_prep(f"vv{l}")
                if on(f"vv{l}"):
                    dsa_act(act, l)
                follow(f"mwo{l}", r + 2, "xa_norm_2", 8 * l)

                def queries(i, k, n):
                    if (i, k) == (0, 0):
                        root(r + 2)
                    if i in (1, 2):
                        for j in range(4 * i + 2 * k - 4, 4 * i + 2 * k - 2):
                            act.activation(cut(y_hi, j)[:, 0:MEM], cut(memn, j, MEM), ACT.Copy, scale=col("mem_norm_2", 8 * l + j))\
                               .then_inc(norm_a.sem, norm_a.mark("mem_hi", l, j))
                only_prep(f"xq{l}", queries)
                evacuate(f"xk{l}", copy_to(xk, MEM))
                evacuate(f"xv{l}", copy_to(xvt, MEM))
                if on(f"xv{l}"):
                    cross_act(act, l)
                follow(f"xo{l}", r + 3, "ffn2_norm_2", 8 * l)
                ffn("f2", r + 3)
            if whole:
                root(14)


        def ssd_dve(dve, link, log1p):
            n = P0["dt"]
            z, relu, e, acc, a, b = (pre[i][0:16, :] for i in (1, 4, 3, 5, 6, 7))
            link(dve.memset(stk, 0.0))
            dve.wait_ge(s_sp, 48)
            for r in range(2):
                link(dve.tensor_copy(small[64 * r:64 * r + 64, 184:192], small[64 * r:64 * r + 64, 200 + r:216:2]))
            dve.wait_ge(s_free, n)
            dve.wait_ge(s_mm, 2 * n + 2)
            dve.tensor_scalar(z, G[2 * (n % 2)][0:16, :], small[0:16, 176:177], None, ALU.add).then_inc(s_free, 1)
            dve.wait_ge(s_free, n + 1)
            dve.tensor_scalar(relu, z, 0.0, None, ALU.max).then_inc(ssd_v.sem, ssd_v.mark("z"))
            dve.wait_ge(ssd_a.sem, ssd_a.at("exp"))
            log1p(acc, e, a, b)
            link(dve.scalar_tensor_tensor(stk[0:16, :], acc, 2.0, relu, ALU.mult, ALU.add))
            link(dve.tensor_scalar(a, stk[0:16, :], small[0:16, 178:179], -1.0, ALU.mult, ALU.mult))
            for c in range(NB):
                cs = slice(c * P, (c + 1) * P)
                ins = dve.tensor_tensor_scan(acs[0:16, cs], ones[0:16, :], a[:, cs], 0.0, ALU.mult, ALU.add)
            link(ins)
            ends = acs[0:16, P - 1:S:P]
            dve.tensor_tensor(small[0:16, 32:96].rearrange("p (c h) -> p c h", c=NB),
                              ident[0:16, None, 0:16].to_broadcast([16, NB, 16]),
                              ends[:, :, None].to_broadcast([16, NB, 16]), ALU.mult).then_inc(ssd_v.sem, ssd_v.mark("ends"))
            for c in range(NB):
                ins = dve.tensor_scalar(b[:, c * P:(c + 1) * P], acs[0:16, c * P:(c + 1) * P],
                                        acs[0:16, (c + 1) * P - 1:(c + 1) * P], -1.0, ALU.subtract, ALU.mult)
            ins.then_inc(ssd_v.sem, ssd_v.mark("to_end"))
            dve.wait_ge(ssd_a.sem, ssd_a.at("sst"))

            def by_head(part, g, k):
                h0 = part + 4 * g + 2 * k
                return sst[:, :, h0:h0 + 2][:, :, :, None].to_broadcast([P, NB, 2, 64])

            for g in range(4):
                for k in range(2):
                    dve.wait_ge(full.sem, full.at("x_tok", g, k))
                    dve.tensor_tensor(xdt[:, :, k * P:(k + 1) * P].rearrange("p c (r d) -> p c r d", r=2),
                                      B[BANK.get(("x_tok", g, k), 0)][:, :].rearrange("p (c r d) -> p c r d", c=NB, r=2),
                                      by_head(0, g, k), ALU.mult).then_inc(ssd_v.sem, ssd_v.mark("xdt", g, k))
                dve.wait_ge(ssd_v.sem, ssd_v.at("xdt", g, 1))
                for k in range(2):
                    ins = dve.tensor_tensor(xdd[:, :, k * P:(k + 1) * P].rearrange("p c (r d) -> p c r d", r=2),
                                            xdt[:, :, k * P:(k + 1) * P].rearrange("p c (r d) -> p c r d", r=2),
                                            by_head(64, g, k), ALU.mult)
                ins.then_inc(ssd_v.sem, ssd_v.mark("xdd", g))
                dve.wait_ge(full.sem, full.at("cb", g))
                dve.tensor_tensor(cb[:, :, :], B[BANK.get(("cb", g), 0)][:, :].rearrange("p (c l) -> p c l", c=NB),
                                  causal[:, None, :].to_broadcast([P, NB, P]), ALU.mult)\
                   .then_inc(ssd_v.sem, ssd_v.mark("cb", g))
                dve.wait_ge(ssd_a.sem, ssd_a.at("ends"))
                dve.wait_ge(full.sem, full.at("st", g, 0))
                b0 = B[BANK.get(("st", g, 0), 0)]
                link(dve.tensor_copy(st[:, 0, :], b0[:, 0:256]))
                decay = lambda c: chunk_decay[:, c, 4 * g:4 * g + 4][:, :, None].to_broadcast([P, 4, 64])
                heads = lambda x: x.rearrange("p (r d) -> p r d", r=4)
                link(dve.tensor_tensor(heads(st[:, 1, :]), heads(st[:, 0, :]), decay(1), ALU.mult))
                dve.tensor_tensor(st[:, 1, :], st[:, 1, :], b0[:, 256:512], ALU.add).then_inc(ssd_v.sem, ssd_v.mark("st", g, 0))
                dve.wait_ge(ssd_v.sem, ssd_v.at("st", g, 0))
                link(dve.tensor_tensor(heads(st[:, 2, :]), heads(st[:, 1, :]), decay(2), ALU.mult))
                dve.wait_ge(full.sem, full.at("st", g, 1))
                dve.tensor_tensor(st[:, 2, :], st[:, 2, :], B[BANK.get(("st", g, 1), 0)][:, 0:256], ALU.add)\
                   .then_inc(ssd_v.sem, ssd_v.mark("st", g, 1))
                for r in range(4):
                    hh = 4 * g + r
                    dve.wait_ge(ssd_a.sem, ssd_a.at("row", g, r))
                    if (g, r) != (0, 0):
                        dve.wait_ge(ssd_v.sem, ssd_v.at("m", *((g, r - 1) if r else (g - 1, 3))))
                    dve.tensor_tensor(pre[9].rearrange("p (c l) -> p c l", c=NB),
                                      B[BANK.get(("row", g, r), 0)][:, :].rearrange("p (c l) -> p c l", c=NB),
                                      sst[:, :, 32 + hh:33 + hh].to_broadcast([P, NB, P]), ALU.subtract)\
                       .then_inc(ssd_v.sem, ssd_v.mark("seg", g, r))
                    dve.wait_ge(ssd_v.sem, ssd_v.at("seg", g, r))
                    dve.tensor_scalar(pre[9], pre[9], 0.0, None, ALU.min).then_inc(ssd_v.sem, ssd_v.mark("min", g, r))
                    if (g, r) != (0, 0):
                        dve.wait_ge(full.sem, full.at("y", *((g, r - 1) if r else (g - 1, 3))))
                    dve.tensor_tensor(tmp(0), cut(xbc, 12 + g), pre[8], ALU.mult).then_inc(ssd_v.sem, ssd_v.mark("ce", g, r))
                    if r == 2:
                        skip(dve, g, 0)
                    dve.wait_ge(ssd_a.sem, ssd_a.at("decay", g, r))
                    dve.tensor_tensor(pre[10], pre[9], cb[:, :, :].rearrange("p c l -> p (c l)"), ALU.mult)\
                       .then_inc(ssd_v.sem, ssd_v.mark("m", g, r))
                skip(dve, g, 1)

        def skip(dve, g, k):
            dve.wait_ge(full.sem, full.at("y", g, 2 * k + 1))
            x = cut(xbc, 2 * g + k)
            dve.scalar_tensor_tensor(x, x, small[:, 184 + 2 * g + k:185 + 2 * g + k], B[BANK.get(("y", g, k), 0)][:, :],
                                     ALU.mult, ALU.add).then_inc(ssd_v.sem, ssd_v.mark("y", g, k))

        def rope(dve, link, l, key, at_):
            x = rope_tile(key)
            dve.wait_ge(full.sem, full.at("rot", l, *key))
            dve.tensor_tensor(tmp(at_ % 2), B[BANK.get(("rot", l) + key, 0)][:, :], sincos_r[:, 1, :], ALU.mult)\
               .then_inc(rope_v.sem, rope_v.mark("rot", l, *key))
            link(dve.tensor_tensor(x, x, sincos_r[:, 0, :], ALU.mult))
            dve.tensor_tensor(x, x, tmp(at_ % 2), ALU.add).then_inc(rope_v.sem, rope_v.mark("tile", l, *key))
            dve.wait_ge(rope_v.sem, rope_v.at("tile", l, *key))

        def dsa_dve(dve, link, l, lo_of):
            dve.wait_ge(full.sem, full.at("w_tok", l))
            dve.tensor_copy(w_tok[:, :, :], B[BANK.get(("w_tok", l), 0)][:, :].rearrange("p (t h) -> p t h", t=NB)[:, :, 0:4])\
               .then_inc(rope_v.sem, rope_v.mark("w_tok", l))
            for t in range(4):
                dve.wait_ge(full.sem, full.at("v_key", l, t))
                dve.tensor_copy(v_key[:, :, t * P:(t + 1) * P], B[BANK.get(("v_key", l, t), 0)][:, :].rearrange("p (b f) -> p b f", b=NB))\
                   .then_inc(rope_v.sem, rope_v.mark("v_key", l, t))

            def mean():
                dve.wait_ge(full.sem, full.at("cln", l, 0))
                dve.tensor_scalar(stat[:, :], B[BANK.get(("cln", l, 0), 0)][:, :], 1.0 / 256, None, ALU.mult)\
                   .then_inc(conv_v.sem, conv_v.mark("stat", l, 0))
                dve.wait_ge(conv_v.sem, conv_v.at("stat", l, 0))
                for k in range(2):
                    link(dve.tensor_tensor(cv[k], cv[k], stat[:, :], ALU.subtract))
                    dve.tensor_tensor(tmp(2 + k), cv[k], cv[k], ALU.mult).then_inc(conv_v.sem, conv_v.mark("summand", l, 1, k))
                for k in range(2):
                    dve.wait_ge(conv_a.sem, conv_a.at("hi", l, 2 + k))
                    lo_of(cut(y_lo, 2 + k), tmp(4 + k), cut(y_hi, 2 + k)).then_inc(conv_v.sem, conv_v.mark("short_lo", l, k))

            def maximum(s):
                b, hh = steps[s]
                w = (b + 1) * P
                m = small[:, 144 + s % 2:145 + s % 2]
                dve.wait_ge(full.sem, full.at("s", l, s))
                if s >= 2:
                    dve.wait_ge(full.sem, full.at("p", l, s - 2))
                dve.tensor_tensor_reduce(att_p(s)[:, 0:w], B[BANK.get(("s", l, s), 0)][:, 0:w],
                                         (bias[b % 2] if b else qcausal)[:, 0:w],
                                         0.125, -3.0e38, ALU.add, ALU.max, m).then_inc(dsa_v.sem, dsa_v.mark("s", l, s))
                dve.wait_ge(dsa_v.sem, dsa_v.at("s", l, s))
                dve.tensor_scalar(small[:, 146 + s % 2:147 + s % 2], m, -1.0, None, ALU.mult)\
                   .then_inc(dsa_v.sem, dsa_v.mark("neg", l, s))

            def index_scores(b):
                w = (b + 1) * P
                for i in range(IDXH):
                    dve.wait_ge(dsa_a.sem, dsa_a.at("idx", l, b, i))
                    if i == 0:
                        ins = dve.tensor_scalar(score[:, 0:w], tmp(0, w), w_tok[:, b, 0:1], None, ALU.mult)
                    else:
                        ins = dve.scalar_tensor_tensor(score[:, 0:w], tmp(i % 2, w), w_tok[:, b, i:i + 1], score[:, 0:w],
                                                       ALU.mult, ALU.add)
                    ins.then_inc(dsa_v.sem, dsa_v.mark("idx", l, b, i))
                    dve.wait_ge(dsa_v.sem, dsa_v.at("idx", l, b, i))

            def select(b, rounds):
                w = (b + 1) * P
                for n in rounds:
                    if n == 0:
                        dve.wait_ge(dsa_p.sem, dsa_p.at(l, b))
                    src = work if n else score
                    link(dve.max(small[:, 160:168], src[:, 0:w]))
                    link(dve.match_replace(work[:, 0:w], small[:, 160:168], src[:, 0:w], TAKEN))
                    if n == TOPK // 8 - 1:
                        link(dve.tensor_scalar(bias[b % 2][:, 0:w], work[:, 0:w], TAKEN, NEG, ALU.is_gt, ALU.mult))

            for i in range(-2, len(steps)):
                if i + 2 < len(steps):
                    maximum(i + 2)
                if i >= 1 and i % 2 == 0:
                    gather(dve, l, i - 2)
                if i >= 0 and steps[i][0] + 1 < NB:
                    b, hh = steps[i]
                    if hh == 0:
                        index_scores(b + 1)
                    select(b + 1, topk_rounds(hh))
                if i + 2 < len(steps):
                    s = i + 2
                    dve.wait_ge(dsa_a.sem, dsa_a.at("exp", l, s))
                    dve.reciprocal(small[:, 150 + s % 2:151 + s % 2], small[:, 148 + s % 2:149 + s % 2])\
                       .then_inc(dsa_v.sem, dsa_v.mark("inverse", l, s))
                if i == mean_step + 1:
                    mean()
                if i == square_step + 1:
                    dve.wait_ge(full.sem, full.at("cln", l, 1))
                    dve.tensor_scalar(stat[:, :], B[BANK.get(("cln", l, 1), 0)][:, :], 1.0 / 256, LN_EPS_2, ALU.mult, ALU.add)\
                       .then_inc(conv_v.sem, conv_v.mark("stat", l, 1))
                if i == root_step:
                    dve.wait_ge(conv_a.sem, conv_a.at("std", l))
                    link(dve.reciprocal(rstd[:, :], stat[:, :]))
                    for k in range(2):
                        dve.tensor_tensor(cv[k], cv[k], rstd[:, :], ALU.mult).then_inc(conv_v.sem, conv_v.mark("ln", l, k))
                if i == root_step + 2:
                    for k in range(2):
                        dve.wait_ge(conv_a.sem, conv_a.at("hi", l, k))
                        lo_of(cut(y_lo, k), cv[k], cut(y_hi, k)).then_inc(conv_v.sem, conv_v.mark("lo", l, k))
            gather(dve, l, len(steps) - 2)
            for t in range(4):
                dve.wait_ge(split_a.sem, split_a.at("dsa", l, t))
                lo_of(cut(y_lo, 4 + t), cut(o_t, t), cut(y_hi, 4 + t)).then_inc(split_v.sem, split_v.mark("dsa", l, t))

        def gather(dve, l, s):
            b, hh = steps[s]
            dve.wait_ge(full.sem, full.at("o", l, b, hh + 1))
            dve.tensor_copy(cut(o_t, hh // 2)[:, b * P:(b + 1) * P], B[BANK.get(("o", l, b, hh // 2), 0)][:, 0:P])\
               .then_inc(dsa_v.sem, dsa_v.mark("o", l, b, hh // 2))

        def cross_dve(dve, link, l, lo_of):
            for j in range(0, KT, 2):
                dve.wait_ge(full.sem, full.at("xv", l, j))
                dve.tensor_copy(xv[:, :, j * P:(j + 2) * P].rearrange("p t (d f) -> p d t f", d=2),
                                B[BANK.get(("xv", l, j), 0)][:, :].rearrange("p (d t f) -> p d t f", d=2, t=2))\
                   .then_inc(xa_v.sem, xa_v.mark("xv", l, j))

            def maximum(x, b):
                m = small[:, 168 + b % 2:169 + b % 2]
                dve.wait_ge(full.sem, full.at("xs", l, x, b))
                link(dve.tensor_reduce(m, B[BANK.get(("xs", l, x, b), 0)][:, 0:MEM], AX.X, ALU.max))
                dve.tensor_scalar(small[:, 152 + b % 2:153 + b % 2], m, -1.0 / 16.0, None, ALU.mult)\
                   .then_inc(xa_v.sem, xa_v.mark("neg", l, x, b))

            steps = [(x, b) for x in range(4) for b in range(NB)]
            maximum(*steps[0])
            for n, (x, b) in enumerate(steps):
                if n + 1 < len(steps):
                    maximum(*steps[n + 1])
                dve.wait_ge(xa_a.sem, xa_a.at("p", l, x, b))
                link(dve.reciprocal(small[:, 156 + b % 2:157 + b % 2], small[:, 154 + b % 2:155 + b % 2]))
                dve.tensor_scalar(xp[b % 2], xp[b % 2], small[:, 156 + b % 2:157 + b % 2], None, ALU.mult)\
                   .then_inc(xa_v.sem, xa_v.mark("p", l, x, b))
                if b == NB - 1:
                    for d in range(2):
                        dve.wait_ge(xa_a.sem, xa_a.at("hi", l, 2 * x + d))
                        lo_of(cut(y_lo, 2 * x + d), B[BANK.get(("xo", l, x, d), 0)][:, :], cut(y_hi, 2 * x + d))\
                            .then_inc(xa_v.sem, xa_v.mark("lo", l, 2 * x + d))

        @block.vector
        def _(dve):
            count = {"n": 0, "more": 0}

            def link(ins):
                count["n"] += 1
                ins.then_inc(s_dve, 1)
                dve.wait_ge(s_dve, count["more"] + count["n"])

            def chained(name, body, per_pair, unroll, peel=0, extra=0):
                base = count["n"]

                def wrapped(i, n, q, landed):
                    first = isinstance(i, int) and i == 0
                    count["n"] = 0
                    count["more"] = i * per_pair + (base if first else base + extra)
                    body(i, n, q, landed)
                    assert count["n"] == per_pair + (extra if first else 0)
                if on(name):
                    loop_pairs(dve, name, wrapped, unroll=unroll or name == names[-1], peel=peel)
                    count["n"], count["more"] = base + per_pair * NPAIR[name] + extra, 0

            def prep_lo(n, q, k):
                if isinstance(n, int) and n + 1 > last_pair:
                    return
                dve.wait_ge(s_whi, 2 * n + (k + 3))
                dve.tensor_tensor(w_lo[:, k], raw[:, 1 - q, :, k * P:(k + 1) * P], w_hi[:, k].bitcast(F32), ALU.subtract)\
                   .then_inc(s_wlo, 1)

            def only_prep(name, extra=None):
                def body(i, n, q, landed):
                    for k in range(2):
                        prep_lo(n, q, k)
                        if extra:
                            extra(2 * i + k)
                if on(name):
                    loop_pairs(dve, name, body, unroll=name == names[-1] or P0[name] < 2)

            def product(n, k):
                dve.wait_ge(s_mm, 2 * n + (k + 1))

            def lo_of(dst, value, hi):
                return dve.tensor_tensor(dst, value, hi.bitcast(F32), ALU.subtract)

            def residual(name, scale=1.0, more=None):
                def body(i, n, q, landed):
                    for k in range(2):
                        prep_lo(n, q, k)
                        if k == 0:
                            dve.wait_ge(s_free, n)
                        product(n, k)
                        ins = dve.scalar_tensor_tensor(cut(h, 2 * i + k), G[2 * q + k][:, :], scale, cut(h, 2 * i + k),
                                                       ALU.mult, ALU.add)
                        if k == 1:
                            ins.then_inc(s_free, 1)
                        if more:
                            more(i, k)
                if on(name):
                    loop_pairs(dve, name, body, unroll=bool(more) or name == names[-1])

            def gates(name, n_):
                def body(i, n, q, landed):
                    prep_lo(n, q, 0)
                    prep_lo(n, q, 1)
                    dve.wait_ge(s_free, n)
                    product(n, 1)
                    dve.wait_ge(s_ao, i + (BASE[name][0] + 1))
                    if n_ == 0:
                        dve.tensor_tensor(cut(merged, i), G[2 * q + 1][:, :], tmp(q), ALU.mult).then_inc(s_free, 1)
                    else:
                        link(dve.tensor_tensor(tmp(4 + q), G[2 * q + 1][:, :], tmp(q), ALU.mult))
                        dve.tensor_tensor(cut(merged, i), cut(merged, i), tmp(4 + q), ALU.add).then_inc(s_free, 1)
                chained(name, body, 0 if n_ == 0 else 1, False)

            def follow(name, scale, r, gain=None, g0=0):
                def body(i, n, q, landed):
                    for k in range(2):
                        prep_lo(n, q, k)
                        if k == 0:
                            dve.wait_ge(s_free, n)
                        product(n, k)
                        j = 2 * i + k
                        ins = dve.scalar_tensor_tensor(cut(h, j), G[2 * q + k][:, :], scale, cut(h, j), ALU.mult, ALU.add)
                        if k == 1:
                            ins.then_inc(s_free, 1)
                        else:
                            ins.then_inc(norm_v.sem, norm_v.mark("h", r, j))
                        if j:
                            norm_tile(r, j - 1, gain, g0)
                    if i == 3:
                        dve.wait_ge(s_free, n + 1)
                        norm_tile(r, KT - 1, gain, g0)
                if on(name):
                    loop_pairs(dve, name, body, unroll=True)

            def norm_tile(r, j, gain=None, g0=0):
                if gain:
                    dve.wait_ge(norm_a.sem, norm_a.at("hi", r, j))
                    dve.scalar_tensor_tensor(cut(xn_lo, j), cut(h, j), col(gain, g0 + j), cut(xn_hi, j).bitcast(F32),
                                             ALU.mult, ALU.subtract).then_inc(norm_v.sem, norm_v.mark("lo", r, j))
                if j:
                    if j > 1:
                        dve.wait_ge(norm_v.sem, norm_v.at("summed", r, j - 1))
                    dve.wait_ge(norm_a.sem, norm_a.at("square", r, j))
                    dve.tensor_tensor(stat[:, :], stat[:, :], tmp(j % 2), ALU.add)\
                       .then_inc(norm_v.sem, norm_v.mark("summed", r, j))

            def norm_var(r, n=S):
                dve.wait_ge(full.sem, full.at("norm", r))
                dve.tensor_scalar(stat[:, 0:n], B[BANK.get(("norm", r), 0)][:, 0:n], 1.0 / D, EPS, ALU.mult, ALU.add)\
                   .then_inc(norm_v.sem, norm_v.mark("var", r))

            def norm_rstd(r, n=S, dst=rstd):
                dve.wait_ge(norm_a.sem, norm_a.at("std", r))
                link(dve.reciprocal(dst[:, 0:n], stat[:, 0:n]))

            def squared_relu(name, r=None):
                def body(i, n, q, landed):
                    first = r is not None and isinstance(i, int) and i == 0
                    if first:
                        norm_var(r)
                    prep_lo(n, q, 0)
                    if first:
                        norm_rstd(r)
                    prep_lo(n, q, 1)
                    dve.wait_ge(s_free, n)
                    dve.wait_ge(s_wlo, 2 * n + 3)
                    for k in range(2):
                        product(n, k)
                        dve.scalar_tensor_tensor(tmp(2 * q + k), G[2 * q + k][:, :], 0.0, rstd[:, :], ALU.max, ALU.mult)\
                           .then_inc(s_free if k else s_ao, 1)
                    for k in range(2):
                        if k == 0:
                            dve.wait_ge(s_ao, i + (BASE[name][0] + 1))
                        else:
                            dve.wait_ge(s_free, n + 1)
                        ins = dve.tensor_tensor(tmp(4 + k), tmp(2 * q + k), tmp(2 * q + k), ALU.mult)
                    squares(ins)
                    for k in range(2):
                        dve.wait_ge(s_yh, 2 * i + (BASE[name][1] + k + 1))
                        lo_of(cut(y_lo, 2 * i + k), tmp(4 + k), cut(y_hi, 2 * i + k)).then_inc(s_yl, 1)

                def squares(ins):
                    link(ins)
                chained(name, body, 1, False, peel=0 if r is None else 2, extra=0 if r is None else 1)

            def swiglu(name, r=None):
                def body(i, n, q, landed):
                    first = r is not None and isinstance(i, int) and i == 0
                    if first:
                        norm_var(r)
                    prep_lo(n, q, 0)
                    if first:
                        norm_rstd(r)
                    dve.wait_ge(s_free, n)
                    product(n, 0)
                    dve.wait_ge(s_wlo, 2 * n + 3)
                    dve.tensor_tensor(tmp(q), G[2 * q][:, :], rstd[:, :], ALU.mult).then_inc(s_ao, 1)
                    prep_lo(n, q, 1)
                    product(n, 1)
                    dve.tensor_tensor(tmp(4 + q), G[2 * q + 1][:, :], rstd[:, :], ALU.mult).then_inc(s_free, 1)
                    dve.wait_ge(s_free, n + 1)
                    dve.wait_ge(s_yh, 2 * i + (BASE[name][1] + 1))
                    dve.tensor_tensor(tmp(2 + q), tmp(4 + q), tmp(q), ALU.mult).then_inc(s_ao, 1)
                    dve.wait_ge(s_ao, 2 * i + (BASE[name][0] + 2))
                    dve.wait_ge(s_yh, 2 * i + (BASE[name][1] + 2))
                    lo_of(cut(y_lo, i), tmp(2 + q), cut(y_hi, i)).then_inc(s_yl, 1)
                if on(name):
                    loop_pairs(dve, name, body, unroll=name == names[-1], peel=0 if r is None else 2)

            def scaled(name, dst, r=None):
                def body(i, n, q, landed):
                    first = r is not None and isinstance(i, int) and i == 0
                    if first:
                        norm_var(r)
                    prep_lo(n, q, 0)
                    if first:
                        norm_rstd(r)
                    prep_lo(n, q, 1)
                    dve.wait_ge(s_free, n)
                    for k in range(2):
                        product(n, k)
                        ins = dve.tensor_tensor(cut(dst, 2 * i + k), G[2 * q + k][:, :], rstd[:, :], ALU.mult)
                    ins.then_inc(s_free, 1)
                    if (name[:2], i) in (("xq", 1), ("xq", 2)):
                        for j in range(4 * i - 4, 4 * i):
                            dve.wait_ge(norm_a.sem, norm_a.at("mem_hi", int(name[2]), j))
                            dve.scalar_tensor_tensor(cut(y_lo, j)[:, 0:MEM], cut(memn, j, MEM), col("mem_norm_2", 8 * int(name[2]) + j),
                                                     cut(y_hi, j)[:, 0:MEM].bitcast(F32), ALU.mult, ALU.subtract)\
                               .then_inc(norm_v.sem, norm_v.mark("mem_lo", int(name[2]), j))
                if on(name):
                    loop_pairs(dve, name, body, unroll=name[:2] == "xq" or name == names[-1])

            def scale_by(r, scale, src_bank, eps, sig, var_key, std_sig, std_key, n=S):
                dve.tensor_scalar(stat[:, 0:n], src_bank[:, 0:n], scale, eps, ALU.mult, ALU.add)\
                   .then_inc(sig.sem, sig.mark(*var_key))
                dve.wait_ge(std_sig.sem, std_sig.at(*std_key))
                link(dve.reciprocal(rstd[:, 0:n], stat[:, 0:n]))

            def norm_dve(r, gain, g0=0):
                norm_var(r)
                norm_rstd(r)
                for j in range(KT + 1):
                    if 2 <= j < KT:
                        dve.wait_ge(norm_v.sem, norm_v.at("lo", r, j - 2))
                    if j < KT:
                        dve.scalar_tensor_tensor(tmp(2 + j % 2), cut(h, j), col(gain, g0 + j), rstd[:, :], ALU.mult, ALU.mult)\
                           .then_inc(norm_v.sem, norm_v.mark("xn", r, j))
                    if j >= 1:
                        dve.wait_ge(norm_a.sem, norm_a.at("hi", r, j - 1))
                        lo_of(cut(xn_lo, j - 1), tmp(2 + (j - 1) % 2), cut(xn_hi, j - 1))\
                            .then_inc(norm_v.sem, norm_v.mark("lo", r, j - 1))

            def norm_in_place(r, gain, then=None):
                norm_var(r)
                norm_rstd(r)
                for j in range(KT + 1):
                    if j < KT:
                        dve.scalar_tensor_tensor(cut(h, j), cut(h, j), col(gain, j), rstd[:, :], ALU.mult, ALU.mult)\
                           .then_inc(norm_v.sem, norm_v.mark("xn", r, j))
                    if then and j:
                        dve.wait_ge(norm_v.sem, norm_v.at("xn", r, j - 1))
                        then(j - 1)

            def log1p(dst, e, a, b):
                link(dve.tensor_scalar(a, e, 2.0, None, ALU.add))
                link(dve.reciprocal(b, a))
                link(dve.tensor_tensor(a, e, b, ALU.mult))
                link(dve.tensor_tensor(b, a, a, ALU.mult))
                link(dve.tensor_scalar(dst, b, 1.0 / 17, None, ALU.mult))
                for d in range(15, 1, -2):
                    link(dve.scalar_tensor_tensor(dst, dst, 1.0 / d, b, ALU.add, ALU.mult))
                link(dve.scalar_tensor_tensor(dst, dst, 1.0, a, ALU.add, ALU.mult))

            for k in range(2):
                dve.wait_ge(s_whi, k + 1)
                dve.tensor_tensor(w_lo[:, k], raw[:, 0, :, k * P:(k + 1) * P], w_hi[:, k].bitcast(F32), ALU.subtract)\
                   .then_inc(s_wlo, 1)
            for b in range(4):
                n = sum(c for _, c in BATCHES[b])
                dve.wait_ge(full.sem, full.at("par", b))
                dve.tensor_copy(par[:, b * P:b * P + n], B[BANK.get(("par", b), 0)][:, 0:n])\
                   .then_inc(turn_v.sem, turn_v.mark("par", b))
            for j in range(KT):
                dve.wait_ge(full.sem, full.at("x", j))
                dve.tensor_copy(cut(h, j), B[BANK.get(("x", j), 0)][:, :]).then_inc(turn_v.sem, turn_v.mark("x", j))
                if j:
                    norm_tile(0, j - 1)
            dve.wait_ge(turn_v.sem, turn_v.at("x", KT - 1))
            norm_tile(0, KT - 1)
            norm_dve(0, "norm_mix_g")

            only_prep("u")
            only_prep("v")
            if on("v"):
                for g in range(0, 8, 4):
                    dve.wait_ge(full.sem, full.at("w_sp", g))
                    dve.tensor_tensor(w_spT[:, g:g + 4, :], B[BANK.get(("w_sp", g), 0)][:, :].rearrange("p (g t) -> p g t", g=4),
                                      causal[:, None, :].to_broadcast([P, 4, P]), ALU.mult)\
                       .then_inc(gmlp_v.sem, gmlp_v.mark("w_sp", g))
                dve.wait_ge(gmlp_a.sem, gmlp_a.at("v", 7))
                dve.wait_ge(s_gb, 48)
                for t in range(NB):
                    s0 = 32 + 16 * t
                    for o in range(2):
                        ins = dve.bn_stats(small[:, s0 + 6 * o:s0 + 6 * o + 6], v_tok[:, t, o * S:(o + 1) * S])
                    link(ins)
                    link(dve.bn_aggr(small[:, s0 + 12:s0 + 14], small[:, s0:s0 + 12]))
                    link(dve.tensor_scalar(small[:, t:t + 1], small[:, s0 + 13:s0 + 14], EPS, None, ALU.add))
                link_mark = dve.tensor_scalar(small[:, 4:5], small[:, 0:1], 0.0, None, ALU.add)
                link_mark.then_inc(gmlp_v.sem, gmlp_v.mark("var"))
                dve.wait_ge(gmlp_a.sem, gmlp_a.at("std"))
                link(dve.reciprocal(small[:, 4:8], small[:, 0:4]))
                for t in range(NB):
                    link(dve.scalar_tensor_tensor(v_tok[:, t, :], v_tok[:, t, :], small[:, 44 + 16 * t:45 + 16 * t], g_bc,
                                                  ALU.subtract, ALU.mult))
                    dve.scalar_tensor_tensor(v_tok[:, t, :], v_tok[:, t, :], small[:, 4 + t:5 + t], b_bc, ALU.mult, ALU.add)\
                       .then_inc(gmlp_v.sem, gmlp_v.mark("normed", t))
                for g in range(9):
                    if 2 <= g < 8:
                        dve.wait_ge(gmlp_v.sem, gmlp_v.at("lo", g - 2))
                    if g < 8:
                        dve.wait_ge(full.sem, full.at("mix", g))
                        dve.tensor_tensor(tmp(g % 2).rearrange("p (c t) -> p c t", c=NB),
                                          B[BANK.get(("mix", g), 0)][:, :].rearrange("p (c t) -> p c t", c=NB),
                                          bs_bc[:, None, g * P:(g + 1) * P].to_broadcast([P, NB, P]), ALU.add)\
                           .then_inc(gmlp_v.sem, gmlp_v.mark("mixed", g))
                        dve.wait_ge(gmlp_v.sem, gmlp_v.at("mixed", g))
                        dve.tensor_tensor(tmp(4 + g % 2), tmp(g % 2), cut(u, g), ALU.mult)\
                           .then_inc(gmlp_v.sem, gmlp_v.mark("y", g))
                    if g >= 1:
                        dve.wait_ge(gmlp_a.sem, gmlp_a.at("hi", g - 1))
                        lo_of(cut(y_lo, g - 1), tmp(4 + (g - 1) % 2), cut(y_hi, g - 1))\
                            .then_inc(gmlp_v.sem, gmlp_v.mark("lo", g - 1))
            gates("ga", 0)

            if on("lru"):
                dve.wait_ge(lru_a.sem, lru_a.at("exp"))
                lam = par[:, COL["lru_lambda"]:COL["lru_lambda"] + 8]
                log1p(small[:, 40:48], small[:, 16:24], small[:, 48:56], small[:, 56:64])
                link(dve.tensor_scalar(small[:, 32:40], lam, -1.0, 0.0, ALU.mult, ALU.max))
                link(dve.scalar_tensor_tensor(small[:, 24:32], small[:, 40:48], 2.0, small[:, 32:40], ALU.mult, ALU.add))
                dve.tensor_scalar(small[:, 24:32], small[:, 24:32], 4.0, None, ALU.mult).then_inc(lru_v.sem, lru_v.mark("rate"))
                for q in range(2):
                    ins = dve.memset(xpad[q][:, 0:3], 0.0)
                ins.then_inc(lru_v.sem, lru_v.mark("pads"))
                for j in range(9):
                    if j < 8:
                        n = P0["lru"] + j
                        q = n % 2
                        prep_lo(n, q, 0)
                        prep_lo(n, q, 1)
                        dve.wait_ge(lru_a.sem, lru_a.at("x", j))
                        x = xpad[q]
                        if j >= 2:
                            dve.wait_ge(full.sem, full.at("ri", j - 2, 1))
                        link(dve.tensor_scalar(lt[j % 2], x[:, 0:S], col("lru_conv_w", j), col("lru_conv_b", j),
                                               ALU.mult, ALU.add))
                        for k in range(1, 4):
                            ins = dve.scalar_tensor_tensor(lt[j % 2], x[:, k:k + S], col("lru_conv_w", 8 * k + j), lt[j % 2],
                                                           ALU.mult, ALU.add)
                            if k < 3:
                                link(ins)
                        ins.then_inc(lru_v.sem, lru_v.mark("conv", j))
                    if j >= 1:
                        jj = j - 1
                        dve.wait_ge(lru_a.sem, lru_a.at("tanh", jj))
                        link(dve.tensor_scalar(lt[8], lt[6], 1.0, None, ALU.add))
                        dve.reciprocal(lt[9], lt[8])
                        link(dve.tensor_scalar(lt[10], lt[6], -1.0, 1.0, ALU.mult, ALU.add))
                        dve.tensor_tensor(lt[10], lt[10], lt[9], ALU.mult)
                        link(dve.tensor_tensor(lt[8], lt[5], lt[jj % 2], ALU.mult))
                        link(dve.scalar_tensor_tensor(lt[8], lt[8], 2.0, lt[9], ALU.mult, ALU.mult))
                        dve.wait_ge(lru_a.sem, lru_a.at("sqrt", jj))
                        dve.tensor_tensor(lt[11], lt[8], lt[7], ALU.mult).then_inc(lru_v.sem, lru_v.mark("inp", jj))
                        dve.wait_ge(lru_v.sem, lru_v.at("inp", jj))
                        link(dve.tensor_tensor_scan(lt[13], lt[10], lt[11], 0.0, ALU.mult, ALU.add))
                        dve.wait_ge(s_free, P0["lru"] + jj + 1)
                        dve.tensor_tensor(lt[12], lt[13], lt[2 + jj % 2], ALU.mult).then_inc(lru_v.sem, lru_v.mark("y", jj))
                        dve.wait_ge(lru_a.sem, lru_a.at("hi", jj))
                        lo_of(cut(y_lo, jj), lt[12], cut(y_hi, jj)).then_inc(lru_v.sem, lru_v.mark("lo", jj))
            gates("gb", 1)

            if on("xbc"):
                for i in range(4):
                    ins = dve.memset(cpad[i][:, 0:3], 0.0)
                ins.then_inc(xbc_v.sem, xbc_v.mark("pads"))
                for i in range(NPAIR["xbc"]):
                    n = P0["xbc"] + i
                    q = n % 2
                    prep_lo(n, q, 0)
                    prep_lo(n, q, 1)
                    for k in range(2):
                        j = 2 * i + k
                        if k == 0:
                            dve.wait_ge(xbc_a.sem, xbc_a.at("x", j))
                        else:
                            dve.wait_ge(s_free, n + 1)
                        if i >= 1:
                            dve.wait_ge(xbc_a.sem, xbc_a.at("silu", j - 2))
                        link(dve.tensor_scalar(cacc[k], cpad[j % 4][:, 0:S], col("ssd_conv_w", j), col("ssd_conv_b", j),
                                               ALU.mult, ALU.add))
                        for w in range(1, 4):
                            ins = dve.scalar_tensor_tensor(cacc[k], cpad[j % 4][:, w:w + S], col("ssd_conv_w", 16 * w + j),
                                                           cacc[k], ALU.mult, ALU.add)
                            if w < 3:
                                link(ins)
                        ins.then_inc(xbc_v.sem, xbc_v.mark("conv", j))
            only_prep("dt")
            if on("dt"):
                ssd_dve(dve, link, log1p)
            if on("z"):
                for i in range(NPAIR["z"]):
                    n = P0["z"] + i
                    q = n % 2
                    for k in range(2):
                        prep_lo(n, q, k)
                    for k in range(2):
                        if k == 0:
                            dve.wait_ge(z_a.sem, z_a.at("silu", 2 * i))
                        else:
                            dve.wait_ge(s_free, n + 1)
                        dve.tensor_tensor(cut(xbc, 2 * i + k), cut(xbc, 2 * i + k), tmp(2 + k), ALU.mult)\
                           .then_inc(z_v.sem, z_v.mark("gated", 2 * i + k))
                for g in range(4):
                    dve.wait_ge(full.sem, full.at("zsum", g))
                    scale_by(0, 1.0 / 256, B[BANK.get(("zsum", g), 0)], EPS, z_v, ("var", g), z_a, ("std", g))
                    for k in range(2):
                        j = 2 * g + k
                        dve.scalar_tensor_tensor(tmp(4 + k), cut(xbc, j), col("ssd_norm_g", j), rstd[:, :], ALU.mult, ALU.mult)\
                           .then_inc(z_v.sem, z_v.mark("y", j))
                    for k in range(2):
                        j = 2 * g + k
                        dve.wait_ge(z_a.sem, z_a.at("hi", j))
                        lo_of(cut(y_lo, j), tmp(4 + k), cut(y_hi, j)).then_inc(z_v.sem, z_v.mark("lo", j))
            gates("gc", 2)
            if on("wo"):
                for j in range(KT):
                    dve.wait_ge(split_a.sem, split_a.at("merged", j))
                    lo_of(cut(y_lo, j), cut(merged, j), cut(y_hi, j)).then_inc(split_v.sem, split_v.mark("merged", j))
            follow("wo", 1.0, 1, "norm_mlp_g")
            for p in range(4):
                squared_relu(f"up{p}", None if p else 1)
                if p < 3:
                    residual(f"down{p}")
            follow("down3", 1.0, 2)

            if on("f1u00"):
                norm_in_place(2, "final_norm_g", lambda j: norm_tile(4, j, "ffn1_norm_2"))

            def memory(i, k):
                if (i, k) == (0, 1):
                    for j in range(0, KT, 2):
                        dve.wait_ge(full.sem, full.at("mem", j))
                        dve.tensor_copy(mem_t[:, j * MEM:(j + 2) * MEM], B[BANK.get(("mem", j), 0)][:, :])\
                           .then_inc(turn_v.sem, turn_v.mark("mem", j))
                if (i, k) == (1, 1):
                    dve.wait_ge(turn_v.sem, turn_v.at("mem", 6))
                    dve.wait_ge(norm_a.sem, norm_a.at("square", 3))
                    for half in (4 * MEM, 2 * MEM):
                        link(dve.tensor_tensor(temps[:, 0:half], temps[:, 0:half], temps[:, half:2 * half], ALU.add))
                    dve.tensor_tensor(stat[:, 0:MEM], temps[:, 0:MEM], temps[:, MEM:2 * MEM], ALU.add)\
                       .then_inc(norm_v.sem, norm_v.mark("summed", 3, KT - 1))
                if (i, k) == (2, 0):
                    norm_var(3, MEM)
                if (i, k) == (2, 1):
                    norm_rstd(3, MEM, mem_rstd)
                    link(dve.tensor_tensor(memn.rearrange("p (j m) -> p j m", j=KT), mem_t.rearrange("p (j m) -> p j m", j=KT),
                                           mem_rstd[:, None, :].to_broadcast([P, KT, MEM]), ALU.mult))

            def angles(i, k):
                if (i, k) == (0, 0):
                    dve.wait_ge(s_pos, 16)
                    link(dve.tensor_copy(ang[0], ang[4].bitcast(I32)))
                    link(dve.tensor_scalar(ang[1], ang[0], inv_freq, None, ALU.mult))
                if k == 1 and i < 2:
                    c = i
                    link(dve.tensor_scalar(ang[0], ang[1], 1.0 / (2 * np.pi), 0.25 * (1 - c), ALU.mult, ALU.add))
                    link(dve.tensor_scalar(ang[0], ang[0], ROUND, ROUND, ALU.add, ALU.subtract))
                    link(dve.scalar_tensor_tensor(ang[2 + c], ang[0], -TURN[0], ang[1], ALU.mult, ALU.add))
                    for part in TURN[1:]:
                        link(dve.scalar_tensor_tensor(ang[2 + c], ang[0], -part, ang[2 + c], ALU.mult, ALU.add))
                    link(dve.tensor_scalar(ang[2 + c], ang[2 + c], (1 - c) * np.pi / 2, PI, ALU.add, ALU.min))
                    dve.tensor_scalar(ang[2 + c], ang[2 + c], -PI, None, ALU.max).then_inc(trig_v.sem, trig_v.mark("angle", c))

            for l in range(2):
                def ffn(f, r):
                    if not on(f"{f}u{l}0"):
                        return
                    for part in range(3):
                        swiglu(f"{f}u{l}{part}", None if part else r)
                        if part < 2:
                            residual(f"{f}d{l}{part}", 0.5, (memory, angles)[part] if (f, l) == ("f1", 0) else None)
                        elif f == "f1":
                            follow(f"{f}d{l}{part}", 0.5, r + 1, "mix_norm_2", 8 * l)
                        elif l == 0:
                            follow(f"{f}d{l}{part}", 0.5, 9, "ffn1_norm_2", 8)
                        else:
                            follow(f"{f}d{l}{part}", 0.5, 14)
                r = 4 + 5 * l
                ffn("f1", r)
                if on(f"conv{l}"):
                    for k in range(2):
                        dve.memset(av[k][:, 0:30], 0.0)
                        ins = dve.memset(hc[k][:, 0:2], 0.0)
                    ins.then_inc(conv_v.sem, conv_v.mark("pads", l))
                    for i in range(5):
                        n = P0[f"conv{l}"] + i
                        q = n % 2
                        if i == 0:
                            norm_var(r + 1)
                        for k in range(2):
                            prep_lo(n, q, k)
                            if (i, k) == (0, 0):
                                norm_rstd(r + 1)
                            product(n, k)
                            dst = (av[k][:, 30:30 + S], tmp(4 + k), bg[k], hc[k][:, 2:2 + S], tmp(2 + k))[i]
                            ins = dve.tensor_tensor(dst, G[2 * q + k][:, :], rstd[:, :], ALU.mult)
                            if i == 1:
                                ins.then_inc(conv_v.sem, conv_v.mark("gate", l, k))
                            elif k == 1:
                                ins.then_inc(s_free, 1)
                        if i == 1:
                            for k in range(2):
                                dve.wait_ge(conv_a.sem, conv_a.at("gate", l, k))
                                ins = dve.tensor_tensor(av[k][:, 30:30 + S], av[k][:, 30:30 + S], tmp(4 + k), ALU.mult)
                            ins.then_inc(s_free, 1)
                        dve.wait_ge(s_free, n + 1)
                        if i == 4:
                            for k in range(2):
                                ins = dve.tensor_tensor(hc[k][:, 2:2 + S], hc[k][:, 2:2 + S], tmp(2 + k), ALU.mult)
                            link(ins)
                            for c in range(2):
                                ins = dve.tensor_tensor(sincos_r[:, c, :], sincos[:, c, :], rstd[:, :], ALU.mult)
                            link(ins)
                    total = sum(NPAIR[f"{x}{l}"] for x in ("kidx", "qidx", "q", "k", "vv")) * 2
                    step = {"at": 0}

                    def taps(_):
                        a = step["at"] * 5
                        step["at"] += 1
                        conv_taps(l, a, a + 5 if step["at"] < total else 2 * CONV_TAPS + 8)

                    def conv_taps(l, a, b):
                        for t in range(a, min(b, 2 * CONV_TAPS + 8)):
                            if t < 2 * CONV_TAPS:
                                k, t = t % 2, t // 2
                                w = col("conf_dw_2", (l * CONV_TAPS + t) * 2 + k)
                                x = av[k][:, t:t + S]
                                if t == 0:
                                    ins = dve.tensor_scalar(cv[k], x, w, col("conf_dw_b_2", 2 * l + k), ALU.mult, ALU.add)
                                else:
                                    ins = dve.scalar_tensor_tensor(cv[k], x, w, cv[k], ALU.mult, ALU.add)
                                if t == CONV_TAPS - 1:
                                    ins.then_inc(conv_v.sem, conv_v.mark("summand", l, 0, k))
                                    continue
                            else:
                                t -= 2 * CONV_TAPS
                                k, t = t % 2, t // 2
                                if t < 3:
                                    w = col("sc_dw_2", (l * 3 + t) * 2 + k)
                                    x = hc[k][:, t:t + S]
                                    if t == 0:
                                        ins = dve.tensor_scalar(tmp(2 + k), x, w, None, ALU.mult)
                                    else:
                                        ins = dve.scalar_tensor_tensor(tmp(2 + k), x, w, tmp(2 + k), ALU.mult, ALU.add)
                                else:
                                    dve.tensor_tensor(tmp(4 + k), tmp(2 + k), bg[k], ALU.mult)\
                                       .then_inc(conv_v.sem, conv_v.mark("short", l, k))
                                    continue
                            link(ins)

                    n = P0[f"kidx{l}"]
                    for k in range(2):
                        prep_lo(n, n % 2, k)
                        product(n, k)
                        if k == 0:
                            dve.tensor_copy(ki, G[2 * (n % 2)][:, :])
                        else:
                            dve.tensor_tensor(wi, G[2 * (n % 2) + 1][:, :], rstd[:, :], ALU.mult).then_inc(s_free, 1)
                        taps(0)
                    only_prep(f"qidx{l}", taps)

                    def more(name):
                        def body(at_):
                            taps(at_)
                            if at_ < len(rotations[name]):
                                rope(dve, link, l, rotations[name][at_], at_)
                        return body
                    for x in ("q", "k"):
                        only_prep(f"{x}{l}", more(x))
                    for i in range(2):
                        n = P0[f"vv{l}"] + i
                        q = n % 2
                        for k in range(2):
                            prep_lo(n, q, k)
                            if k == 0:
                                dve.wait_ge(s_free, n)
                            product(n, k)
                            ins = dve.tensor_tensor(cut(vt2, 2 * i + k), G[2 * q + k][:, :], rstd[:, :], ALU.mult)
                            if k == 1:
                                ins.then_inc(s_free, 1)
                            more("vv")(2 * i + k)
                if on(f"vv{l}"):
                    dsa_dve(dve, link, l, lo_of)
                follow(f"mwo{l}", 1.0, r + 2, "xa_norm_2", 8 * l)
                scaled(f"xq{l}", xq, r + 2)
                only_prep(f"xk{l}")
                only_prep(f"xv{l}")
                if on(f"xv{l}"):
                    cross_dve(dve, link, l, lo_of)
                follow(f"xo{l}", 1.0, r + 3, "ffn2_norm_2", 8 * l)
                ffn("f2", r + 3)
            if whole:
                norm_in_place(14, "final_norm_2")
                for t in range(NB):
                    for o in range(2):
                        dve.wait_ge(full.sem, full.at("out", t, o))
                        dve.tensor_copy(v_out(t)[:, o * S:(o + 1) * S], B[BANK.get(("out", t, o), 0)][:, :])\
                           .then_inc(turn_v.sem, turn_v.mark("out", t, o))

        @block.gpsimd
        def _(pool):
            pool.dma_start(x_in[:, :, :], A["x"][0].rearrange("(t p) d -> p t d", p=P)).then_inc(s_x, 16)
            pool.dma_start(consts[:, :], A["consts"]).then_inc(s_const, 16)
            for b, items in enumerate(BATCHES):
                r = 0
                for n, c in items:
                    v = A[n]
                    if len(v.shape) > 1:
                        v = v.rearrange({2: "a b -> (a b)", 3: "a b c -> (a b c)"}[len(v.shape)])
                    pool.dma_start(prow[r:r + c, b, :], v.rearrange("(r p) -> r p", p=P)).then_inc(s_par, 16)
                    r += c
            pool.dma_start(small[0:16, 176:177], A["ssd_dt_bias"].rearrange("o h -> h o")).then_inc(s_sp, 16)
            pool.dma_start(small[0:16, 177:178], A["ssd_a_log"].rearrange("o h -> h o")).then_inc(s_sp, 16)
            pool.dma_start(w_sp[:, :, :], A["gmlp_w_s"][0].rearrange("g t s -> t g s")).then_inc(s_gw, 16)
            for dst, src in ((g_bc, A["gmlp_ln_g"]), (b_bc, A["gmlp_ln_b"]),
                             (bs_bc, A["gmlp_b_s"].rearrange("o g t -> o (g t)"))):
                pool.dma_start(dst, src.to_broadcast([P, D])).then_inc(s_gb, 16)
            if on("lru"):
                pool.wait_ge(gmlp_v.sem, gmlp_v.at("lo", 7))
                for g, w in enumerate(("lru_w_r", "lru_w_i")):
                    pool.dma_start(lru_w[:, g, :, :], A[w][0].rearrange("h i j -> i h j")).then_inc(s_lw, 16)
            if on("dt"):
                pool.dma_start(small[:, 200:216], A["ssd_d"].to_broadcast([P, 16])).then_inc(s_sp, 16)
            if on("f1u00"):
                pool.wait_ge(s_mm, 2 * P0["up0"] + 2)
                pool.dma_start(mem_in[:, :, :], A["mem_2"][0].rearrange("(t p) d -> p t d", p=P)).then_inc(s_mem, 16)
                pool.dma_start(ang[4].bitcast(I32), A["positions_2"].to_broadcast([P, S])).then_inc(s_pos, 16)
            for l in range(2):
                if on(f"vv{l}"):
                    for b in range(1, NB):
                        pool.wait_ge(dsa_v.sem, dsa_v.at("idx", l, b, IDXH - 1))
                        pool.affine_select(out=score[:, b * P:(b + 1) * P], in_=score[:, b * P:(b + 1) * P],
                                           compare_op=ALU.is_ge, fill=NEG, base=0, pattern=[[-1, P]],
                                           channel_multiplier=1).then_inc(dsa_p.sem, dsa_p.mark(l, b))


def constants():
    i = np.arange(P)
    ident = np.eye(P, dtype=np.float32)
    ones = np.ones((P, P), np.float32)
    causal = (i[None, :] >= i[:, None]).astype(np.float32)
    rot = np.zeros((P, P), np.float32)
    for m in range(P):
        if m % 64 < 32:
            rot[m + 32, m] = -1.0
        else:
            rot[m - 32, m] = 1.0
    qcausal = np.where(i[None, :] <= i[:, None], 0.0, NEG).astype(np.float32)
    freq = np.float32(10000.0) ** (-np.arange(0, 64, 2, dtype=np.float32) / np.float32(64))
    return np.concatenate([ident, ones, causal, rot, qcausal, np.tile(freq, 4)[:, None].astype(np.float32)], axis=1)


NAMES = ["x", "norm_mix_g", "w_in", "b_gate", "gmlp_ln_g", "gmlp_ln_b", "gmlp_w_s", "gmlp_b_s", "lru_conv_w", "lru_conv_b",
         "lru_w_r", "lru_b_r", "lru_w_i", "lru_b_i", "lru_lambda", "ssd_conv_w", "ssd_conv_b", "ssd_dt_bias",
         "ssd_a_log", "ssd_d", "ssd_norm_g", "w_branch_a", "w_branch_b", "w_branch_c", "w_out", "norm_mlp_g",
         "w_mlp_up", "w_mlp_down", "final_norm_g", "mem_2", "positions_2", "ffn1_norm_2", "ffn1_w_gate_2",
         "ffn1_w_up_2", "ffn1_w_down_2", "mix_norm_2", "w_in_2", "conf_dw_2", "conf_dw_b_2", "conf_ln_g_2",
         "conf_ln_b_2", "sc_dw_2", "w_out_2", "xa_norm_2", "mem_norm_2", "xa_wq_2", "xa_wkv_2", "xa_wo_2",
         "ffn2_norm_2", "ffn2_w_gate_2", "ffn2_w_up_2", "ffn2_w_down_2", "final_norm_2"]


def kernel(**inputs):
    import concourse.bacc as bacc
    import concourse.bass_utils as bass_utils

    arrays = {f"in_{n}": np.ascontiguousarray(inputs[n]) for n in NAMES}
    arrays["in_consts"] = constants()

    def build():
        nc = bacc.Bacc("TRN2", target_bir_lowering=False, num_devices=1)
        A = {n[3:]: nc.dram_tensor(n, a.shape, mybir.dt.from_np(a.dtype), kind="ExternalInput").ap()
             for n, a in arrays.items()}
        out = nc.dram_tensor("out_0", (1, S, D), F32, kind="ExternalOutput").ap()
        build_program(nc, A, out)
        return nc

    build()
    nc = build()
    r = bass_utils.run_bass_kernel_spmd(nc, [arrays], core_ids=[0])
    return r.results[0]["out_0"]
```

```python
from contextlib import ExitStack

import numpy as np

import concourse.bass as bass
from concourse import mybir

P = 128
S = 512
D = 1024
KT = D // P
NB = S // P
MEM = 256
EPS = 1e-6
LN_EPS_2 = 1e-5
F_GMLP_U, F_GMLP_V, F_LRU_X, F_LRU_G, F_Z, F_XBC, F_DT, F_GATE = 0, 1024, 2048, 3072, 4096, 5120, 7168, 7184
FFN_PARTS = (8, 8, 6)
DFF = 2816
HEADS2, IDXH = 8, 4
TOPK = 128
NEG = -1.0e30
TAKEN = -3.0e38
IDX_SCALE = 0.0625
CONV_TAPS = 31

F32 = mybir.dt.float32
F32R = mybir.dt.float32r
I32 = mybir.dt.int32
ACT = mybir.ActivationFunctionType
ALU = mybir.AluOpType
AX = mybir.AxisListType

BATCHES = [
    [("norm_mix_g", 8), ("b_gate", 24), ("lru_conv_b", 8), ("lru_b_r", 8), ("lru_b_i", 8),
     ("lru_lambda", 8), ("ssd_conv_b", 16), ("ssd_norm_g", 8), ("norm_mlp_g", 8), ("final_norm_g", 8),
     ("final_norm_2", 8)],
    [("lru_conv_w", 32), ("ssd_conv_w", 64), ("conf_dw_b_2", 4), ("conf_ln_g_2", 4), ("conf_ln_b_2", 4),
     ("sc_dw_2", 12)],
    [("ffn1_norm_2", 16), ("mix_norm_2", 16), ("xa_norm_2", 16), ("mem_norm_2", 16), ("ffn2_norm_2", 16)],
    [("conf_dw_2", 124)],
]
COL = {}
for _b, _items in enumerate(BATCHES):
    _r = 0
    for _n, _c in _items:
        COL[_n] = _b * P + _r
        _r += _c
    assert _r <= P

PHASES = [("v", 4, 8), ("u", 4, 8), ("ga", 8, 8), ("lru", 8, 8), ("gb", 8, 8), ("xbc", 8, 8), ("dt", 1, 8),
          ("z", 4, 8), ("gc", 8, 8), ("wo", 4, 8)]
for _p in range(4):
    PHASES += [(f"up{_p}", 4, 8), (f"down{_p}", 4, 8)]
for _l in range(2):
    for _i, _n in enumerate(FFN_PARTS):
        PHASES += [(f"f1u{_l}{_i}", _n, 8), (f"f1d{_l}{_i}", 4, _n)]
    PHASES += [(f"kidx{_l}", 1, 8), (f"qidx{_l}", 1, 8), (f"conv{_l}", 5, 8), (f"q{_l}", 2, 8), (f"k{_l}", 2, 8),
               (f"vv{_l}", 2, 8),
               (f"mwo{_l}", 4, 8), (f"xq{_l}", 4, 8), (f"xk{_l}", 4, 8), (f"xv{_l}", 4, 8), (f"xo{_l}", 4, 8)]
    for _i, _n in enumerate(FFN_PARTS):
        PHASES += [(f"f2u{_l}{_i}", _n, 8), (f"f2d{_l}{_i}", 4, _n)]
P0, NPAIR, KTS = {}, {}, {}
_at = 0
for _name, _n, _k in PHASES:
    P0[_name], NPAIR[_name], KTS[_name] = _at, _n, _k
    _at += _n
TOTAL = _at
BANK = {}
ROUND = 12582912.0
PI = 3.1415925
TURN = (6.28125, 0.001934051513671875, 1.2556659146e-06)


def three_dmas(name):
    return name.startswith("kidx")


def kind(name):
    if name in ("ga", "gb", "gc"):
        return "gated"
    if name.startswith("up"):
        return "relu2"
    if name[:3] in ("f1u", "f2u"):
        return "swiglu"
    return ""


INCS = {"gated": (1, 0, 0), "relu2": (1, 2, 2), "swiglu": (2, 2, 1), "": (0, 0, 0)}
BASE = {}
_acc = [0, 0, 0]
for _name, _n, _k in PHASES:
    BASE[_name] = tuple(_acc)
    _acc = [a + _n * d for a, d in zip(_acc, INCS[kind(_name)])]
LANDED = []
_slot = [0, 0]
for _name, _n, _k in PHASES:
    for _i in range(_n):
        _s = len(LANDED) % 2
        _slot[_s] += 48 if three_dmas(_name) else 32
        LANDED.append(_slot[_s])
LANDED.append(0)


def loop_pairs(eng, name, body, unroll=False, peel=0):
    count, p0 = NPAIR[name], P0[name]
    if unroll or count - peel < 4:
        peel = count
    for i in range(peel):
        body(i, p0 + i, (p0 + i) % 2, LANDED[p0 + i + 1])
    times = (count - peel) // 2
    if times:
        p1 = p0 + peel
        with eng.Fori(0, times) as it:
            for b in range(2):
                body(2 * it + (peel + b), 2 * it + (p1 + b), (p1 + b) % 2, it * 32 + LANDED[p1 + b + 1])
    for i in range(peel + 2 * times, count):
        body(i, p0 + i, (p0 + i) % 2, LANDED[p0 + i + 1])


class Signal:
    marks = {}

    def __init__(self, sem, name):
        self.sem, self.name, self.n = sem, name, 0

    def mark(self, *key):
        self.n += 1
        Signal.marks[self.name, key] = self.n
        return 1

    def at(self, *key):
        return Signal.marks.get((self.name, key), 1)


def cut(t, i, n=S):
    if isinstance(i, int):
        return t[:, i * n:(i + 1) * n]
    return t[:, bass.ds(i * n, n)]


def build_program(nc, A, out):
    names = [n for n, _, _ in PHASES]
    last_pair = TOTAL - 1

    with ExitStack() as ctx:
        def sb(name, shape, dt=F32):
            return ctx.enter_context(nc.sbuf_tensor(name, shape, dt))

        def sem(name):
            return ctx.enter_context(nc.semaphore(name))

        def signal(name):
            return Signal(sem(name), name)

        raw = sb("raw", [P, 2, KT, 256])
        w_hi = sb("w_hi", [P, 2, KT, P], F32R)
        w_lo = sb("w_lo", [P, 2, KT, P], F32R)
        xn_hi = sb("xn_hi", [P, KT * S], F32R)
        xn_lo = sb("xn_lo", [P, KT * S], F32R)
        y_hi = sb("y_hi", [P, KT * S], F32R)
        y_lo = sb("y_lo", [P, KT * S], F32R)
        h = sb("h", [P, KT * S])
        consts = sb("consts", [P, 5 * P + 1])
        ident, ones, causal, rot, qcausal = (consts[:, i * P:(i + 1) * P] for i in range(5))
        inv_freq = consts[:, 5 * P:5 * P + 1]
        par = sb("par", [P, 4 * P])
        temps = sb("temps", [P, 6 * S])
        stat = sb("stat", [P, S])
        rstd = sb("rstd", [P, S])
        small = sb("small", [P, 256])
        size = 37 * S
        arena = sb("arena", [P, size])

        def tmp(i, n=S):
            return temps[:, i * S:i * S + n]

        def at(off, *shape):
            n = int(np.prod(shape))
            assert off + n <= size, (off, shape, size)
            v = arena[:, off:off + n]
            if len(shape) == 1:
                return v
            dims = "abcd"[:len(shape)]
            return v.rearrange(f"p ({' '.join(dims)}) -> p {' '.join(dims)}", **dict(zip(dims[:-1], shape[:-1])))

        def col(name, i=0, rows=P):
            if isinstance(i, int):
                return par[0:rows, COL[name] + i:COL[name] + i + 1]
            return par[0:rows, bass.ds(i + COL[name], 1)]

        G = [ctx.enter_context(nc.psum_tensor(f"G{i}", [P, S], F32)) for i in range(4)]
        B = [ctx.enter_context(nc.psum_tensor(f"B{i}", [P, S], F32)) for i in range(4)] + G

        s_load = [sem("s_load0"), sem("s_load1")]
        s_whi, s_wlo = sem("s_weights_hi"), sem("s_weights_lo")
        s_mm, s_free = sem("s_panels_multiplied"), sem("s_pairs_evacuated")
        s_par_more = sem("s_more_params_in")
        s_ao, s_yh, s_yl = sem("s_evacuated_part"), sem("s_y_hi"), sem("s_y_lo")
        s_const, s_par, s_x, s_gw, s_gb, s_lw, s_sp, s_mem, s_pos, s_out = (sem("s_" + n) for n in (
            "const_in", "params_in", "x_in", "gmlp_w_in", "gmlp_rows_in", "lru_w_in", "ssd_params_in", "mem_in",
            "pos_in", "out"))
        full = signal("s_bank_full")
        norm_a, norm_v = signal("s_norm_act"), signal("s_norm_vector")
        turn_a, turn_v = signal("s_turned_out_act"), signal("s_turned_out_vector")
        gmlp_v, gmlp_a, gmlp_p = signal("s_gmlp_vector"), signal("s_gmlp_act"), signal("s_gmlp_pool")
        lru_v, lru_a = signal("s_lru_vector"), signal("s_lru_act")
        xbc_v, xbc_a = signal("s_xbc_vector"), signal("s_xbc_act")
        ssd_v, ssd_a = signal("s_ssd_vector"), signal("s_ssd_act")
        z_v, z_a = signal("s_z_vector"), signal("s_z_act")
        split_a, split_v = signal("s_split_hi"), signal("s_split_lo")
        trig_v, trig_a = signal("s_angles"), signal("s_sines")
        rope_v = signal("s_rope")
        conv_v, conv_a, conv_p = signal("s_conv_vector"), signal("s_conv_act"), signal("s_conv_pool")
        dsa_v, dsa_a = signal("s_dsa_vector"), signal("s_dsa_act")
        xa_v, xa_a = signal("s_cross_vector"), signal("s_cross_act")
        s_dve, s_act = sem("s_vector_chain"), sem("s_act_chain")
        loads_free = signal("s_loads_free")

        T = S
        MERGED = 0
        merged = arena[:, 0:8 * T]
        u = arena[:, 8 * T:16 * T]
        vt = arena[:, 16 * T:24 * T]
        v_tok = at(24 * T, NB, D)
        w_sp = at(32 * T, 8, P)
        w_spT = at(34 * T, 8, P)
        g_bc, b_bc, bs_bc = at(0, D), at(D, D), at(2 * D, D)
        x_in = at(8 * T, NB, D)
        prow = at(16 * T, 4, P)
        lru_w = at(8 * T, 2, 8, P)
        xpad = [at(12 * T + q * (S + 3), S + 3) for q in range(2)]
        lt = [at(12 * T + 2 * (S + 3) + i * T, T) for i in range(16)]
        xbc = arena[:, 8 * T:24 * T]
        sst = at(24 * T, NB, 96)
        chunk_decay = at(24 * T + 384, NB, 16)
        acs = at(25 * T, T)
        pre = [at((26 + i) * T, T) for i in range(11)]
        stk = pre[0]
        b_tok = at(26 * T, NB, P)
        xdt = at(27 * T, NB, 256)
        xdd = at(29 * T, NB, 256)
        cb = at(31 * T, NB, P)
        st = at(32 * T, 3, 256)
        head_exp, head_decay = [pre[8], tmp(4)], [pre[9], tmp(2)]
        head_m, head_ce = [pre[10], tmp(3)], [tmp(0), tmp(1)]
        cpad = [at(26 * T + i * (S + 3), S + 3) for i in range(4)]
        cacc = [at(31 * T + i * T, T) for i in range(2)]
        memn = arena[:, 0:8 * MEM]
        sincos = at(4 * T, 2, T)
        mem_in = at(6 * T, 2, D)
        mem_t = arena[:, 10 * T:14 * T]
        ang = [at((14 + i) * T, T) for i in range(5)]
        qkv = arena[:, 6 * T:14 * T]
        qi = arena[:, 14 * T:16 * T]
        ki = arena[:, 16 * T:17 * T]
        vt2 = arena[:, 17 * T:21 * T]
        wi = arena[:, 21 * T:22 * T]
        v_key = at(22 * T, NB, 512)
        w_tok = small[:, 128:144].rearrange("p (t h) -> p t h", h=4)
        av = [at(22 * T + k * (S + 30), S + 30) for k in range(2)]
        hc = [at(24 * T + 60 + k * (S + 2), S + 2) for k in range(2)]
        bg = [at((27 + k) * T, T) for k in range(2)]
        cv = [at((35 + k) * T, T) for k in range(2)]
        score, work = at(29 * T, T), at(30 * T, T)
        relus = [at(31 * T, T), at(32 * T, T)]
        bias = [qcausal, tmp(0, 2 * P), at(26 * T + 64, 3 * P), at(21 * T, 4 * P)]
        att = [at((29 + i) * T, T) for i in range(4)]
        o_t = arena[:, 33 * T:37 * T]
        sincos_r = at(33 * T, 2, T)
        mem_rstd = at(20 * T, MEM)
        xq = arena[:, 6 * T:14 * T]
        xk = arena[:, 14 * T:18 * T]
        xvt = arena[:, 18 * T:22 * T]
        xv = at(22 * T, 2, D)
        xp = [at(26 * T + i * MEM, MEM) for i in range(2)]
        xpt = [at((27 + 2 * i) * T, 2, S) for i in range(2)]

        def source(name, i):
            nk = KTS[name]
            l = int(name[-1]) if name[-1].isdigit() else 0

            def columns(W, c0, r0=0):
                v = W[r0:r0 + nk * P, bass.ds(c0, 256)].rearrange("(k p) n -> p k n", p=P)
                hk = nk // 2
                return [((slice(0, hk), slice(0, 256)), v[:, 0:hk, :]), ((slice(hk, nk), slice(0, 256)), v[:, hk:nk, :])]

            def two(W1, c1, W2, c2):
                return [((slice(0, 8), slice(0, P)), W1[:, bass.ds(c1, P)].rearrange("(k p) n -> p k n", p=P)),
                        ((slice(0, 8), slice(P, 256)), W2[:, bass.ds(c2, P)].rearrange("(k p) n -> p k n", p=P))]

            w_in = A["w_in"][0]
            if name in ("u", "v", "xbc", "z"):
                return columns(w_in, i * 256 + {"u": F_GMLP_U, "v": F_GMLP_V, "xbc": F_XBC, "z": F_Z}[name])
            if name in ("ga", "gb", "gc"):
                return two(w_in, i * P + (F_GATE + "abc".index(name[1]) * D), A["w_branch_" + name[1]][0], i * P)
            if name == "lru":
                return two(w_in, i * P + F_LRU_X, w_in, i * P + F_LRU_G)
            if name == "dt":
                v = w_in[:, F_DT:F_DT + 16].rearrange("(k p) n -> p k n", p=P)
                return [((slice(a, a + 4), slice(0, 16)), v[:, a:a + 4, :]) for a in (0, 4)]
            if name == "wo":
                return columns(A["w_out"][0], i * 256)
            if name.startswith("up"):
                return columns(A["w_mlp_up"][0], i * 256 + l * D)
            if name.startswith("down"):
                return columns(A["w_mlp_down"][0], i * 256, l * D)
            if name[0] == "f":
                layer, part = int(name[3]), int(name[4])
                k0 = sum(FFN_PARTS[:part]) * P
                f = "ffn" + name[1]
                if name[2] == "u":
                    return two(A[f + "_w_gate_2"][layer], i * P + k0, A[f + "_w_up_2"][layer], i * P + k0)
                return columns(A[f + "_w_down_2"][layer], i * 256, k0)
            w2, n = A["w_in_2"][l], name[:-1]
            if n == "kidx":
                v = w2[:, 3072:3136].rearrange("(k p) n -> p k n", p=P)
                w = w2[:, 3136:3140].rearrange("(k p) n -> p k n", p=P)
                return [((slice(0, 8), slice(0, 64)), v), ((slice(0, 8), slice(64, P)), v),
                        ((slice(0, 8), slice(P, P + 4)), w)]
            first = {"conv": 0, "q": 1280, "k": 1792, "vv": 2304, "qidx": 2816}
            if n in first:
                return columns(w2, i * 256 + first[n])
            W, c0 = {"mwo": ("w_out_2", 0), "xk": ("xa_wkv_2", 0), "xv": ("xa_wkv_2", D), "xq": ("xa_wq_2", 0),
                     "xo": ("xa_wo_2", 0)}[n]
            return columns(A[W][l], i * 256 + c0)

        def v_out(t):
            return arena[:, (2 * t) * T:(2 * t + 2) * T]

        steps = [(b, hh) for b in range(NB) for hh in range(HEADS2)]
        MIX = ("kidx", "qidx", "conv", "q", "k", "vv")
        first_panel = {x: 2 * (P0[x + "0"] - P0["kidx0"]) for x in MIX}

        rotations = {4: ("ki", 0), 5: ("qi", 0), 6: ("qi", 1)}
        rotations |= {first_panel["k"] + t: ("q", t) for t in range(4)} | {first_panel["vv"] + t: ("k", t) for t in range(4)}
        index_heads = {p + i: (b, (2 * i, 2 * i + 1)) for b, p in ((1, 7), (2, 12), (3, 17)) for i in range(2)}
        selections = {p0 + i: (b, range(i * each, min(16, (i + 1) * each)))
                      for b, p0, each in ((1, 8, 4), (2, 13, 4), (3, 18, 2)) for i in range(-(-16 // each))}
        mean_step, square_step, root_step = -2, 0, 2

        def load_params(eng, b):
            r = 0
            for n, c in BATCHES[b]:
                v = A[n]
                if len(v.shape) > 1:
                    v = v.rearrange({2: "a b -> (a b)", 3: "a b c -> (a b c)"}[len(v.shape)])
                eng.dma_start(prow[r:r + c, b, :], v.rearrange("(r p) -> r p", p=P)).then_inc(s_par if b == 0 else s_par_more, 16)
                r += c

        products = [(kind_, t, k) for kind_, taps in (("conf", CONV_TAPS), ("short", 3)) for t in range(taps) for k in range(2)]
        adds = {x: a for a, x in enumerate(x for x in products if x[1])}
        first_products, PRODUCTS_EACH = 8, 4
        tap_buffers = [tmp(1), stat[:, :], tmp(4), tmp(5)]

        def rope_tile(key):
            kind_, t = key
            return {"q": lambda: cut(qkv, t), "k": lambda: cut(qkv, 4 + t), "qi": lambda: cut(qi, t), "ki": lambda: ki}[kind_]()

        cross_steps = [(x, b) for x in range(4) for b in range(NB)]

        def att_p(s):
            return att[2 * (s % 2)]

        def att_pt(s):
            return att[2 * (s % 2) + 1]

        block = ctx.enter_context(nc.Block())

        @block.sync
        def _(sp):
            for name in names:
                def load(i, n, q, landed):
                    if not isinstance(n, int) or n >= 2:
                        sp.wait_ge(s_wlo, 2 * n - 2)
                    for (ks, cs), src in source(name, i):
                        sp.dma_start(raw[:, q, ks, cs], src).then_inc(s_load[q], 16)
                loop_pairs(sp, name, load, unroll=P0[name] < 2)
            for t in range(NB):
                sp.wait_ge(turn_v.sem, turn_v.at("out", t, 1))
                sp.dma_start(out[0, t * P:(t + 1) * P, :], v_out(t)).then_inc(s_out, 16)
            sp.wait_ge(s_out, 16 * NB)

        def ssd_pe(pe, take, turn):
            pe.wait_ge(ssd_a.sem, ssd_a.at("stk"))
            turn(("sst",), [stk[:, c * P:(c + 1) * P] for c in range(NB)], (ssd_a, ("sst",)))
            pe.wait_ge(ssd_v.sem, ssd_v.at("ends"))
            bank = take(("ends",), (ssd_a, ("ends",)))
            pe.matmul(bank[:, 0:64], ones[0:16, :], small[0:16, 32:96], start=True, stop=True)\
              .then_inc(full.sem, full.mark("ends"))

            def row(hh):
                g, r = hh // 4, hh % 4
                bank = take(("row", g, r), (ssd_v, ("seg", g, r)))
                pe.matmul(bank[:, :], ident[0:16, hh:hh + 1].to_broadcast([16, P]), acs[0:16, :],
                          start=True, stop=True).then_inc(full.sem, full.mark("row", g, r))

            row(0)
            row(1)
            for g in range(4):
                bt, ct = cut(xbc, 8 + g), cut(xbc, 12 + g)
                if g == 0:
                    pe.wait_ge(xbc_a.sem, xbc_a.at("silu", 15))
                turn(("b_tok", g), [bt[:, c * P:(c + 1) * P] for c in range(NB)], (ssd_a, ("b_tok", g)))
                for k in range(2):
                    turn(("x_tok", g, k), [cut(xbc, 2 * g + k)[:, c * P:(c + 1) * P] for c in range(NB)],
                         (ssd_v, ("xdt", g, k)))
                bank = take(("cb", g), (ssd_v, ("cb", g)))
                for c in range(NB):
                    cs = slice(c * P, (c + 1) * P)
                    m = pe.matmul(bank[:, cs], bt[:, cs], ct[:, cs], start=True, stop=True)
                m.then_inc(full.sem, full.mark("cb", g))
                pe.wait_ge(ssd_a.sem, ssd_a.at("b_tok", g))
                pe.wait_ge(ssd_v.sem, ssd_v.at("xdd", g))
                for o in range(2):
                    bank = take(("st", g, o), (ssd_v, ("st", g, o)))
                    for c in range(2 * o, min(2 * o + 2, 3)):
                        m = pe.matmul(bank[:, (c % 2) * 256:(c % 2) * 256 + 256], b_tok[:, c, :], xdd[:, c, :],
                                      start=True, stop=True)
                    m.then_inc(full.sem, full.mark("st", g, o))

                for r in range(4):
                    if r % 2 == 0:
                        bank = take(("y", g, r // 2), (ssd_v, ("y", g, r // 2)))
                    if 4 * g + r + 2 < 16:
                        row(4 * g + r + 2)
                    pe.wait_ge(ssd_v.sem, ssd_v.at("m", g, r))
                    if r == 0:
                        pe.wait_ge(ssd_v.sem, ssd_v.at("st", g, 1))
                    o = bank[64 * (r % 2):64 * (r % 2) + 64, :]
                    for c in range(NB):
                        cs = slice(c * P, (c + 1) * P)
                        m = pe.matmul(o[:, cs], xdt[:, c, 64 * r:64 * r + 64], head_m[r % 2][:, cs], start=True, stop=c == 0)
                        if c:
                            m = pe.matmul(o[:, cs], st[:, c - 1, 64 * r:64 * r + 64], head_ce[r % 2][:, cs],
                                          start=False, stop=True)
                    m.then_inc(full.sem, full.mark("y", g, r))

        def dsa_pe(pe, l, take, turn):
            for t in range(4):
                turn(("v_key", l, t), [cut(vt2, t)[:, b * P:(b + 1) * P] for b in range(NB)], (rope_v, ("v_key", l, t)))
            pe.wait_ge(rope_v.sem, rope_v.at("tile", l, "k", 3))

            def scores(s):
                b, hh = steps[s]
                o, w = 64 * (hh % 2), (b + 1) * P
                bank = take(("s", l, s), (dsa_v, ("s", l, s)))
                pe.matmul(bank[:, 0:w], cut(qkv, hh // 2)[o:o + 64, b * P:(b + 1) * P],
                          cut(qkv, 4 + hh // 2)[o:o + 64, 0:w], start=True, stop=True)\
                  .then_inc(full.sem, full.mark("s", l, s))

            def sums(step):
                bank = take(("cln", l, step), (conv_v, ("stat", l, step)))
                for k in range(2):
                    if step:
                        pe.wait_ge(conv_v.sem, conv_v.at("summand", l, step, k))
                    else:
                        pe.wait_ge(conv_p.sem, conv_p.at("add", l, adds["conf", CONV_TAPS - 1, k]))
                    m = pe.matmul(bank[:, :], ones, cv[k] if step == 0 else tmp(4 + k), start=k == 0, stop=k == 1)
                m.then_inc(full.sem, full.mark("cln", l, step))

            obank = None
            for i in range(-3, len(steps)):
                if i + 3 < len(steps):
                    scores(i + 3)
                if i == mean_step:
                    sums(0)
                if i == square_step:
                    sums(1)
                if i >= 0:
                    b, hh = steps[i]
                    if i == 0:
                        pe.wait_ge(rope_v.sem, rope_v.at("v_key", l, 3))
                    if hh % 2 == 0:
                        obank = take(("o", l, b, hh // 2), (dsa_v, ("o", l, b, hh // 2)))
                    pe.wait_ge(dsa_a.sem, dsa_a.at("pt", l, i))
                    o = 64 * (hh % 2)
                    for t in range(b + 1):
                        m = pe.matmul(obank[o:o + 64, 0:P], v_key[:, t, hh * 64:hh * 64 + 64],
                                      att_pt(i)[:, t * P:(t + 1) * P], start=t == 0, stop=t == b)
                    m.then_inc(full.sem, full.mark("o", l, b, hh))
                if 0 <= i + 1 < len(steps):
                    pe.wait_ge(dsa_a.sem, dsa_a.at("p", l, i + 1))
                    turn(("p", l, i + 1), [att_p(i + 1)[:, t * P:(t + 1) * P] for t in range(steps[i + 1][0] + 1)],
                         (dsa_a, ("pt", l, i + 1)))

        def cross_pe(pe, l, take, turn):
            for j in range(0, KT, 2):
                turn(("xv", l, j), [xvt[:, (j + d) * MEM + t * P:(j + d) * MEM + (t + 1) * P] for d in range(2) for t in range(2)],
                     (xa_v, ("xv", l, j)))

            def scores(s):
                x, b = cross_steps[s]
                bank = take(("xs", l, s), (xa_a, ("exp", l, s)))
                for d in range(2):
                    m = pe.matmul(bank[:, 0:MEM], cut(xq, 2 * x + d)[:, b * P:(b + 1) * P], cut(xk, 2 * x + d, MEM),
                                  start=d == 0, stop=d == 1)
                m.then_inc(full.sem, full.mark("xs", l, s))

            for i in range(-3, len(cross_steps)):
                if i + 3 < len(cross_steps):
                    scores(i + 3)
                if i >= 0 and cross_steps[i][1] == NB - 1:
                    x = cross_steps[i][0]
                    pe.wait_ge(xa_v.sem, xa_v.at("xv", l, 6))
                    pe.wait_ge(xa_a.sem, xa_a.at("pt", l, i))
                    for d in range(2):
                        bank = take(("xo", l, x, d), (xa_v, ("lo", l, 2 * x + d)))
                        for t in range(2):
                            m = pe.matmul(bank[:, :], xv[:, t, (2 * x + d) * P:(2 * x + d + 1) * P],
                                          xpt[x % 2][:, t, :], start=t == 0, stop=t == 1)
                        m.then_inc(full.sem, full.mark("xo", l, x, d))
                if 0 <= i + 1 < len(cross_steps):
                    pe.wait_ge(xa_a.sem, xa_a.at("p", l, i + 1))
                    turn(("xp", l, i + 1), [xp[(i + 1) % 2][:, t * P:(t + 1) * P] for t in range(2)],
                         (xa_a, ("pt", l, i + 1)))

        banks = {}

        @block.tensor
        def _(pe):
            banks.update(next=0, count=4, until=[None] * 8)

            def wide(on_):
                banks["count"] = 8 if on_ else 4
                if not on_:
                    for b in range(4, 8):
                        if banks["until"][b] is not None:
                            s_, k_ = banks["until"][b]
                            pe.wait_ge(s_.sem, s_.at(*k_))
                        banks["until"][b] = None

            def take(key, until):
                b = banks["next"] % banks["count"]
                banks["next"] += 1
                if banks["until"][b] is not None:
                    s_, k_ = banks["until"][b]
                    pe.wait_ge(s_.sem, s_.at(*k_))
                banks["until"][b] = until
                BANK[key] = b
                return B[b]

            def turn(key, blocks, until, idn=None):
                bank, m = take(key, until), None
                for o, src in enumerate(blocks):
                    m = pe.transpose(bank[0:src.shape[1], o * P:o * P + src.shape[0]], src,
                                     ident[0:src.shape[0], 0:src.shape[0]])
                m.then_inc(full.sem, full.mark(*key))

            def panel(k, bank, hi, lo, nk, n, ready=None):
                m = None
                for kt in range(nk):
                    if ready:
                        ready(k, kt)
                    for t, (a, b) in enumerate(((w_hi, hi), (w_hi, lo), (w_lo, hi))):
                        m = pe.matmul(bank[:, 0:n], a[:, k, kt, :], b[:, kt * S:kt * S + n],
                                      start=(kt == 0 and t == 0), stop=(kt == nk - 1 and t == 2))
                return m

            def pair(name, i, n, q, first, second, width, ready=None, after=None):
                if not isinstance(n, int) or n >= 2:
                    pe.wait_ge(s_free, n - 1)
                for k, (hi, lo) in enumerate((first, second)):
                    pe.wait_ge(s_wlo, 2 * n + (k + 1))
                    panel(k, G[2 * q + k], hi, lo, KTS[name], width, ready if isinstance(i, int) and i == 0 else None)\
                        .then_inc(s_mm, 1)
                    if after and isinstance(i, int):
                        after(i, k)

            xn, y = (xn_hi, xn_lo), (y_hi, y_lo)

            def gemm(name, first, second=None, width=S, unroll=False, ready=None, after=None):
                loop_pairs(pe, name,
                           lambda i, n, q, landed: pair(name, i, n, q, first, second or first, width, ready, after),
                           unroll=unroll or P0[name] < 2, peel=2 if ready else 0)

            def norm_pe(r, n=S):
                bank = take(("norm", r), (norm_v, ("var", r)))
                pe.wait_ge(norm_v.sem, norm_v.at("summed", r, KT - 1))
                pe.matmul(bank[:, 0:n], ones, stat[:, 0:n], start=True, stop=True)\
                  .then_inc(full.sem, full.mark("norm", r))

            def by_tile(sig, key, panel_=0):
                def ready(k, kt):
                    if k == panel_:
                        pe.wait_ge(sig.sem, sig.at(*key, kt))
                return ready

            def sums_after_first(r):
                return lambda i, k: norm_pe(r) if (i, k) == (0, 0) else None

            def y_ready(base, nk):
                def ready(k, kt):
                    if k == 0:
                        pe.wait_ge(s_yl, base - (nk - 1 - kt))
                return ready

            pe.wait_ge(s_const, 16)
            pe.wait_ge(s_x, 16)
            for j in range(KT):
                turn(("x", j), [x_in[:, t, j * P:(j + 1) * P] for t in range(NB)], (turn_v, ("x", j)))
            pe.wait_ge(s_par, 16 * len(BATCHES[0]))
            pe.wait_ge(s_par_more, 16 * sum(len(b) for b in BATCHES[1:]))
            for b in range(4):
                n = sum(c for _, c in BATCHES[b])
                turn(("par", b), [prow[0:n, b, :]], (turn_v, ("par", b)))
            norm_pe(0)
            gemm("v", xn, unroll=True, ready=by_tile(norm_v, ("lo", 0)))

            def gmlp_turns(i, k):
                if (i, k) == (0, 0):
                    pe.wait_ge(s_gw, 16)
                    for g in range(0, 8, 4):
                        turn(("w_sp", g), [w_sp[:, g + x, :] for x in range(4)], (gmlp_v, ("w_sp", g)))
                if (i, k) in ((0, 1), (1, 0)):
                    pe.wait_ge(s_free, P0["v"] + 4)
                    for j in range(4 * i, 4 * i + 4):
                        turn(("v", j), [vt[:, j * S + t * P:j * S + (t + 1) * P] for t in range(NB)], (gmlp_a, ("v", j)))

            gemm("u", xn, unroll=True, after=gmlp_turns)
            pe.wait_ge(gmlp_v.sem, gmlp_v.at("normed", NB - 1))
            for g in range(8):
                bank = take(("mix", g), (gmlp_v, ("mixed", g)))
                for c in range(NB):
                    m = pe.matmul(bank[:, c * P:(c + 1) * P], v_tok[:, c, g * P:(g + 1) * P], w_spT[:, g, :],
                                  start=True, stop=True)
                m.then_inc(full.sem, full.mark("mix", g))
            gemm("ga", xn, y, ready=by_tile(gmlp_v, ("lo",), 1))
            pe.wait_ge(s_lw, 32)
            for j in range(9):
                if j < 8:
                    n = P0["lru"] + j
                    pair("lru", j, n, n % 2, xn, xn, S)
                if j >= 1:
                    jj = j - 1
                    pe.wait_ge(lru_v.sem, lru_v.at("conv", jj))
                    for g in range(2):
                        bank = take(("ri", jj, g), (lru_a, ("ri", jj, g)))
                        pe.matmul(bank[:, :], lru_w[:, g, jj, :], lt[jj % 2], start=True, stop=True)\
                          .then_inc(full.sem, full.mark("ri", jj, g))
            gemm("gb", xn, y, ready=by_tile(lru_v, ("lo",), 1))
            gemm("xbc", xn, unroll=True)
            gemm("dt", xn)
            pe.wait_ge(s_free, P0["dt"] + 1)
            wide(True)
            ssd_pe(pe, take, turn)
            wide(False)
            def group_sums(g):
                bank = take(("zsum", g), (z_v, ("var", g)))
                for k in range(2):
                    pe.wait_ge(z_a.sem, z_a.at("square", g, k))
                    m = pe.matmul(bank[:, :], ones, tmp(k), start=k == 0, stop=k == 1)
                m.then_inc(full.sem, full.mark("zsum", g))

            gemm("z", xn, unroll=True, after=lambda i, k: group_sums(i - 1) if i and k == 0 else None)
            group_sums(3)
            gemm("gc", xn, y, ready=by_tile(z_v, ("lo",), 1))
            gemm("wo", y, ready=by_tile(split_v, ("merged",)))
            for p in range(4):
                gemm(f"up{p}", xn, ready=None if p else by_tile(norm_v, ("lo", 1)), after=None if p else sums_after_first(1))
                gemm(f"down{p}", y, ready=y_ready(BASE[f"down{p}"][2], 8))
            norm_pe(2)

            def memory(i, k):
                if (i, k) == (0, 0):
                    pe.wait_ge(s_mem, 16)
                    for j in range(0, KT, 2):
                        turn(("mem", j), [mem_in[:, t, (j + d) * P:(j + d + 1) * P] for d in range(2) for t in range(2)],
                             (turn_v, ("mem", j)))
                if (i, k) == (2, 0):
                    norm_pe(3, MEM)

            def between_panels(l, p):
                if p == 0:
                    norm_pe(5 + 5 * l)
                if p == 2:
                    pe.wait_ge(s_free, P0[f"kidx{l}"] + 1)
                    turn(("w_tok", l), [wi[:, t * P:(t + 1) * P] for t in range(NB)], (rope_v, ("w_tok", l)))
                if p in rotations:
                    kind_, t = key = rotations[p]
                    pe.wait_ge(s_free, P0[{"qi": "qidx", "ki": "kidx"}.get(kind_, kind_) + str(l)] + t // 2 + 1)
                    bank = take(("rot", l) + key, (rope_v, ("rot", l) + key))
                    pe.matmul(bank[:, :], rot, rope_tile(key), start=True, stop=True)\
                      .then_inc(full.sem, full.mark("rot", l, *key))
                if p in index_heads:
                    b, heads = index_heads[p]
                    w = (b + 1) * P
                    pe.wait_ge(rope_v.sem, rope_v.at("tile", l, "qi", 1))
                    for i in heads:
                        o = 64 * (i % 2)
                        bank = take(("idx", l, b, i), (dsa_a, ("idx", l, b, i)))
                        pe.matmul(bank[:, 0:w], cut(qi, i // 2)[o:o + 64, b * P:(b + 1) * P], ki[o:o + 64, 0:w],
                                  start=True, stop=True).then_inc(full.sem, full.mark("idx", l, b, i))

            for l in range(2):
                def ffn(f, r):
                    for part in range(3):
                        gemm(f"{f}u{l}{part}", xn, ready=None if part else by_tile(norm_v, ("lo", r)),
                             after=None if part else sums_after_first(r))
                        first = (f, l, part) == ("f1", 0, 0)
                        gemm(f"{f}d{l}{part}", y, ready=y_ready(BASE[f"{f}d{l}{part}"][2], FFN_PARTS[part]),
                             after=memory if first else None, unroll=first)
                r = 4 + 5 * l
                ffn("f1", r)

                def between(name):
                    return lambda i, k: between_panels(l, first_panel[name] + 2 * i + k)

                for name in MIX:
                    gemm(f"{name}{l}", xn, unroll=True, after=between(name),
                         ready=by_tile(norm_v, ("lo", r + 1)) if name == "kidx" else None)
                pe.wait_ge(s_free, P0[f"vv{l}"] + 2)
                wide(True)
                dsa_pe(pe, l, take, turn)
                wide(False)
                pe.wait_ge(conv_v.sem, conv_v.at("lo", l, 1))
                pe.wait_ge(split_v.sem, split_v.at("dsa", l, 3))
                gemm(f"mwo{l}", y)
                gemm(f"xq{l}", xn, ready=by_tile(norm_v, ("lo", r + 2)), after=sums_after_first(r + 2))
                gemm(f"xk{l}", y, width=MEM, ready=by_tile(norm_v, ("mem_lo", l)))
                gemm(f"xv{l}", y, width=MEM)
                pe.wait_ge(s_free, P0[f"xv{l}"] + 4)
                wide(True)
                cross_pe(pe, l, take, turn)
                wide(False)
                gemm(f"xo{l}", y, ready=by_tile(xa_v, ("lo", l)))
                ffn("f2", r + 3)
            norm_pe(14)
            pe.wait_ge(norm_v.sem, norm_v.at("xn", 14, KT - 1))
            for t in range(NB):
                for o in range(2):
                    turn(("out", t, o), [cut(h, 4 * o + j)[:, t * P:(t + 1) * P] for j in range(4)],
                         (turn_v, ("out", t, o)))


        def ssd_act(act, link):
            act.wait_ge(s_sp, 48)
            act.activation(small[0:16, 178:179], small[0:16, 177:178], ACT.Exp).then_inc(ssd_a.sem, ssd_a.mark("a"))
            act.wait_ge(ssd_v.sem, ssd_v.at("z"))
            link(act.activation(pre[2][0:16, :], pre[1][0:16, :], ACT.Abs))
            act.activation(pre[3][0:16, :], pre[2][0:16, :], ACT.Exp, scale=-1.0).then_inc(ssd_a.sem, ssd_a.mark("exp"))
            act.wait_ge(ssd_v.sem, ssd_v.at("to_end"))
            act.activation(stk[32:48, :], acs[0:16, :], ACT.Copy)
            act.activation(stk[64:80, :], pre[7][0:16, :], ACT.Exp).then_inc(ssd_a.sem, ssd_a.mark("stk"))
            act.wait_ge(full.sem, full.at("sst"))
            act.activation(sst[:, :, :], B[BANK.get(("sst",), 0)][:, :].rearrange("p (c n) -> p c n", c=NB)[:, :, 0:96], ACT.Copy)\
               .then_inc(ssd_a.sem, ssd_a.mark("sst"))
            act.wait_ge(full.sem, full.at("ends"))
            act.activation(chunk_decay[:, :, :].rearrange("p c h -> p (c h)"), B[BANK.get(("ends",), 0)][:, 0:64], ACT.Exp)\
               .then_inc(ssd_a.sem, ssd_a.mark("ends"))
            for g in range(4):
                act.wait_ge(full.sem, full.at("b_tok", g))
                if g:
                    act.wait_ge(full.sem, full.at("st", g - 1, 1))
                act.activation(b_tok[:, :, :].rearrange("p c n -> p (c n)"), B[BANK.get(("b_tok", g), 0)][:, :], ACT.Copy)\
                   .then_inc(ssd_a.sem, ssd_a.mark("b_tok", g))
                def exponentials(r):
                    act.wait_ge(full.sem, full.at("row", g, r))
                    if 4 * g + r >= 2:
                        act.wait_ge(ssd_v.sem, ssd_v.at("ce", (4 * g + r - 2) // 4, (r - 2) % 4))
                    act.activation(head_exp[r % 2], B[BANK.get(("row", g, r), 0)][:, :], ACT.Exp)\
                       .then_inc(ssd_a.sem, ssd_a.mark("row", g, r))

                exponentials(0)
                for r in range(4):
                    if r < 3:
                        exponentials(r + 1)
                    act.wait_ge(ssd_v.sem, ssd_v.at("min", g, r))
                    act.activation(head_decay[r % 2], head_decay[r % 2], ACT.Exp).then_inc(ssd_a.sem, ssd_a.mark("decay", g, r))

        def tap_product(act, l, kind_, t, k):
            if kind_ == "conf":
                src, w, acc = av[k][:, t:t + S], col("conf_dw_2", (l * CONV_TAPS + t) * 2 + k), cv[k]
                act.wait_ge(s_free, P0[f"conv{l}"] + 2)
            else:
                src, w, acc = hc[k][:, t:t + S], col("sc_dw_2", (l * 3 + t) * 2 + k), tmp(2 + k)
                act.wait_ge(conv_v.sem, conv_v.at("short_in", l))
            if (kind_, t) == ("conf", 0):
                ins = act.activation(acc, src, ACT.Identity, scale=w, bias=col("conf_dw_b_2", 2 * l + k))
            elif t == 0:
                ins = act.activation(acc, src, ACT.Copy, scale=w)
            else:
                a = adds[kind_, t, k]
                if a >= 4:
                    act.wait_ge(conv_p.sem, conv_p.at("add", l, a - 4))
                ins = act.activation(tap_buffers[a % 4], src, ACT.Copy, scale=w)
            ins.then_inc(conv_a.sem, conv_a.mark("product", l, kind_, t, k))

        def dsa_act(act, l):
            for k in range(2):
                act.wait_ge(conv_p.sem, conv_p.at("short", l, k))
                act.activation(cut(y_hi, 2 + k), tmp(2 + k), ACT.Copy).then_inc(conv_a.sem, conv_a.mark("hi", l, 2 + k))
            for i in range(-2, len(steps)):
                s = i + 1
                if 0 <= s < len(steps):
                    w = (steps[s][0] + 1) * P
                    act.wait_ge(dsa_v.sem, dsa_v.at("inverse", l, s))
                    act.activation(att_p(s)[:, 0:w], att_p(s)[:, 0:w], ACT.Copy, scale=small[:, 150 + s % 2:151 + s % 2])\
                       .then_inc(dsa_a.sem, dsa_a.mark("p", l, s))
                s = i + 2
                if s < len(steps):
                    w = (steps[s][0] + 1) * P
                    act.wait_ge(dsa_v.sem, dsa_v.at("neg", l, s))
                    act.activation(att_p(s)[:, 0:w], att_p(s)[:, 0:w], ACT.Exp, bias=small[:, 146 + s % 2:147 + s % 2],
                                   accum_out=small[:, 148 + s % 2:149 + s % 2]).then_inc(dsa_a.sem, dsa_a.mark("exp", l, s))
                s = i + 1
                if 0 <= s < len(steps):
                    w = (steps[s][0] + 1) * P
                    act.wait_ge(full.sem, full.at("p", l, s))
                    act.activation(att_pt(s)[:, 0:w], B[BANK.get(("p", l, s), 0)][:, 0:w], ACT.Copy)\
                       .then_inc(dsa_a.sem, dsa_a.mark("pt", l, s))
                if i == root_step:
                    act.wait_ge(conv_v.sem, conv_v.at("stat", l, 1))
                    act.activation(stat[:, :], stat[:, :], ACT.Sqrt).then_inc(conv_a.sem, conv_a.mark("std", l))
                if i == root_step + 1:
                    for k in range(2):
                        act.wait_ge(conv_v.sem, conv_v.at("ln", l, k))
                        act.activation(cv[k], cv[k], ACT.Silu, scale=col("conf_ln_g_2", 2 * l + k),
                                       bias=col("conf_ln_b_2", 2 * l + k)).then_inc(conv_a.sem, conv_a.mark("y", l, k))
                    act.wait_ge(conv_a.sem, conv_a.at("y", l, 1))
                    for k in range(2):
                        act.activation(cut(y_hi, k), cv[k], ACT.Copy).then_inc(conv_a.sem, conv_a.mark("hi", l, k))
            for t in range(4):
                act.wait_ge(dsa_v.sem, dsa_v.at("o", l, NB - 1, t))
                act.activation(cut(y_hi, 4 + t), cut(o_t, t), ACT.Copy).then_inc(split_a.sem, split_a.mark("dsa", l, t))

        def cross_act(act, l):
            for i in range(-2, len(cross_steps)):
                s = i + 1
                if 0 <= s < len(cross_steps):
                    act.wait_ge(xa_v.sem, xa_v.at("inverse", l, s))
                    act.activation(xp[s % 2], xp[s % 2], ACT.Copy, scale=small[:, 156 + s % 2:157 + s % 2])\
                       .then_inc(xa_a.sem, xa_a.mark("p", l, s))
                s = i + 2
                if s < len(cross_steps):
                    act.wait_ge(xa_v.sem, xa_v.at("neg", l, s))
                    if s >= 2:
                        act.wait_ge(full.sem, full.at("xp", l, s - 2))
                    act.activation(xp[s % 2], B[BANK.get(("xs", l, s), 0)][:, 0:MEM], ACT.Exp, scale=1.0 / 16.0,
                                   bias=small[:, 152 + s % 2:153 + s % 2],
                                   accum_out=small[:, 154 + s % 2:155 + s % 2]).then_inc(xa_a.sem, xa_a.mark("exp", l, s))
                s = i + 1
                if 0 <= s < len(cross_steps):
                    x, b = cross_steps[s]
                    act.wait_ge(full.sem, full.at("xp", l, s))
                    if b == 0 and x >= 2:
                        act.wait_ge(full.sem, full.at("xo", l, x - 2, 1))
                    act.activation(xpt[x % 2][:, :, b * P:(b + 1) * P],
                                   B[BANK.get(("xp", l, s), 0)][:, 0:MEM].rearrange("p (t q) -> p t q", t=2), ACT.Copy)\
                       .then_inc(xa_a.sem, xa_a.mark("pt", l, s))
                if i >= 0 and cross_steps[i][1] == NB - 1:
                    x = cross_steps[i][0]
                    for d in range(2):
                        act.wait_ge(full.sem, full.at("xo", l, x, d))
                        act.activation(cut(y_hi, 2 * x + d), B[BANK.get(("xo", l, x, d), 0)][:, :], ACT.Copy)\
                           .then_inc(xa_a.sem, xa_a.mark("hi", l, 2 * x + d))

        @block.scalar
        def _(act):
            chain = [0]

            def link(ins):
                chain[0] += 1
                ins.then_inc(s_act, 1)
                act.wait_ge(s_act, chain[0])

            def prep(n, q, landed, k):
                if isinstance(n, int) and n + 1 > last_pair:
                    return
                act.wait_ge(s_load[1 - q], landed)
                act.wait_ge(s_mm, 2 * n + (k + 1))
                act.activation(w_hi[:, k], raw[:, 1 - q, :, k * P:(k + 1) * P], ACT.Copy).then_inc(s_whi, 1)

            def product(n, k):
                act.wait_ge(s_mm, 2 * n + (k + 1))

            def evacuate(name, store, unroll=False):
                def body(i, n, q, landed):
                    for k in range(2):
                        prep(n, q, landed, k)
                        if k == 0 and (not isinstance(n, int) or n >= 1):
                            act.wait_ge(s_free, n)
                        product(n, k)
                        ins = store(i, k, G[2 * q + k])
                        if k == 1:
                            ins.then_inc(s_free, 1)
                loop_pairs(act, name, body, unroll=unroll)

            def gates(name, n_):
                def body(i, n, q, landed):
                    prep(n, q, landed, 0)
                    act.wait_ge(s_free, n - 1)
                    product(n, 0)
                    act.activation(tmp(q), G[2 * q][:, :], ACT.Sigmoid, bias=col("b_gate", i + 8 * n_))\
                       .then_inc(s_ao, 1)
                    prep(n, q, landed, 1)
                loop_pairs(act, name, body)

            def squared_relu(name, r=None):
                def body(i, n, q, landed):
                    prep(n, q, landed, 0)
                    if r is not None and isinstance(i, int) and i == 0:
                        root(r)
                    prep(n, q, landed, 1)
                    for k in range(2):
                        if k == 0:
                            act.wait_ge(s_ao, i + (BASE[name][0] + 1))
                        else:
                            act.wait_ge(s_free, n + 1)
                        act.activation(cut(y_hi, 2 * i + k), tmp(2 * q + k), ACT.Square).then_inc(s_yh, 1)
                loop_pairs(act, name, body, peel=0 if r is None else 2)

            def swiglu(name, r=None):
                def body(i, n, q, landed):
                    prep(n, q, landed, 0)
                    if r is not None and isinstance(i, int) and i == 0:
                        root(r)
                    act.wait_ge(s_ao, 2 * i + (BASE[name][0] + 1))
                    act.activation(tmp(q), tmp(q), ACT.Silu).then_inc(s_yh, 1)
                    prep(n, q, landed, 1)
                    act.wait_ge(s_ao, 2 * i + (BASE[name][0] + 2))
                    act.activation(cut(y_hi, i), tmp(2 + q), ACT.Copy).then_inc(s_yh, 1)
                loop_pairs(act, name, body, peel=0 if r is None else 2)

            def only_prep(name, more=None):
                def body(i, n, q, landed):
                    for k in range(2):
                        prep(n, q, landed, k)
                        if more:
                            more(i, k, n)
                loop_pairs(act, name, body, unroll=bool(more))

            def root(r, n=S):
                act.wait_ge(norm_v.sem, norm_v.at("var", r))
                act.activation(stat[:, 0:n], stat[:, 0:n], ACT.Sqrt).then_inc(norm_a.sem, norm_a.mark("std", r))

            def norm_tile(r, j, gain=None, g0=0):
                if gain:
                    act.activation(cut(xn_hi, j), cut(h, j), ACT.Copy, scale=col(gain, g0 + j))\
                       .then_inc(norm_a.sem, norm_a.mark("hi", r, j))
                if j >= 3:
                    act.wait_ge(norm_v.sem, norm_v.at("summed", r, j - 2))
                act.activation(tmp(j % 2) if j else stat[:, :], cut(h, j), ACT.Square)\
                   .then_inc(norm_a.sem, norm_a.mark("square", r, j))

            def follow(name, r, gain=None, g0=0):
                def more(i, k, n):
                    if k == 0:
                        act.wait_ge(norm_v.sem, norm_v.at("h", r, 2 * i))
                    else:
                        act.wait_ge(s_free, n + 1)
                    norm_tile(r, 2 * i + k, gain, g0)
                only_prep(name, more)

            def gelu(dst):
                return lambda i, k, bank: act.activation(cut(dst, 2 * i + k), bank[:, :], ACT.Gelu_apprx_tanh)

            def copy_to(dst, width=S):
                return lambda i, k, bank: act.activation(cut(dst, 2 * i + k, width), bank[:, 0:width], ACT.Copy)

            for b in range(1, 4):
                load_params(act, b)
            for k in range(2):
                act.wait_ge(s_load[0], LANDED[0])
                act.activation(w_hi[:, k], raw[:, 0, :, k * P:(k + 1) * P], ACT.Copy).then_inc(s_whi, 1)
            for j in range(KT):
                act.wait_ge(turn_v.sem, turn_v.at("x", j))
                norm_tile(0, j)
            root(0)
            for j in range(KT):
                act.wait_ge(norm_v.sem, norm_v.at("xn", 0, j))
                act.activation(cut(xn_hi, j), tmp(2 + j % 2), ACT.Copy).then_inc(norm_a.sem, norm_a.mark("hi", 0, j))

            evacuate("v", gelu(vt), unroll=True)
            for i in range(4):
                n = P0["u"] + i
                for k in range(2):
                    prep(n, n % 2, LANDED[n + 1], k)
                    if k == 0:
                        act.wait_ge(s_free, n)
                    product(n, k)
                    ins = act.activation(cut(u, 2 * i + k), G[2 * (n % 2) + k][:, :], ACT.Gelu_apprx_tanh)
                    if k == 1:
                        ins.then_inc(s_free, 1)
                    if (i, k) in ((0, 1), (1, 0)):
                        for j in range(4 * i, 4 * i + 4):
                            act.wait_ge(full.sem, full.at("v", j))
                            act.activation(v_tok[:, :, j * P:(j + 1) * P],
                                           B[BANK.get(("v", j), 0)][:, :].rearrange("p (t f) -> p t f", t=NB),
                                           ACT.Copy).then_inc(gmlp_a.sem, gmlp_a.mark("v", j))
                    if (i, k) == (2, 0):
                        act.wait_ge(gmlp_v.sem, gmlp_v.at("var"))
                        act.activation(small[:, 0:4], small[:, 0:4], ACT.Sqrt).then_inc(gmlp_a.sem, gmlp_a.mark("std"))
            for g in range(8):
                act.wait_ge(gmlp_v.sem, gmlp_v.at("y", g))
                act.activation(cut(y_hi, g), tmp(4 + g % 2), ACT.Copy).then_inc(gmlp_a.sem, gmlp_a.mark("hi", g))
            gates("ga", 0)

            act.activation(small[:, 16:24], par[:, COL["lru_lambda"]:COL["lru_lambda"] + 8], ACT.Abs)\
               .then_inc(lru_a.sem, lru_a.mark("abs"))
            act.wait_ge(lru_a.sem, lru_a.at("abs"))
            act.activation(small[:, 16:24], small[:, 16:24], ACT.Exp, scale=-1.0)\
               .then_inc(lru_a.sem, lru_a.mark("exp"))
            for j in range(9):
                if j < 8:
                    n = P0["lru"] + j
                    q = n % 2
                    prep(n, q, LANDED[n + 1], 0)
                    product(n, 0)
                    act.wait_ge(s_free, n)
                    if j >= 2:
                        act.wait_ge(lru_v.sem, lru_v.at("conv", j - 2))
                    else:
                        act.wait_ge(lru_v.sem, lru_v.at("pads"))
                    act.activation(xpad[q][:, 3:3 + S], G[2 * q][:, :], ACT.Copy).then_inc(lru_a.sem, lru_a.mark("x", j))
                    prep(n, q, LANDED[n + 1], 1)
                    product(n, 1)
                    if j >= 2:
                        act.wait_ge(lru_v.sem, lru_v.at("y", j - 2))
                    act.activation(lt[2 + j % 2], G[2 * q + 1][:, :], ACT.Gelu_apprx_tanh).then_inc(s_free, 1)
                if j >= 1:
                    jj = j - 1
                    if jj >= 1:
                        act.wait_ge(lru_v.sem, lru_v.at("inp", jj - 1))
                    for g in range(2):
                        act.wait_ge(full.sem, full.at("ri", jj, g))
                        act.activation(lt[4 + g], B[BANK.get(("ri", jj, g), 0)][:, :], ACT.Sigmoid,
                                       bias=col(("lru_b_r", "lru_b_i")[g], jj)).then_inc(lru_a.sem, lru_a.mark("ri", jj, g))
                    act.wait_ge(lru_a.sem, lru_a.at("ri", jj, 0))
                    act.wait_ge(lru_v.sem, lru_v.at("rate"))
                    act.activation(lt[6], lt[4], ACT.Tanh, scale=small[:, 24 + jj:25 + jj])\
                       .then_inc(lru_a.sem, lru_a.mark("tanh", jj))
                    act.wait_ge(lru_a.sem, lru_a.at("tanh", jj))
                    act.activation(lt[7], lt[6], ACT.Sqrt).then_inc(lru_a.sem, lru_a.mark("sqrt", jj))
                    act.wait_ge(lru_v.sem, lru_v.at("y", jj))
                    act.activation(cut(y_hi, jj), lt[12], ACT.Copy).then_inc(lru_a.sem, lru_a.mark("hi", jj))
            gates("gb", 1)

            for i in range(NPAIR["xbc"]):
                n = P0["xbc"] + i
                q = n % 2
                for k in range(2):
                    j = 2 * i + k
                    prep(n, q, LANDED[n + 1], k)
                    product(n, k)
                    if k == 0:
                        act.wait_ge(s_free, n)
                    act.wait_ge(xbc_v.sem, xbc_v.at("pads") if j < 4 else xbc_v.at("conv", j - 4))
                    ins = act.activation(cpad[j % 4][:, 3:3 + S], G[2 * q + k][:, :], ACT.Copy)
                    if k == 1:
                        ins.then_inc(s_free, 1)
                    else:
                        ins.then_inc(xbc_a.sem, xbc_a.mark("x", j))
                for k in range(2):
                    j = 2 * i + k
                    act.wait_ge(xbc_v.sem, xbc_v.at("conv", j))
                    act.activation(cut(xbc, j), cacc[k], ACT.Silu).then_inc(xbc_a.sem, xbc_a.mark("silu", j))
            only_prep("dt")
            ssd_act(act, link)
            def group_squares(g):
                for k in range(2):
                    act.wait_ge(z_v.sem, z_v.at("gated", 2 * g + k))
                    if g >= 1:
                        act.wait_ge(full.sem, full.at("zsum", g - 1))
                    act.activation(tmp(k), cut(xbc, 2 * g + k), ACT.Square).then_inc(z_a.sem, z_a.mark("square", g, k))

            def group_root(g):
                act.wait_ge(z_v.sem, z_v.at("var", g))
                act.activation(stat[:, :], stat[:, :], ACT.Sqrt).then_inc(z_a.sem, z_a.mark("std", g))

            def group_norm(g):
                for k in range(2):
                    act.wait_ge(z_v.sem, z_v.at("y", 2 * g + k))
                    act.activation(cut(y_hi, 2 * g + k), tmp(4 + k), ACT.Copy).then_inc(z_a.sem, z_a.mark("hi", 2 * g + k))

            for i in range(NPAIR["z"]):
                n = P0["z"] + i
                q = n % 2
                for k in range(2):
                    prep(n, q, LANDED[n + 1], k)
                    if i and k == 0:
                        group_squares(i - 1)
                    product(n, k)
                    if k == 0:
                        act.wait_ge(s_free, n)
                    if i >= 1:
                        act.wait_ge(z_v.sem, z_v.at("gated", 2 * i - 2 + k))
                    elif k == 0:
                        act.wait_ge(ssd_v.sem, ssd_v.at("y", 3, 1))
                    ins = act.activation(tmp(2 + k), G[2 * q + k][:, :], ACT.Silu)
                    if k == 1:
                        ins.then_inc(s_free, 1)
                    else:
                        ins.then_inc(z_a.sem, z_a.mark("silu", 2 * i))
                    if i and k == 0:
                        group_root(i - 1)
                if i:
                    group_norm(i - 1)
            group_squares(3)
            group_root(3)
            group_norm(3)
            gates("gc", 2)
            act.wait_ge(s_free, P0["wo"])
            for j in range(KT):
                act.activation(cut(y_hi, j), cut(merged, j), ACT.Copy).then_inc(split_a.sem, split_a.mark("merged", j))
            follow("wo", 1, "norm_mlp_g")
            for p in range(4):
                squared_relu(f"up{p}", None if p else 1)
                if p < 3:
                    only_prep(f"down{p}")
            follow("down3", 2)
            root(2)

            def memory(i, k, n):
                if (i, k) == (1, 0):
                    act.wait_ge(turn_v.sem, turn_v.at("mem", 6))
                    act.activation(temps[:, 0:KT * MEM], mem_t, ACT.Square).then_inc(norm_a.sem, norm_a.mark("square", 3))
                if (i, k) == (2, 0):
                    root(3, MEM)

            def sines(i, k, n):
                if k == 1 and i < 2:
                    act.wait_ge(trig_v.sem, trig_v.at("angle", i))
                    act.activation(sincos[:, i, :], ang[2 + i], ACT.Sin).then_inc(trig_a.sem, trig_a.mark(i))
            for l in range(2):
                def ffn(f, r):
                    if (f, l) == ("f1", 0):
                        for j in range(KT):
                            act.wait_ge(norm_v.sem, norm_v.at("xn", 2, j))
                            norm_tile(r, j, "ffn1_norm_2")
                    for part in range(3):
                        swiglu(f"{f}u{l}{part}", None if part else r)
                        if part < 2:
                            only_prep(f"{f}d{l}{part}", (memory, sines)[part] if (f, l) == ("f1", 0) else None)
                        elif (f, l) == ("f1", 0) or f == "f1":
                            follow(f"{f}d{l}{part}", r + 1, "mix_norm_2", 8 * l)
                        elif l == 0:
                            follow(f"{f}d{l}{part}", 9, "ffn1_norm_2", 8)
                        else:
                            follow(f"{f}d{l}{part}", 14)
                r = 4 + 5 * l
                ffn("f1", r)
                mix = [(name, i, k) for name in MIX for i in range(NPAIR[name + "0"]) for k in range(2)]
                for p, (name, i, k) in enumerate(mix):
                    n = P0[f"{name}{l}"] + i
                    prep(n, n % 2, LANDED[n + 1], k)
                    if p == 0:
                        root(r + 1)
                    if name == "conv" and i == 1:
                        act.wait_ge(conv_v.sem, conv_v.at("gate", l, k))
                        act.activation(tmp(4 + k), tmp(4 + k), ACT.Sigmoid).then_inc(conv_a.sem, conv_a.mark("gate", l, k))
                    if name in ("qidx", "q", "k"):
                        if k == 0:
                            act.wait_ge(s_free, n)
                        product(n, k)
                        dst = cut(qi if name == "qidx" else qkv, 2 * i + k + (4 if name == "k" else 0))
                        ins = act.activation(dst, G[2 * (n % 2) + k][:, :], ACT.Copy)
                        if k == 1:
                            ins.then_inc(s_free, 1)
                    if p in index_heads:
                        b, heads = index_heads[p]
                        w = (b + 1) * P
                        for x in heads:
                            act.wait_ge(full.sem, full.at("idx", l, b, x))
                            if x >= 2 or b >= 2:
                                act.wait_ge(dsa_v.sem, dsa_v.at("idx", l, *((b, x - 2) if x >= 2 else (b - 1, x + 2))))
                            act.activation(relus[x % 2][:, 0:w], B[BANK.get(("idx", l, b, x), 0)][:, 0:w], ACT.Relu,
                                           scale=IDX_SCALE).then_inc(dsa_a.sem, dsa_a.mark("idx", l, b, x))
                    if p >= first_products:
                        n0 = (p - first_products) * PRODUCTS_EACH
                        for x in products[n0:n0 + PRODUCTS_EACH]:
                            tap_product(act, l, *x)
                dsa_act(act, l)
                follow(f"mwo{l}", r + 2, "xa_norm_2", 8 * l)

                def queries(i, k, n):
                    if (i, k) == (0, 0):
                        root(r + 2)
                    if i in (1, 2):
                        for j in range(4 * i + 2 * k - 4, 4 * i + 2 * k - 2):
                            act.activation(cut(y_hi, j)[:, 0:MEM], cut(memn, j, MEM), ACT.Copy, scale=col("mem_norm_2", 8 * l + j))\
                               .then_inc(norm_a.sem, norm_a.mark("mem_hi", l, j))
                only_prep(f"xq{l}", queries)
                evacuate(f"xk{l}", copy_to(xk, MEM))
                evacuate(f"xv{l}", copy_to(xvt, MEM))
                cross_act(act, l)
                follow(f"xo{l}", r + 3, "ffn2_norm_2", 8 * l)
                ffn("f2", r + 3)
            root(14)


        def ssd_dve(dve, link, log1p):
            n = P0["dt"]
            z, relu, e, acc, a, b = (pre[i][0:16, :] for i in (1, 4, 3, 5, 6, 7))
            link(dve.memset(stk, 0.0))
            dve.wait_ge(s_sp, 48)
            for r in range(2):
                link(dve.tensor_copy(small[64 * r:64 * r + 64, 184:192], small[64 * r:64 * r + 64, 200 + r:216:2]))
            dve.wait_ge(s_free, n)
            dve.wait_ge(s_mm, 2 * n + 2)
            dve.tensor_scalar(z, G[2 * (n % 2)][0:16, :], small[0:16, 176:177], None, ALU.add).then_inc(s_free, 1)
            dve.wait_ge(s_free, n + 1)
            dve.tensor_scalar(relu, z, 0.0, None, ALU.max).then_inc(ssd_v.sem, ssd_v.mark("z"))
            dve.wait_ge(ssd_a.sem, ssd_a.at("exp"))
            log1p(acc, e, a, b)
            link(dve.scalar_tensor_tensor(stk[0:16, :], acc, 2.0, relu, ALU.mult, ALU.add))
            link(dve.tensor_scalar(a, stk[0:16, :], small[0:16, 178:179], -1.0, ALU.mult, ALU.mult))
            for c in range(NB):
                cs = slice(c * P, (c + 1) * P)
                ins = dve.tensor_tensor_scan(acs[0:16, cs], ones[0:16, :], a[:, cs], 0.0, ALU.mult, ALU.add)
            link(ins)
            ends = acs[0:16, P - 1:S:P]
            dve.tensor_tensor(small[0:16, 32:96].rearrange("p (c h) -> p c h", c=NB),
                              ident[0:16, None, 0:16].to_broadcast([16, NB, 16]),
                              ends[:, :, None].to_broadcast([16, NB, 16]), ALU.mult).then_inc(ssd_v.sem, ssd_v.mark("ends"))
            for c in range(NB):
                ins = dve.tensor_scalar(b[:, c * P:(c + 1) * P], acs[0:16, c * P:(c + 1) * P],
                                        acs[0:16, (c + 1) * P - 1:(c + 1) * P], -1.0, ALU.subtract, ALU.mult)
            ins.then_inc(ssd_v.sem, ssd_v.mark("to_end"))
            dve.wait_ge(ssd_a.sem, ssd_a.at("sst"))

            def by_head(part, g, k):
                h0 = part + 4 * g + 2 * k
                return sst[:, :, h0:h0 + 2][:, :, :, None].to_broadcast([P, NB, 2, 64])

            for g in range(4):
                for k in range(2):
                    dve.wait_ge(full.sem, full.at("x_tok", g, k))
                    dve.tensor_tensor(xdt[:, :, k * P:(k + 1) * P].rearrange("p c (r d) -> p c r d", r=2),
                                      B[BANK.get(("x_tok", g, k), 0)][:, :].rearrange("p (c r d) -> p c r d", c=NB, r=2),
                                      by_head(0, g, k), ALU.mult).then_inc(ssd_v.sem, ssd_v.mark("xdt", g, k))
                dve.wait_ge(ssd_v.sem, ssd_v.at("xdt", g, 1))
                for k in range(2):
                    ins = dve.tensor_tensor(xdd[:, :, k * P:(k + 1) * P].rearrange("p c (r d) -> p c r d", r=2),
                                            xdt[:, :, k * P:(k + 1) * P].rearrange("p c (r d) -> p c r d", r=2),
                                            by_head(64, g, k), ALU.mult)
                ins.then_inc(ssd_v.sem, ssd_v.mark("xdd", g))
                dve.wait_ge(full.sem, full.at("cb", g))
                dve.tensor_tensor(cb[:, :, :], B[BANK.get(("cb", g), 0)][:, :].rearrange("p (c l) -> p c l", c=NB),
                                  causal[:, None, :].to_broadcast([P, NB, P]), ALU.mult)\
                   .then_inc(ssd_v.sem, ssd_v.mark("cb", g))
                dve.wait_ge(ssd_a.sem, ssd_a.at("ends"))
                dve.wait_ge(full.sem, full.at("st", g, 0))
                b0 = B[BANK.get(("st", g, 0), 0)]
                link(dve.tensor_copy(st[:, 0, :], b0[:, 0:256]))
                decay = lambda c: chunk_decay[:, c, 4 * g:4 * g + 4][:, :, None].to_broadcast([P, 4, 64])
                heads = lambda x: x.rearrange("p (r d) -> p r d", r=4)
                link(dve.tensor_tensor(heads(st[:, 1, :]), heads(st[:, 0, :]), decay(1), ALU.mult))
                dve.tensor_tensor(st[:, 1, :], st[:, 1, :], b0[:, 256:512], ALU.add).then_inc(ssd_v.sem, ssd_v.mark("st", g, 0))
                dve.wait_ge(ssd_v.sem, ssd_v.at("st", g, 0))
                link(dve.tensor_tensor(heads(st[:, 2, :]), heads(st[:, 1, :]), decay(2), ALU.mult))
                dve.wait_ge(full.sem, full.at("st", g, 1))
                dve.tensor_tensor(st[:, 2, :], st[:, 2, :], B[BANK.get(("st", g, 1), 0)][:, 0:256], ALU.add)\
                   .then_inc(ssd_v.sem, ssd_v.mark("st", g, 1))
                def differences(r):
                    hh = 4 * g + r
                    before = ((hh - 2) // 4, (hh - 2) % 4)
                    d = head_decay[r % 2]
                    dve.wait_ge(ssd_a.sem, ssd_a.at("row", g, r))
                    if hh >= 2:
                        dve.wait_ge(ssd_v.sem, ssd_v.at("m", *before))
                    dve.tensor_tensor(d.rearrange("p (c l) -> p c l", c=NB),
                                      B[BANK.get(("row", g, r), 0)][:, :].rearrange("p (c l) -> p c l", c=NB),
                                      sst[:, :, 32 + hh:33 + hh].to_broadcast([P, NB, P]), ALU.subtract)\
                       .then_inc(ssd_v.sem, ssd_v.mark("seg", g, r))
                    dve.wait_ge(ssd_v.sem, ssd_v.at("seg", g, r))
                    dve.tensor_scalar(d, d, 0.0, None, ALU.min).then_inc(ssd_v.sem, ssd_v.mark("min", g, r))
                    if hh >= 2:
                        dve.wait_ge(full.sem, full.at("y", *before))
                    dve.tensor_tensor(head_ce[r % 2], cut(xbc, 12 + g), head_exp[r % 2], ALU.mult)\
                       .then_inc(ssd_v.sem, ssd_v.mark("ce", g, r))

                differences(0)
                for r in range(4):
                    if r < 3:
                        differences(r + 1)
                    dve.wait_ge(ssd_a.sem, ssd_a.at("decay", g, r))
                    dve.tensor_tensor(head_m[r % 2], head_decay[r % 2], cb[:, :, :].rearrange("p c l -> p (c l)"), ALU.mult)\
                       .then_inc(ssd_v.sem, ssd_v.mark("m", g, r))
                    if r == 2:
                        skip(dve, g, 0)
                skip(dve, g, 1)

        def skip(dve, g, k):
            dve.wait_ge(full.sem, full.at("y", g, 2 * k + 1))
            x = cut(xbc, 2 * g + k)
            dve.scalar_tensor_tensor(x, x, small[:, 184 + 2 * g + k:185 + 2 * g + k], B[BANK.get(("y", g, k), 0)][:, :],
                                     ALU.mult, ALU.add).then_inc(ssd_v.sem, ssd_v.mark("y", g, k))

        def rope(dve, link, l, key, at_):
            x = rope_tile(key)
            dve.wait_ge(full.sem, full.at("rot", l, *key))
            dve.tensor_tensor(relus[at_ % 2], B[BANK.get(("rot", l) + key, 0)][:, :], sincos_r[:, 1, :], ALU.mult)\
               .then_inc(rope_v.sem, rope_v.mark("rot", l, *key))
            link(dve.tensor_tensor(x, x, sincos_r[:, 0, :], ALU.mult))
            dve.tensor_tensor(x, x, relus[at_ % 2], ALU.add).then_inc(rope_v.sem, rope_v.mark("tile", l, *key))
            dve.wait_ge(rope_v.sem, rope_v.at("tile", l, *key))

        def index_scores(dve, link, l, b, heads):
            w = (b + 1) * P
            for i in heads:
                dve.wait_ge(dsa_a.sem, dsa_a.at("idx", l, b, i))
                if i == 0:
                    ins = dve.tensor_scalar(score[:, 0:w], relus[0][:, 0:w], w_tok[:, b, 0:1], None, ALU.mult)
                else:
                    ins = dve.scalar_tensor_tensor(score[:, 0:w], relus[i % 2][:, 0:w], w_tok[:, b, i:i + 1], score[:, 0:w],
                                                   ALU.mult, ALU.add)
                ins.then_inc(dsa_v.sem, dsa_v.mark("idx", l, b, i))
                dve.wait_ge(dsa_v.sem, dsa_v.at("idx", l, b, i))
            if heads[-1] == IDXH - 1:
                diagonal = score[:, b * P:(b + 1) * P]
                link(dve.tensor_tensor(diagonal, diagonal, qcausal, ALU.add))

        def select(dve, link, b, rounds):
            w = (b + 1) * P
            for n in rounds:
                src = work if n else score
                link(dve.max(small[:, 160:168], src[:, 0:w]))
                link(dve.match_replace(work[:, 0:w], small[:, 160:168], src[:, 0:w], TAKEN))
                if n == TOPK // 8 - 1:
                    link(dve.tensor_scalar(bias[b], work[:, 0:w], TAKEN, NEG, ALU.is_gt, ALU.mult))

        def dsa_dve(dve, link, l, lo_of):
            for k in range(2):
                dve.wait_ge(conv_p.sem, conv_p.at("short", l, k))
            for t in range(4):
                dve.wait_ge(full.sem, full.at("v_key", l, t))
                dve.tensor_copy(v_key[:, :, t * P:(t + 1) * P], B[BANK.get(("v_key", l, t), 0)][:, :].rearrange("p (b f) -> p b f", b=NB))\
                   .then_inc(rope_v.sem, rope_v.mark("v_key", l, t))

            def mean():
                dve.wait_ge(full.sem, full.at("cln", l, 0))
                dve.tensor_scalar(stat[:, :], B[BANK.get(("cln", l, 0), 0)][:, :], 1.0 / 256, None, ALU.mult)\
                   .then_inc(conv_v.sem, conv_v.mark("stat", l, 0))
                dve.wait_ge(conv_v.sem, conv_v.at("stat", l, 0))
                for k in range(2):
                    link(dve.tensor_tensor(cv[k], cv[k], stat[:, :], ALU.subtract))
                    dve.tensor_tensor(tmp(4 + k), cv[k], cv[k], ALU.mult).then_inc(conv_v.sem, conv_v.mark("summand", l, 1, k))
                for k in range(2):
                    dve.wait_ge(conv_a.sem, conv_a.at("hi", l, 2 + k))
                    lo_of(cut(y_lo, 2 + k), tmp(2 + k), cut(y_hi, 2 + k)).then_inc(conv_v.sem, conv_v.mark("short_lo", l, k))

            def maximum(s):
                b, hh = steps[s]
                w = (b + 1) * P
                m = small[:, 144 + s % 2:145 + s % 2]
                dve.wait_ge(full.sem, full.at("s", l, s))
                if s >= 2:
                    dve.wait_ge(full.sem, full.at("p", l, s - 2))
                dve.tensor_tensor_reduce(att_p(s)[:, 0:w], B[BANK.get(("s", l, s), 0)][:, 0:w],
                                         bias[b][:, 0:w],
                                         0.125, -3.0e38, ALU.add, ALU.max, m).then_inc(dsa_v.sem, dsa_v.mark("s", l, s))
                dve.wait_ge(dsa_v.sem, dsa_v.at("s", l, s))
                dve.tensor_scalar(small[:, 146 + s % 2:147 + s % 2], m, -1.0, None, ALU.mult)\
                   .then_inc(dsa_v.sem, dsa_v.mark("neg", l, s))

            for i in range(-2, len(steps)):
                if 0 <= i + 1 < len(steps):
                    s = i + 1
                    dve.wait_ge(dsa_a.sem, dsa_a.at("exp", l, s))
                    dve.reciprocal(small[:, 150 + s % 2:151 + s % 2], small[:, 148 + s % 2:149 + s % 2])\
                       .then_inc(dsa_v.sem, dsa_v.mark("inverse", l, s))
                if i + 2 < len(steps):
                    maximum(i + 2)
                if i >= 1 and i % 2 == 0:
                    gather(dve, l, i - 2)
                if i == mean_step + 1:
                    mean()
                if i == square_step + 1:
                    dve.wait_ge(full.sem, full.at("cln", l, 1))
                    dve.tensor_scalar(stat[:, :], B[BANK.get(("cln", l, 1), 0)][:, :], 1.0 / 256, LN_EPS_2, ALU.mult, ALU.add)\
                       .then_inc(conv_v.sem, conv_v.mark("stat", l, 1))
                if i == root_step:
                    dve.wait_ge(conv_a.sem, conv_a.at("std", l))
                    link(dve.reciprocal(rstd[:, :], stat[:, :]))
                    for k in range(2):
                        dve.tensor_tensor(cv[k], cv[k], rstd[:, :], ALU.mult).then_inc(conv_v.sem, conv_v.mark("ln", l, k))
                if i == root_step + 2:
                    for k in range(2):
                        dve.wait_ge(conv_a.sem, conv_a.at("hi", l, k))
                        lo_of(cut(y_lo, k), cv[k], cut(y_hi, k)).then_inc(conv_v.sem, conv_v.mark("lo", l, k))
            gather(dve, l, len(steps) - 2)
            for t in range(4):
                dve.wait_ge(split_a.sem, split_a.at("dsa", l, t))
                lo_of(cut(y_lo, 4 + t), cut(o_t, t), cut(y_hi, 4 + t)).then_inc(split_v.sem, split_v.mark("dsa", l, t))

        def gather(dve, l, s):
            b, hh = steps[s]
            dve.wait_ge(full.sem, full.at("o", l, b, hh + 1))
            dve.tensor_copy(cut(o_t, hh // 2)[:, b * P:(b + 1) * P], B[BANK.get(("o", l, b, hh // 2), 0)][:, 0:P])\
               .then_inc(dsa_v.sem, dsa_v.mark("o", l, b, hh // 2))

        def cross_dve(dve, link, l, lo_of):
            for j in range(0, KT, 2):
                dve.wait_ge(full.sem, full.at("xv", l, j))
                dve.tensor_copy(xv[:, :, j * P:(j + 2) * P].rearrange("p t (d f) -> p d t f", d=2),
                                B[BANK.get(("xv", l, j), 0)][:, :].rearrange("p (d t f) -> p d t f", d=2, t=2))\
                   .then_inc(xa_v.sem, xa_v.mark("xv", l, j))

            def maximum(s):
                m = small[:, 168 + s % 2:169 + s % 2]
                dve.wait_ge(full.sem, full.at("xs", l, s))
                link(dve.tensor_reduce(m, B[BANK.get(("xs", l, s), 0)][:, 0:MEM], AX.X, ALU.max))
                dve.tensor_scalar(small[:, 152 + s % 2:153 + s % 2], m, -1.0 / 16.0, None, ALU.mult)\
                   .then_inc(xa_v.sem, xa_v.mark("neg", l, s))

            for i in range(-2, len(cross_steps)):
                s = i + 1
                if 0 <= s < len(cross_steps):
                    dve.wait_ge(xa_a.sem, xa_a.at("exp", l, s))
                    dve.reciprocal(small[:, 156 + s % 2:157 + s % 2], small[:, 154 + s % 2:155 + s % 2])\
                       .then_inc(xa_v.sem, xa_v.mark("inverse", l, s))
                if i + 2 < len(cross_steps):
                    maximum(i + 2)
                if i >= 0 and cross_steps[i][1] == NB - 1:
                    x = cross_steps[i][0]
                    for d in range(2):
                        dve.wait_ge(xa_a.sem, xa_a.at("hi", l, 2 * x + d))
                        lo_of(cut(y_lo, 2 * x + d), B[BANK.get(("xo", l, x, d), 0)][:, :], cut(y_hi, 2 * x + d))\
                            .then_inc(xa_v.sem, xa_v.mark("lo", l, 2 * x + d))

        @block.vector
        def _(dve):
            count = {"n": 0, "more": 0}

            def link(ins):
                count["n"] += 1
                ins.then_inc(s_dve, 1)
                dve.wait_ge(s_dve, count["more"] + count["n"])

            def chained(name, body, per_pair, unroll, peel=0, extra=0):
                base = count["n"]

                def wrapped(i, n, q, landed):
                    first = isinstance(i, int) and i == 0
                    count["n"] = 0
                    count["more"] = i * per_pair + (base if first else base + extra)
                    body(i, n, q, landed)
                    assert count["n"] == per_pair + (extra if first else 0)
                loop_pairs(dve, name, wrapped, unroll=unroll, peel=peel)
                count["n"], count["more"] = base + per_pair * NPAIR[name] + extra, 0

            def prep_lo(n, q, k):
                if isinstance(n, int) and n + 1 > last_pair:
                    return
                dve.wait_ge(s_whi, 2 * n + (k + 3))
                dve.tensor_tensor(w_lo[:, k], raw[:, 1 - q, :, k * P:(k + 1) * P], w_hi[:, k].bitcast(F32), ALU.subtract)\
                   .then_inc(s_wlo, 1)

            def only_prep(name, extra=None):
                def body(i, n, q, landed):
                    for k in range(2):
                        prep_lo(n, q, k)
                        if extra:
                            extra(2 * i + k)
                loop_pairs(dve, name, body, unroll=bool(extra) or P0[name] < 2)

            def product(n, k):
                dve.wait_ge(s_mm, 2 * n + (k + 1))

            def lo_of(dst, value, hi):
                return dve.tensor_tensor(dst, value, hi.bitcast(F32), ALU.subtract)

            def residual(name, scale=1.0, more=None):
                def body(i, n, q, landed):
                    for k in range(2):
                        prep_lo(n, q, k)
                        if k == 0:
                            dve.wait_ge(s_free, n)
                        product(n, k)
                        ins = dve.scalar_tensor_tensor(cut(h, 2 * i + k), G[2 * q + k][:, :], scale, cut(h, 2 * i + k),
                                                       ALU.mult, ALU.add)
                        if k == 1:
                            ins.then_inc(s_free, 1)
                        if more:
                            more(i, k)
                loop_pairs(dve, name, body, unroll=bool(more))

            def gates(name, n_):
                def body(i, n, q, landed):
                    prep_lo(n, q, 0)
                    prep_lo(n, q, 1)
                    dve.wait_ge(s_free, n)
                    product(n, 1)
                    dve.wait_ge(s_ao, i + (BASE[name][0] + 1))
                    if n_ == 0:
                        dve.tensor_tensor(cut(merged, i), G[2 * q + 1][:, :], tmp(q), ALU.mult).then_inc(s_free, 1)
                    else:
                        link(dve.tensor_tensor(tmp(4 + q), G[2 * q + 1][:, :], tmp(q), ALU.mult))
                        dve.tensor_tensor(cut(merged, i), cut(merged, i), tmp(4 + q), ALU.add).then_inc(s_free, 1)
                chained(name, body, 0 if n_ == 0 else 1, False)

            def follow(name, scale, r, gain=None, g0=0):
                def body(i, n, q, landed):
                    for k in range(2):
                        prep_lo(n, q, k)
                        if k == 0:
                            dve.wait_ge(s_free, n)
                        product(n, k)
                        j = 2 * i + k
                        ins = dve.scalar_tensor_tensor(cut(h, j), G[2 * q + k][:, :], scale, cut(h, j), ALU.mult, ALU.add)
                        if k == 1:
                            ins.then_inc(s_free, 1)
                        else:
                            ins.then_inc(norm_v.sem, norm_v.mark("h", r, j))
                        if j:
                            norm_tile(r, j - 1, gain, g0)
                    if i == 3:
                        dve.wait_ge(s_free, n + 1)
                        norm_tile(r, KT - 1, gain, g0)
                loop_pairs(dve, name, body, unroll=True)

            def norm_tile(r, j, gain=None, g0=0):
                if gain:
                    dve.wait_ge(norm_a.sem, norm_a.at("hi", r, j))
                    dve.scalar_tensor_tensor(cut(xn_lo, j), cut(h, j), col(gain, g0 + j), cut(xn_hi, j).bitcast(F32),
                                             ALU.mult, ALU.subtract).then_inc(norm_v.sem, norm_v.mark("lo", r, j))
                if j:
                    if j > 1:
                        dve.wait_ge(norm_v.sem, norm_v.at("summed", r, j - 1))
                    dve.wait_ge(norm_a.sem, norm_a.at("square", r, j))
                    dve.tensor_tensor(stat[:, :], stat[:, :], tmp(j % 2), ALU.add)\
                       .then_inc(norm_v.sem, norm_v.mark("summed", r, j))

            def norm_var(r, n=S):
                dve.wait_ge(full.sem, full.at("norm", r))
                dve.tensor_scalar(stat[:, 0:n], B[BANK.get(("norm", r), 0)][:, 0:n], 1.0 / D, EPS, ALU.mult, ALU.add)\
                   .then_inc(norm_v.sem, norm_v.mark("var", r))

            def norm_rstd(r, n=S, dst=rstd):
                dve.wait_ge(norm_a.sem, norm_a.at("std", r))
                link(dve.reciprocal(dst[:, 0:n], stat[:, 0:n]))

            def squared_relu(name, r=None):
                def body(i, n, q, landed):
                    first = r is not None and isinstance(i, int) and i == 0
                    if first:
                        norm_var(r)
                    prep_lo(n, q, 0)
                    if first:
                        norm_rstd(r)
                    prep_lo(n, q, 1)
                    dve.wait_ge(s_free, n)
                    dve.wait_ge(s_wlo, 2 * n + 3)
                    for k in range(2):
                        product(n, k)
                        dve.scalar_tensor_tensor(tmp(2 * q + k), G[2 * q + k][:, :], 0.0, rstd[:, :], ALU.max, ALU.mult)\
                           .then_inc(s_free if k else s_ao, 1)
                    for k in range(2):
                        if k == 0:
                            dve.wait_ge(s_ao, i + (BASE[name][0] + 1))
                        else:
                            dve.wait_ge(s_free, n + 1)
                        ins = dve.tensor_tensor(tmp(4 + k), tmp(2 * q + k), tmp(2 * q + k), ALU.mult)
                    squares(ins)
                    for k in range(2):
                        dve.wait_ge(s_yh, 2 * i + (BASE[name][1] + k + 1))
                        lo_of(cut(y_lo, 2 * i + k), tmp(4 + k), cut(y_hi, 2 * i + k)).then_inc(s_yl, 1)

                def squares(ins):
                    link(ins)
                chained(name, body, 1, False, peel=0 if r is None else 2, extra=0 if r is None else 1)

            def swiglu(name, r=None):
                def body(i, n, q, landed):
                    first = r is not None and isinstance(i, int) and i == 0
                    if first:
                        norm_var(r)
                    prep_lo(n, q, 0)
                    if first:
                        norm_rstd(r)
                    dve.wait_ge(s_free, n)
                    product(n, 0)
                    dve.wait_ge(s_wlo, 2 * n + 3)
                    dve.tensor_tensor(tmp(q), G[2 * q][:, :], rstd[:, :], ALU.mult).then_inc(s_ao, 1)
                    prep_lo(n, q, 1)
                    product(n, 1)
                    dve.tensor_tensor(tmp(4 + q), G[2 * q + 1][:, :], rstd[:, :], ALU.mult).then_inc(s_free, 1)
                    dve.wait_ge(s_free, n + 1)
                    dve.wait_ge(s_yh, 2 * i + (BASE[name][1] + 1))
                    dve.tensor_tensor(tmp(2 + q), tmp(4 + q), tmp(q), ALU.mult).then_inc(s_ao, 1)
                    dve.wait_ge(s_ao, 2 * i + (BASE[name][0] + 2))
                    dve.wait_ge(s_yh, 2 * i + (BASE[name][1] + 2))
                    lo_of(cut(y_lo, i), tmp(2 + q), cut(y_hi, i)).then_inc(s_yl, 1)
                loop_pairs(dve, name, body, peel=0 if r is None else 2)

            def scaled(name, dst, r=None):
                def body(i, n, q, landed):
                    first = r is not None and isinstance(i, int) and i == 0
                    if first:
                        norm_var(r)
                    prep_lo(n, q, 0)
                    if first:
                        norm_rstd(r)
                    prep_lo(n, q, 1)
                    dve.wait_ge(s_free, n)
                    for k in range(2):
                        product(n, k)
                        ins = dve.tensor_tensor(cut(dst, 2 * i + k), G[2 * q + k][:, :], rstd[:, :], ALU.mult)
                    ins.then_inc(s_free, 1)
                    if (name[:2], i) in (("xq", 1), ("xq", 2)):
                        for j in range(4 * i - 4, 4 * i):
                            dve.wait_ge(norm_a.sem, norm_a.at("mem_hi", int(name[2]), j))
                            dve.scalar_tensor_tensor(cut(y_lo, j)[:, 0:MEM], cut(memn, j, MEM), col("mem_norm_2", 8 * int(name[2]) + j),
                                                     cut(y_hi, j)[:, 0:MEM].bitcast(F32), ALU.mult, ALU.subtract)\
                               .then_inc(norm_v.sem, norm_v.mark("mem_lo", int(name[2]), j))
                loop_pairs(dve, name, body, unroll=name[:2] == "xq")

            def scale_by(r, scale, src_bank, eps, sig, var_key, std_sig, std_key, n=S):
                dve.tensor_scalar(stat[:, 0:n], src_bank[:, 0:n], scale, eps, ALU.mult, ALU.add)\
                   .then_inc(sig.sem, sig.mark(*var_key))
                dve.wait_ge(std_sig.sem, std_sig.at(*std_key))
                link(dve.reciprocal(rstd[:, 0:n], stat[:, 0:n]))

            def norm_dve(r, gain, g0=0):
                norm_var(r)
                norm_rstd(r)
                for j in range(KT + 1):
                    if 2 <= j < KT:
                        dve.wait_ge(norm_v.sem, norm_v.at("lo", r, j - 2))
                    if j < KT:
                        dve.scalar_tensor_tensor(tmp(2 + j % 2), cut(h, j), col(gain, g0 + j), rstd[:, :], ALU.mult, ALU.mult)\
                           .then_inc(norm_v.sem, norm_v.mark("xn", r, j))
                    if j >= 1:
                        dve.wait_ge(norm_a.sem, norm_a.at("hi", r, j - 1))
                        lo_of(cut(xn_lo, j - 1), tmp(2 + (j - 1) % 2), cut(xn_hi, j - 1))\
                            .then_inc(norm_v.sem, norm_v.mark("lo", r, j - 1))

            def norm_in_place(r, gain, then=None):
                norm_var(r)
                norm_rstd(r)
                for j in range(KT + 1):
                    if j < KT:
                        dve.scalar_tensor_tensor(cut(h, j), cut(h, j), col(gain, j), rstd[:, :], ALU.mult, ALU.mult)\
                           .then_inc(norm_v.sem, norm_v.mark("xn", r, j))
                    if then and j:
                        dve.wait_ge(norm_v.sem, norm_v.at("xn", r, j - 1))
                        then(j - 1)

            def log1p(dst, e, a, b):
                link(dve.tensor_scalar(a, e, 2.0, None, ALU.add))
                link(dve.reciprocal(b, a))
                link(dve.tensor_tensor(a, e, b, ALU.mult))
                link(dve.tensor_tensor(b, a, a, ALU.mult))
                link(dve.tensor_scalar(dst, b, 1.0 / 17, None, ALU.mult))
                for d in range(15, 1, -2):
                    link(dve.scalar_tensor_tensor(dst, dst, 1.0 / d, b, ALU.add, ALU.mult))
                link(dve.scalar_tensor_tensor(dst, dst, 1.0, a, ALU.add, ALU.mult))

            for k in range(2):
                dve.wait_ge(s_whi, k + 1)
                dve.tensor_tensor(w_lo[:, k], raw[:, 0, :, k * P:(k + 1) * P], w_hi[:, k].bitcast(F32), ALU.subtract)\
                   .then_inc(s_wlo, 1)
            for j in range(KT):
                dve.wait_ge(full.sem, full.at("x", j))
                dve.tensor_copy(cut(h, j), B[BANK.get(("x", j), 0)][:, :]).then_inc(turn_v.sem, turn_v.mark("x", j))
                if j:
                    norm_tile(0, j - 1)
            dve.wait_ge(turn_v.sem, turn_v.at("x", KT - 1))
            norm_tile(0, KT - 1)
            for b in range(4):
                n = sum(c for _, c in BATCHES[b])
                dve.wait_ge(full.sem, full.at("par", b))
                dve.tensor_copy(par[:, b * P:b * P + n], B[BANK.get(("par", b), 0)][:, 0:n])\
                   .then_inc(turn_v.sem, turn_v.mark("par", b))
            norm_dve(0, "norm_mix_g")

            only_prep("v")

            def gmlp_norm(at_):
                if at_ == 0:
                    for g in range(0, 8, 4):
                        dve.wait_ge(full.sem, full.at("w_sp", g))
                        dve.tensor_tensor(w_spT[:, g:g + 4, :], B[BANK.get(("w_sp", g), 0)][:, :].rearrange("p (g t) -> p g t", g=4),
                                          causal[:, None, :].to_broadcast([P, 4, P]), ALU.mult)\
                           .then_inc(gmlp_v.sem, gmlp_v.mark("w_sp", g))
                if at_ == 3:
                    dve.wait_ge(gmlp_a.sem, gmlp_a.at("v", 7))
                    for t in range(NB):
                        s0 = 32 + 16 * t
                        for o in range(2):
                            ins = dve.bn_stats(small[:, s0 + 6 * o:s0 + 6 * o + 6], v_tok[:, t, o * S:(o + 1) * S])
                        link(ins)
                        link(dve.bn_aggr(small[:, s0 + 12:s0 + 14], small[:, s0:s0 + 12]))
                        ins = dve.tensor_scalar(small[:, t:t + 1], small[:, s0 + 13:s0 + 14], EPS, None, ALU.add)
                    ins.then_inc(gmlp_v.sem, gmlp_v.mark("var"))
                if at_ == 5:
                    dve.wait_ge(gmlp_a.sem, gmlp_a.at("std"))
                    dve.wait_ge(s_gb, 48)
                    link(dve.reciprocal(small[:, 4:8], small[:, 0:4]))
                if at_ in (5, 6):
                    for t in (2 * at_ - 10, 2 * at_ - 9):
                        link(dve.scalar_tensor_tensor(v_tok[:, t, :], v_tok[:, t, :], small[:, 44 + 16 * t:45 + 16 * t], g_bc,
                                                      ALU.subtract, ALU.mult))
                        dve.scalar_tensor_tensor(v_tok[:, t, :], v_tok[:, t, :], small[:, 4 + t:5 + t], b_bc, ALU.mult, ALU.add)\
                           .then_inc(gmlp_v.sem, gmlp_v.mark("normed", t))

            only_prep("u", gmlp_norm)
            dve.wait_ge(s_free, P0["u"] + 4)
            for g in range(9):
                if 2 <= g < 8:
                    dve.wait_ge(gmlp_v.sem, gmlp_v.at("lo", g - 2))
                if g < 8:
                    dve.wait_ge(full.sem, full.at("mix", g))
                    dve.tensor_tensor(tmp(g % 2).rearrange("p (c t) -> p c t", c=NB),
                                      B[BANK.get(("mix", g), 0)][:, :].rearrange("p (c t) -> p c t", c=NB),
                                      bs_bc[:, None, g * P:(g + 1) * P].to_broadcast([P, NB, P]), ALU.add)\
                       .then_inc(gmlp_v.sem, gmlp_v.mark("mixed", g))
                    dve.wait_ge(gmlp_v.sem, gmlp_v.at("mixed", g))
                    dve.tensor_tensor(tmp(4 + g % 2), tmp(g % 2), cut(u, g), ALU.mult)\
                       .then_inc(gmlp_v.sem, gmlp_v.mark("y", g))
                if g >= 1:
                    dve.wait_ge(gmlp_a.sem, gmlp_a.at("hi", g - 1))
                    lo_of(cut(y_lo, g - 1), tmp(4 + (g - 1) % 2), cut(y_hi, g - 1))\
                        .then_inc(gmlp_v.sem, gmlp_v.mark("lo", g - 1))
            gates("ga", 0)

            dve.wait_ge(lru_a.sem, lru_a.at("exp"))
            lam = par[:, COL["lru_lambda"]:COL["lru_lambda"] + 8]
            log1p(small[:, 40:48], small[:, 16:24], small[:, 48:56], small[:, 56:64])
            link(dve.tensor_scalar(small[:, 32:40], lam, -1.0, 0.0, ALU.mult, ALU.max))
            link(dve.scalar_tensor_tensor(small[:, 24:32], small[:, 40:48], 2.0, small[:, 32:40], ALU.mult, ALU.add))
            dve.tensor_scalar(small[:, 24:32], small[:, 24:32], 4.0, None, ALU.mult).then_inc(lru_v.sem, lru_v.mark("rate"))
            for q in range(2):
                ins = dve.memset(xpad[q][:, 0:3], 0.0)
            ins.then_inc(lru_v.sem, lru_v.mark("pads"))
            for j in range(9):
                if j < 8:
                    n = P0["lru"] + j
                    q = n % 2
                    prep_lo(n, q, 0)
                    prep_lo(n, q, 1)
                    dve.wait_ge(lru_a.sem, lru_a.at("x", j))
                    x = xpad[q]
                    if j >= 2:
                        dve.wait_ge(full.sem, full.at("ri", j - 2, 1))
                    link(dve.tensor_scalar(lt[j % 2], x[:, 0:S], col("lru_conv_w", j), col("lru_conv_b", j),
                                           ALU.mult, ALU.add))
                    for k in range(1, 4):
                        ins = dve.scalar_tensor_tensor(lt[j % 2], x[:, k:k + S], col("lru_conv_w", 8 * k + j), lt[j % 2],
                                                       ALU.mult, ALU.add)
                        if k < 3:
                            link(ins)
                    ins.then_inc(lru_v.sem, lru_v.mark("conv", j))
                if j >= 1:
                    jj = j - 1
                    dve.wait_ge(lru_a.sem, lru_a.at("tanh", jj))
                    link(dve.tensor_scalar(lt[8], lt[6], 1.0, None, ALU.add))
                    dve.reciprocal(lt[9], lt[8])
                    link(dve.tensor_scalar(lt[10], lt[6], -1.0, 1.0, ALU.mult, ALU.add))
                    dve.tensor_tensor(lt[10], lt[10], lt[9], ALU.mult)
                    link(dve.tensor_tensor(lt[8], lt[5], lt[jj % 2], ALU.mult))
                    link(dve.scalar_tensor_tensor(lt[8], lt[8], 2.0, lt[9], ALU.mult, ALU.mult))
                    dve.wait_ge(lru_a.sem, lru_a.at("sqrt", jj))
                    dve.tensor_tensor(lt[11], lt[8], lt[7], ALU.mult).then_inc(lru_v.sem, lru_v.mark("inp", jj))
                    dve.wait_ge(lru_v.sem, lru_v.at("inp", jj))
                    link(dve.tensor_tensor_scan(lt[13], lt[10], lt[11], 0.0, ALU.mult, ALU.add))
                    dve.wait_ge(s_free, P0["lru"] + jj + 1)
                    dve.tensor_tensor(lt[12], lt[13], lt[2 + jj % 2], ALU.mult).then_inc(lru_v.sem, lru_v.mark("y", jj))
                    dve.wait_ge(lru_a.sem, lru_a.at("hi", jj))
                    lo_of(cut(y_lo, jj), lt[12], cut(y_hi, jj)).then_inc(lru_v.sem, lru_v.mark("lo", jj))
            gates("gb", 1)

            for i in range(4):
                ins = dve.memset(cpad[i][:, 0:3], 0.0)
            ins.then_inc(xbc_v.sem, xbc_v.mark("pads"))
            for i in range(NPAIR["xbc"]):
                n = P0["xbc"] + i
                q = n % 2
                prep_lo(n, q, 0)
                prep_lo(n, q, 1)
                for k in range(2):
                    j = 2 * i + k
                    if k == 0:
                        dve.wait_ge(xbc_a.sem, xbc_a.at("x", j))
                    else:
                        dve.wait_ge(s_free, n + 1)
                    if i >= 1:
                        dve.wait_ge(xbc_a.sem, xbc_a.at("silu", j - 2))
                    link(dve.tensor_scalar(cacc[k], cpad[j % 4][:, 0:S], col("ssd_conv_w", j), col("ssd_conv_b", j),
                                           ALU.mult, ALU.add))
                    for w in range(1, 4):
                        ins = dve.scalar_tensor_tensor(cacc[k], cpad[j % 4][:, w:w + S], col("ssd_conv_w", 16 * w + j),
                                                       cacc[k], ALU.mult, ALU.add)
                        if w < 3:
                            link(ins)
                    ins.then_inc(xbc_v.sem, xbc_v.mark("conv", j))
            only_prep("dt")
            ssd_dve(dve, link, log1p)
            def group_rstd(g):
                dve.wait_ge(full.sem, full.at("zsum", g))
                scale_by(0, 1.0 / 256, B[BANK.get(("zsum", g), 0)], EPS, z_v, ("var", g), z_a, ("std", g))

            def group_norm(g):
                for k in range(2):
                    j = 2 * g + k
                    dve.scalar_tensor_tensor(tmp(4 + k), cut(xbc, j), col("ssd_norm_g", j), rstd[:, :], ALU.mult, ALU.mult)\
                       .then_inc(z_v.sem, z_v.mark("y", j))
                for k in range(2):
                    j = 2 * g + k
                    dve.wait_ge(z_a.sem, z_a.at("hi", j))
                    lo_of(cut(y_lo, j), tmp(4 + k), cut(y_hi, j)).then_inc(z_v.sem, z_v.mark("lo", j))

            for i in range(NPAIR["z"]):
                n = P0["z"] + i
                q = n % 2
                for k in range(2):
                    prep_lo(n, q, k)
                    if i and k == 0:
                        group_rstd(i - 1)
                for k in range(2):
                    if k == 0:
                        dve.wait_ge(z_a.sem, z_a.at("silu", 2 * i))
                    else:
                        dve.wait_ge(s_free, n + 1)
                    dve.tensor_tensor(cut(xbc, 2 * i + k), cut(xbc, 2 * i + k), tmp(2 + k), ALU.mult)\
                       .then_inc(z_v.sem, z_v.mark("gated", 2 * i + k))
                if i:
                    group_norm(i - 1)
            group_rstd(3)
            group_norm(3)
            gates("gc", 2)
            for j in range(KT):
                dve.wait_ge(split_a.sem, split_a.at("merged", j))
                lo_of(cut(y_lo, j), cut(merged, j), cut(y_hi, j)).then_inc(split_v.sem, split_v.mark("merged", j))
            follow("wo", 1.0, 1, "norm_mlp_g")
            for p in range(4):
                squared_relu(f"up{p}", None if p else 1)
                if p < 3:
                    residual(f"down{p}")
            follow("down3", 1.0, 2)

            norm_in_place(2, "final_norm_g", lambda j: norm_tile(4, j, "ffn1_norm_2"))

            def memory(i, k):
                if (i, k) == (0, 1):
                    for j in range(0, KT, 2):
                        dve.wait_ge(full.sem, full.at("mem", j))
                        dve.tensor_copy(mem_t[:, j * MEM:(j + 2) * MEM], B[BANK.get(("mem", j), 0)][:, :])\
                           .then_inc(turn_v.sem, turn_v.mark("mem", j))
                if (i, k) == (1, 1):
                    dve.wait_ge(turn_v.sem, turn_v.at("mem", 6))
                    dve.wait_ge(norm_a.sem, norm_a.at("square", 3))
                    for half in (4 * MEM, 2 * MEM):
                        link(dve.tensor_tensor(temps[:, 0:half], temps[:, 0:half], temps[:, half:2 * half], ALU.add))
                    dve.tensor_tensor(stat[:, 0:MEM], temps[:, 0:MEM], temps[:, MEM:2 * MEM], ALU.add)\
                       .then_inc(norm_v.sem, norm_v.mark("summed", 3, KT - 1))
                if (i, k) == (2, 0):
                    norm_var(3, MEM)
                if (i, k) == (2, 1):
                    norm_rstd(3, MEM, mem_rstd)
                    link(dve.tensor_tensor(memn.rearrange("p (j m) -> p j m", j=KT), mem_t.rearrange("p (j m) -> p j m", j=KT),
                                           mem_rstd[:, None, :].to_broadcast([P, KT, MEM]), ALU.mult))

            def angles(i, k):
                if (i, k) == (0, 0):
                    dve.wait_ge(s_pos, 16)
                    link(dve.tensor_copy(ang[0], ang[4].bitcast(I32)))
                    link(dve.tensor_scalar(ang[1], ang[0], inv_freq, None, ALU.mult))
                if k == 1 and i < 2:
                    c = i
                    link(dve.tensor_scalar(ang[0], ang[1], 1.0 / (2 * np.pi), 0.25 * (1 - c), ALU.mult, ALU.add))
                    link(dve.tensor_scalar(ang[0], ang[0], ROUND, ROUND, ALU.add, ALU.subtract))
                    link(dve.scalar_tensor_tensor(ang[2 + c], ang[0], -TURN[0], ang[1], ALU.mult, ALU.add))
                    for part in TURN[1:]:
                        link(dve.scalar_tensor_tensor(ang[2 + c], ang[0], -part, ang[2 + c], ALU.mult, ALU.add))
                    link(dve.tensor_scalar(ang[2 + c], ang[2 + c], (1 - c) * np.pi / 2, PI, ALU.add, ALU.min))
                    dve.tensor_scalar(ang[2 + c], ang[2 + c], -PI, None, ALU.max).then_inc(trig_v.sem, trig_v.mark("angle", c))

            for l in range(2):
                def ffn(f, r):
                    for part in range(3):
                        swiglu(f"{f}u{l}{part}", None if part else r)
                        if part < 2:
                            residual(f"{f}d{l}{part}", 0.5, (memory, angles)[part] if (f, l) == ("f1", 0) else None)
                        elif f == "f1":
                            follow(f"{f}d{l}{part}", 0.5, r + 1, "mix_norm_2", 8 * l)
                        elif l == 0:
                            follow(f"{f}d{l}{part}", 0.5, 9, "ffn1_norm_2", 8)
                        else:
                            follow(f"{f}d{l}{part}", 0.5, 14)
                r = 4 + 5 * l
                ffn("f1", r)
                for k in range(2):
                    dve.memset(av[k][:, 0:30], 0.0)
                    ins = dve.memset(hc[k][:, 0:2], 0.0)
                ins.then_inc(conv_v.sem, conv_v.mark("pads", l))
                mix = [(name, i, k) for name in MIX for i in range(NPAIR[name + "0"]) for k in range(2)]
                for p, (name, i, k) in enumerate(mix):
                    n = P0[f"{name}{l}"] + i
                    q = n % 2
                    bank = G[2 * q + k][:, :]
                    if p == 0:
                        norm_var(r + 1)
                    prep_lo(n, q, k)
                    if p == 0:
                        norm_rstd(r + 1)
                        for c in range(2):
                            ins = dve.tensor_tensor(sincos_r[:, c, :], sincos[:, c, :], rstd[:, :], ALU.mult)
                        link(ins)
                    if name in ("kidx", "conv", "vv"):
                        if k == 0:
                            dve.wait_ge(s_free, n)
                        product(n, k)
                        dst = ((ki, wi)[k] if name == "kidx" else cut(vt2, 2 * i + k) if name == "vv" else
                               (av[k][:, 30:30 + S], tmp(4 + k), bg[k], hc[k][:, 2:2 + S], tmp(2 + k))[i])
                        if (name, k) == ("kidx", 0):
                            ins = dve.tensor_copy(dst, bank)
                        else:
                            ins = dve.tensor_tensor(dst, bank, rstd[:, :], ALU.mult)
                        if name == "conv" and i == 1:
                            ins.then_inc(conv_v.sem, conv_v.mark("gate", l, k))
                        elif k == 1:
                            ins.then_inc(s_free, 1)
                    if (name, i, k) == ("conv", 1, 1):
                        for x in range(2):
                            dve.wait_ge(conv_a.sem, conv_a.at("gate", l, x))
                            ins = dve.tensor_tensor(av[x][:, 30:30 + S], av[x][:, 30:30 + S], tmp(4 + x), ALU.mult)
                        ins.then_inc(s_free, 1)
                    if (name, i, k) == ("conv", 4, 1):
                        dve.wait_ge(s_free, n + 1)
                        for x in range(2):
                            ins = dve.tensor_tensor(hc[x][:, 2:2 + S], hc[x][:, 2:2 + S], tmp(2 + x), ALU.mult)
                        ins.then_inc(conv_v.sem, conv_v.mark("short_in", l))
                    if p == 3:
                        dve.wait_ge(full.sem, full.at("w_tok", l))
                        dve.tensor_copy(w_tok[:, :, :],
                                        B[BANK.get(("w_tok", l), 0)][:, :].rearrange("p (t h) -> p t h", t=NB)[:, :, 0:4])\
                           .then_inc(rope_v.sem, rope_v.mark("w_tok", l))
                        dve.wait_ge(rope_v.sem, rope_v.at("w_tok", l))
                    if p in index_heads:
                        index_scores(dve, link, l, *index_heads[p])
                    if p in rotations:
                        rope(dve, link, l, rotations[p], p)
                    if p in selections:
                        select(dve, link, *selections[p])
                dsa_dve(dve, link, l, lo_of)
                follow(f"mwo{l}", 1.0, r + 2, "xa_norm_2", 8 * l)
                scaled(f"xq{l}", xq, r + 2)
                only_prep(f"xk{l}")
                only_prep(f"xv{l}")
                cross_dve(dve, link, l, lo_of)
                follow(f"xo{l}", 1.0, r + 3, "ffn2_norm_2", 8 * l)
                ffn("f2", r + 3)
            norm_in_place(14, "final_norm_2")
            for t in range(NB):
                for o in range(2):
                    dve.wait_ge(full.sem, full.at("out", t, o))
                    dve.tensor_copy(v_out(t)[:, o * S:(o + 1) * S], B[BANK.get(("out", t, o), 0)][:, :])\
                       .then_inc(turn_v.sem, turn_v.mark("out", t, o))

        @block.gpsimd
        def _(pool):
            pool.dma_start(x_in[:, :, :], A["x"][0].rearrange("(t p) d -> p t d", p=P)).then_inc(s_x, 16)
            pool.dma_start(consts[:, :], A["consts"]).then_inc(s_const, 16)
            load_params(pool, 0)
            pool.dma_start(small[0:16, 176:177], A["ssd_dt_bias"].rearrange("o h -> h o")).then_inc(s_sp, 16)
            pool.dma_start(small[0:16, 177:178], A["ssd_a_log"].rearrange("o h -> h o")).then_inc(s_sp, 16)
            pool.dma_start(w_sp[:, :, :], A["gmlp_w_s"][0].rearrange("g t s -> t g s")).then_inc(s_gw, 16)
            for dst, src in ((g_bc, A["gmlp_ln_g"]), (b_bc, A["gmlp_ln_b"]),
                             (bs_bc, A["gmlp_b_s"].rearrange("o g t -> o (g t)"))):
                pool.dma_start(dst, src.to_broadcast([P, D])).then_inc(s_gb, 16)
            pool.wait_ge(gmlp_v.sem, gmlp_v.at("lo", 7))
            for g, w in enumerate(("lru_w_r", "lru_w_i")):
                pool.dma_start(lru_w[:, g, :, :], A[w][0].rearrange("h i j -> i h j")).then_inc(s_lw, 16)
            pool.dma_start(small[:, 200:216], A["ssd_d"].to_broadcast([P, 16])).then_inc(s_sp, 16)
            pool.wait_ge(s_mm, 2 * P0["up0"] + 2)
            pool.dma_start(mem_in[:, :, :], A["mem_2"][0].rearrange("(t p) d -> p t d", p=P)).then_inc(s_mem, 16)
            pool.dma_start(ang[4].bitcast(I32), A["positions_2"].to_broadcast([P, S])).then_inc(s_pos, 16)
            for l in range(2):
                for (kind_, t, k), a in adds.items():
                    acc = cv[k] if kind_ == "conf" else tmp(2 + k)
                    pool.wait_ge(conv_a.sem, conv_a.at("product", l, kind_, t, k))
                    if t > 1:
                        pool.wait_ge(conv_p.sem, conv_p.at("add", l, a - 2))
                    pool.tensor_tensor(acc, acc, tap_buffers[a % 4], ALU.add).then_inc(conv_p.sem, conv_p.mark("add", l, a))
                for k in range(2):
                    pool.wait_ge(conv_p.sem, conv_p.at("add", l, adds["short", 2, k]))
                    pool.tensor_tensor(tmp(2 + k), tmp(2 + k), bg[k], ALU.mult).then_inc(conv_p.sem, conv_p.mark("short", l, k))


def constants():
    i = np.arange(P)
    ident = np.eye(P, dtype=np.float32)
    ones = np.ones((P, P), np.float32)
    causal = (i[None, :] >= i[:, None]).astype(np.float32)
    rot = np.zeros((P, P), np.float32)
    for m in range(P):
        if m % 64 < 32:
            rot[m + 32, m] = -1.0
        else:
            rot[m - 32, m] = 1.0
    qcausal = np.where(i[None, :] <= i[:, None], 0.0, NEG).astype(np.float32)
    freq = np.float32(10000.0) ** (-np.arange(0, 64, 2, dtype=np.float32) / np.float32(64))
    return np.concatenate([ident, ones, causal, rot, qcausal, np.tile(freq, 4)[:, None].astype(np.float32)], axis=1)


NAMES = ["x", "norm_mix_g", "w_in", "b_gate", "gmlp_ln_g", "gmlp_ln_b", "gmlp_w_s", "gmlp_b_s", "lru_conv_w", "lru_conv_b",
         "lru_w_r", "lru_b_r", "lru_w_i", "lru_b_i", "lru_lambda", "ssd_conv_w", "ssd_conv_b", "ssd_dt_bias",
         "ssd_a_log", "ssd_d", "ssd_norm_g", "w_branch_a", "w_branch_b", "w_branch_c", "w_out", "norm_mlp_g",
         "w_mlp_up", "w_mlp_down", "final_norm_g", "mem_2", "positions_2", "ffn1_norm_2", "ffn1_w_gate_2",
         "ffn1_w_up_2", "ffn1_w_down_2", "mix_norm_2", "w_in_2", "conf_dw_2", "conf_dw_b_2", "conf_ln_g_2",
         "conf_ln_b_2", "sc_dw_2", "w_out_2", "xa_norm_2", "mem_norm_2", "xa_wq_2", "xa_wkv_2", "xa_wo_2",
         "ffn2_norm_2", "ffn2_w_gate_2", "ffn2_w_up_2", "ffn2_w_down_2", "final_norm_2"]


def kernel(**inputs):
    import concourse.bacc as bacc
    import concourse.bass_utils as bass_utils

    arrays = {f"in_{n}": np.ascontiguousarray(inputs[n]) for n in NAMES}
    arrays["in_consts"] = constants()

    def build():
        nc = bacc.Bacc("TRN2", target_bir_lowering=False, num_devices=1)
        A = {n[3:]: nc.dram_tensor(n, a.shape, mybir.dt.from_np(a.dtype), kind="ExternalInput").ap()
             for n, a in arrays.items()}
        out = nc.dram_tensor("out_0", (1, S, D), F32, kind="ExternalOutput").ap()
        build_program(nc, A, out)
        return nc

    build()
    nc = build()
    r = bass_utils.run_bass_kernel_spmd(nc, [arrays], core_ids=[0])
    return r.results[0]["out_0"]
```
